# Optimizing a Trainium2 kernel written in Bass

```python
import jax, jax.numpy as jnp
from jax import lax
import numpy as np

D_MODEL = 1024
BATCH = 1
SEQ = 512
DEPTH = 2

N_A = DEPTH // 2
N_B = DEPTH - N_A
N_DENSE = (DEPTH + 1) // 2
N_MOE = DEPTH // 2

POOL_WINDOWS = (2, 4, 8, 16)
N_POOL_GROUPS = len(POOL_WINDOWS)
GW = D_MODEL // N_POOL_GROUPS

HEAD_DIM = 64
N_HEADS = D_MODEL // HEAD_DIM
Q_BLOCK = 128

D_FF = 2816
N_EXPERTS = 8
TOP_K = 2
D_FF_EXPERT = 3584
EXPERT_BLOCK = 128

RMS_EPS = 1e-6

kernel_name = "yoco_pool_stickbreak_moe_trunk"

def rmsnorm(x, g):
    xf = x.astype(jnp.float32)
    inv = lax.rsqrt(jnp.mean(xf * xf, axis=-1, keepdims=True) + RMS_EPS)
    return (xf * inv).astype(x.dtype) * g

def multiscale_pool(h, w_groups, scale):
    B, S, D = h.shape
    hf = h.astype(jnp.float32)
    cs = jnp.cumsum(hf, axis=1)
    t = jnp.arange(S)
    pooled = []
    for gi, w in enumerate(POOL_WINDOWS):
        sl = slice(gi * GW, (gi + 1) * GW)
        csg = cs[..., sl]
        lagged = jnp.pad(csg, ((0, 0), (w, 0), (0, 0)))[:, :S]
        count = jnp.minimum(t + 1, w).astype(jnp.float32)[None, :, None]
        pooled.append((csg - lagged) / count - hf[..., sl])
    p = jnp.stack(pooled, axis=2).astype(h.dtype)
    y = jnp.einsum('bsgc,gcd->bsgd', p, w_groups).reshape(B, S, D)
    return y * scale

def stick_breaking_attention(q, k, v):
    S = q.shape[2]
    scale = HEAD_DIM ** -0.5
    outs = []
    for i in range(S // Q_BLOCK):
        L = (i + 1) * Q_BLOCK
        qb = q[:, :, i * Q_BLOCK:L]
        kb = k[:, :, :L]
        vb = v[:, :, :L]
        z = jnp.einsum('bhqd,bhkd->bhqk', qb, kb).astype(jnp.float32) * scale
        qpos = i * Q_BLOCK + jnp.arange(Q_BLOCK)
        kpos = jnp.arange(L)
        causal = kpos[None, :] < qpos[:, None]
        log_beta = jax.nn.log_sigmoid(z)
        log_keep = jnp.where(causal, log_beta - z, 0.0)
        log_after = lax.cumsum(log_keep, axis=3, reverse=True) - log_keep
        a = jnp.where(causal, jnp.exp(log_beta + log_after), 0.0)
        outs.append(jnp.einsum('bhqk,bhkd->bhqd', a.astype(vb.dtype), vb))
    return jnp.concatenate(outs, axis=2)

def split_heads(t):
    B, S, _ = t.shape
    return t.reshape(B, S, N_HEADS, HEAD_DIM).transpose(0, 2, 1, 3)

def merge_heads(t):
    B, H, S, Dh = t.shape
    return t.transpose(0, 2, 1, 3).reshape(B, S, H * Dh)

def swiglu(h, w_in, w_out):
    g, u = jnp.split(h @ w_in, 2, axis=-1)
    return (jax.nn.silu(g) * u) @ w_out

def moe_swiglu(h, w_router, w_in, w_out):
    B, S, D = h.shape
    N = B * S
    NK = N * TOP_K
    hf = h.reshape(N, D)
    logits = hf.astype(jnp.float32) @ w_router.astype(jnp.float32)
    top_v, top_e = lax.top_k(logits, TOP_K)
    gates = jax.nn.softmax(top_v, axis=-1)
    flat_e = top_e.reshape(NK).astype(jnp.int32)
    flat_g = gates.reshape(NK).astype(h.dtype)
    flat_tok = jnp.arange(NK, dtype=jnp.int32) // TOP_K

    order = jnp.argsort(flat_e)
    sorted_e = flat_e[order]
    counts = jnp.bincount(flat_e, length=N_EXPERTS).astype(jnp.int32)
    padded = (counts + EXPERT_BLOCK - 1) // EXPERT_BLOCK * EXPERT_BLOCK
    pend = jnp.cumsum(padded)
    pstart = pend - padded
    cstart = jnp.cumsum(counts) - counts
    dest = pstart[sorted_e] + jnp.arange(NK, dtype=jnp.int32) - cstart[sorted_e]

    cap = NK + N_EXPERTS * EXPERT_BLOCK
    n_blk = cap // EXPERT_BLOCK
    tok_buf = jnp.zeros((cap,), jnp.int32).at[dest].set(flat_tok[order])
    gate_buf = jnp.zeros((cap,), h.dtype).at[dest].set(flat_g[order])
    blk_start = jnp.arange(n_blk, dtype=jnp.int32) * EXPERT_BLOCK
    blk_e = jnp.minimum(jnp.searchsorted(pend, blk_start, side='right'), N_EXPERTS - 1)

    xs = hf[tok_buf].reshape(n_blk, EXPERT_BLOCK, D)

    def expert_block(args):
        xb, e = args
        g, u = jnp.split(xb @ w_in[e], 2, axis=-1)
        return (jax.nn.silu(g) * u) @ w_out[e]

    ys = lax.map(expert_block, (xs, blk_e)).reshape(cap, D)
    y = jnp.zeros_like(hf).at[tok_buf].add(ys * gate_buf[:, None])
    return y.reshape(B, S, D)

def setup_inputs(seed: int = 0) -> dict:
    key = jax.random.key(seed)
    ks = jax.random.split(key, 16)
    f32 = jnp.float32

    def nrm(k, shape, fan_in):
        return jax.random.normal(k, shape, f32) * (fan_in ** -0.5)

    def gain(k, shape):
        return 1.0 + 0.02 * jax.random.normal(k, shape, f32)

    return {
        "x": jax.random.normal(ks[0], (BATCH, SEQ, D_MODEL), f32),
        "g_mix": gain(ks[1], (DEPTH, D_MODEL)),
        "g_ffn": gain(ks[2], (DEPTH, D_MODEL)),
        "pool_w": nrm(ks[3], (N_A, N_POOL_GROUPS, GW, GW), GW),
        "pool_scale": gain(ks[4], (N_A, D_MODEL)),
        "g_kv": gain(ks[5], (D_MODEL,)),
        "w_kv": nrm(ks[6], (D_MODEL, 2 * D_MODEL), D_MODEL),
        "w_q": nrm(ks[7], (N_B, D_MODEL, D_MODEL), D_MODEL),
        "w_o": nrm(ks[8], (N_B, D_MODEL, D_MODEL), D_MODEL),
        "ffn_in": nrm(ks[9], (N_DENSE, D_MODEL, 2 * D_FF), D_MODEL),
        "ffn_out": nrm(ks[10], (N_DENSE, D_FF, D_MODEL), D_FF),
        "w_router": nrm(ks[11], (N_MOE, D_MODEL, N_EXPERTS), D_MODEL),
        "moe_in": nrm(ks[12], (N_MOE, N_EXPERTS, D_MODEL, 2 * D_FF_EXPERT), D_MODEL),
        "moe_out": nrm(ks[13], (N_MOE, N_EXPERTS, D_FF_EXPERT, D_MODEL), D_FF_EXPERT),
        "g_final": gain(ks[14], (D_MODEL,)),
    }

def reference(x, g_mix, g_ffn, pool_w, pool_scale, g_kv, w_kv, w_q, w_o,
              ffn_in, ffn_out, w_router, moe_in, moe_out, g_final):
    k_sh = None
    v_sh = None
    for l in range(DEPTH):
        h = rmsnorm(x, g_mix[l])
        if l < N_A:
            x = x + multiscale_pool(h, pool_w[l], pool_scale[l])
        else:
            b = l - N_A
            q = split_heads(h @ w_q[b])
            o = stick_breaking_attention(q, k_sh, v_sh)
            x = x + merge_heads(o) @ w_o[b]
        h = rmsnorm(x, g_ffn[l])
        if l % 2 == 0:
            x = x + swiglu(h, ffn_in[l // 2], ffn_out[l // 2])
        else:
            x = x + moe_swiglu(h, w_router[l // 2], moe_in[l // 2], moe_out[l // 2])
        if l == N_A - 1:
            kv = rmsnorm(x, g_kv) @ w_kv
            k_part, v_part = jnp.split(kv, 2, axis=-1)
            k_sh = split_heads(k_part)
            v_sh = split_heads(v_part)
    return rmsnorm(x, g_final)


_drawn_inputs = setup_inputs


def setup_inputs(seed=0):
    import zlib

    import numpy as np

    out = dict(_drawn_inputs(seed))
    spreads = {}
    factors = {'g_kv': 3.289, 'g_final': 2.86}
    for name, (base, spread) in spreads.items():
        noise = np.random.default_rng([zlib.crc32(name.encode()), seed]).standard_normal(out[name].shape)
        drawn = base * np.exp(spread * noise) if base else spread * noise
        out[name] = __import__('jax').numpy.asarray(drawn.astype(out[name].dtype))
    for name, factor in factors.items():
        out[name] = (out[name] * factor).astype(out[name].dtype)
    return out
```

```python
from contextlib import ExitStack

import concourse.bass as bass
from concourse import mybir

F32 = mybir.dt.float32
F32R = mybir.dt.float32r
I32 = mybir.dt.int32
U32 = mybir.dt.uint32
ALU = mybir.AluOpType
ACT = mybir.ActivationFunctionType
AX_X = mybir.AxisListType.X

P = 128
STOP = "all"


def trunk(nc, x, g_mix, g_ffn, pool_w, pool_scale, g_kv, w_kv, w_q, w_o, ffn_in, ffn_out,
          w_router, moe_in, moe_out, g_final, out):
    _, T, D = x.shape
    DT, TT = D // P, T // P
    NG, GW = pool_w.shape[1], pool_w.shape[2]
    WINDOWS = (2, 4, 8, 16)
    FF = ffn_out.shape[1]
    NE, FE = moe_out.shape[1], moe_out.shape[2]
    HD = 64
    NH = D // HD
    EPS = 1e-6
    RING = 4
    SUB = 2048
    CW = SUB // DT
    AHEAD = 3
    F_TILES = FF // P
    F_HALF = (12, F_TILES - 12)
    S_POOL = 0
    S_FFN = 1
    S_IN = (S_FFN, S_FFN + F_HALF[0] + 8)
    S_OUT = (S_FFN + F_HALF[0], S_FFN + F_TILES + 8)
    S_K = S_FFN + F_TILES + 16
    S_V = S_K + 4
    S_Q = S_V + 4
    S_O = S_Q + 4
    S_MOE = S_O + 4
    NT = 144
    MAX_EXTRA = (2 * T - 1) // NT
    MAX_TASKS = NE + MAX_EXTRA
    FE_TILES = FE // P
    SUBS_IN = FE_TILES
    Q_OUT = D // 256
    SUBS_OUT = Q_OUT * 4
    FS = FE_TILES // 4
    SUBS_TASK = SUBS_IN + SUBS_OUT
    assert SUBS_TASK % RING == 0 and SUBS_IN % RING == 0

    with ExitStack() as ctx:
        base = 16512
        place = [base]

        def at(name, shape, dt, offset):
            return nc.alloc_sbuf_tensor_at(name, shape, dt, offset=offset)

        def take(nbytes):
            o = place[0]
            place[0] += nbytes
            return o

        o_raw, o_hi, o_lo = take(RING * SUB * 4), take(RING * SUB * 4), take(RING * SUB * 4)
        o_xT = take(DT * T * 4)
        o_hT = take(2 * DT * T * 4)
        o_big = take(12 * T * 4 * 2)
        o_tmp = take(5 * T * 4)
        o_const = place[0]

        raw = at("raw", [P, RING, SUB], F32, o_raw)
        w_hi = at("w_hi", [P, RING, SUB], F32R, o_hi)
        w_lo = at("w_lo", [P, RING, SUB], F32R, o_lo)
        xT = at("xT", [P, DT, T], F32, o_xT)
        hT_hi = at("hT_hi", [P, DT, T], F32R, o_hT)
        hT_lo = at("hT_lo", [P, DT, T], F32R, o_hT + DT * T * 4)
        tmp = at("tmp", [P, 5, T], F32, o_tmp)
        hid_hi = at("hid_hi", [P, 12, T], F32R, o_big)
        hid_lo = at("hid_lo", [P, 12, T], F32R, o_big + 12 * T * 4)
        x_in = at("x_in", [P, TT, D], F32, o_big)
        PAD = 16
        hp = at("hp", [P, 2, PAD + T], F32, o_big + 16384)
        sums = at("sums", [P, 4, PAD + T], F32, o_big + 16384 + 2 * (PAD + T) * 4)
        KT = at("KT", [P, DT, T], F32, o_big)
        QT = at("QT", [P, DT, T], F32, o_big + 16384)
        V = at("V", [P, TT, D], F32, o_big + 32768)
        SEG = {0: 0, 1: 512, 3: 896, 2: 1024}
        HC = 1280
        E = at("E", [P, 2, HC], F32, o_tmp)
        sp_hi = at("sp_hi", [P, 2, HC], F32R, o_hi)
        sp_lo = at("sp_lo", [P, 2, HC], F32R, o_lo)

        def const(name, shape, dt=F32):
            n = 4
            for s in shape[1:]:
                n *= s
            return at(name, shape, dt, take((n + 31) // 32 * 32))

        NV = 48 // 8 * 8
        gains_in = at("gains_in", [NV, P], F32, o_tmp)
        gains = const("gains", [P, NV])
        ident = const("ident", [P, P])
        ones = const("ones", [P, P])
        neg_ones = const("neg_ones", [P, P], F32R)
        neg_tri = const("neg_tri", [P, P], F32R)
        eps = const("eps", [P, 1])
        inv_count = const("inv_count", [P, PAD])
        count = const("count", [P, PAD])
        rows_hi = at("rows_hi", [P, TT, D], F32R, o_big)
        rows_lo = at("rows_lo", [P, TT, D], F32R, o_big + TT * D * 4)
        x2_rows = at("x2_rows", [P, TT, D], F32, o_big + 2 * TT * D * 4)
        o_free = o_big + 2 * TT * D * 4
        SLOTS = 2 * P
        pick = at("pick", [P, TT, SLOTS], F32R, o_free)
        y_rows = at("y_rows", [P, 2, D], F32, o_free + TT * SLOTS * 4)
        g_row = at("g_row", [P, D], F32, o_free + TT * SLOTS * 4 + 2 * D * 4)
        x_sel = at("x_sel", [P, 2, DT, NT], F32R, o_xT)
        hid = at("hid", [P, 2, FE_TILES, NT], F32R, o_xT + 2 * DT * NT * 4)
        o_yT = o_xT + 2 * (DT + FE_TILES) * NT * 4
        yT = at("yT", [P, 2, 2, SLOTS], F32, o_yT)
        assert o_yT + 4 * SLOTS * 4 <= o_big
        gate_s = at("gate_s", [P, 2, 2, NT], F32, o_tmp)
        up_s = at("up_s", [P, 2, 2, NT], F32, o_tmp + 4 * NT * 4)
        y_s = at("y_s", [P, 2, 2, NT], F32, o_tmp + 8 * NT * 4)
        TC = MAX_TASKS + 1
        o_t = [o_tmp]

        def table(name, shape, dt=F32):
            n = 4
            for k in shape[1:]:
                n *= k
            a = at(name, shape, dt, o_t[0])
            o_t[0] += (n + 31) // 32 * 32
            return a

        logits, top_v = table("logits", [P, TT, NE]), table("top_v", [P, TT, NE])
        top_i, top_f = table("top_i", [P, TT, NE], U32), table("top_f", [P, TT, NE])
        first, second = table("first", [P, TT, NE]), table("second", [P, TT, NE])
        chosen, gate_e = table("chosen", [P, TT, NE]), table("gate_e", [P, TT, NE])
        rank, row_e = table("rank", [P, TT, NE]), table("row_e", [P, TT, NE])
        gates = table("gates", [P, 4, TT])
        cnt = table("cnt", [P, NE])
        extra = table("extra", [P, 3, NE])
        cum = table("cum", [P, 4, NE + 4])
        before = table("before", [P, NE])
        n_f = table("n_f", [P, 1])
        is_mine = table("is_mine", [P, TC, NE])
        is_past = table("is_past", [P, 2, TC - NE, NE])
        start = table("start", [P, TC, NE])
        e_f = table("e_f", [P, TC])
        wide = table("wide", [P, TT, TC, NE])
        assert o_t[0] <= o_const
        pos = const("pos", [P, TT, TC])
        row_gate = const("row_gate", [P, TT, TC, 2])
        task_e = const("task_e", [P, TC], I32)
        n_tasks_i = const("n_tasks_i", [P, 1], I32)
        slot_iota = const("slot_iota", [P, NT])
        e_iota = const("e_iota", [P, NE])
        row0 = const("row0", [P, TT])
        spare_row = const("spare_row", [P, 2])
        earlier = const("earlier", [P, P])
        wr = const("wr", [P, DT, NE])
        wr_hi, wr_lo = const("wr_hi", [P, DT, NE], F32R), const("wr_lo", [P, DT, NE], F32R)
        info = const("info", [P, 2, 2])
        info_t = const("info_t", [P, 2])
        info_row = const("info_row", [P, 2], I32)
        ss = const("ss", [P, TT])
        primed = const("primed", [P, 7])
        wait_holder = const("wait_holder", [P, 1])
        x2_dram = nc.dram_tensor("x2_dram", (T, D), F32, kind="Internal").ap()
        y2_dram = nc.dram_tensor("y2_dram", (2 * T + SLOTS, D), F32, kind="Internal").ap()
        y2_in = at("y2_in", [P, TT, 2, D], F32, o_xT)
        x2_in = at("x2_in", [P, TT, D], F32, o_xT + TT * 2 * D * 4)
        psum = ctx.enter_context(nc.psum_tensor("psum", [P, 8, T], F32))
        assert place[0] <= nc.sbuf_usable_end, place[0]

        def sem(name):
            return ctx.enter_context(nc.semaphore(name))

        raw_landed = [sem(f"raw_landed{s}") for s in range(RING)]
        hi_ready, lo_ready = sem("hi_ready"), sem("lo_ready")
        half_done, w_used = sem("half_done"), sem("w_used")
        consts, const_steps, gains_landed, gains_T, gains_ready = (
            sem("consts"), sem("const_steps"), sem("gains_landed"), sem("gains_T"), sem("gains_ready"))
        x_landed, x_turned, x_act, x_dve = sem("x_landed"), sem("x_turned"), sem("x_act"), sem("x_dve")
        sq_ready, sq_summed, root_ready, rstd_ready, hf_ready, h_hi, h_lo = (
            sem("sq_ready"), sem("sq_summed"), sem("root_ready"), sem("rstd_ready"),
            sem("hf_ready"), sem("h_hi"), sem("h_lo"))
        hp_step = sem("hp_step")
        pool_added = sem("pool_added")
        sil_ready, hm_ready, hid_hi_ready, hid_lo_ready = (
            sem("sil_ready"), sem("hm_ready"), sem("hid_hi_ready"), sem("hid_lo_ready"))
        fo_added, proj_kept, o_added = sem("fo_added"), sem("proj_kept"), sem("o_added")
        z_done, abs_ready, exp_ready, ln_ready, sp_ready, sp_masked, sph_ready, spl_ready = (
            sem("z_done"), sem("abs_ready"), sem("exp_ready"), sem("ln_ready"), sem("sp_ready"),
            sem("sp_masked"), sem("sph_ready"), sem("spl_ready"))
        c_done, a_ready, a_masked, av_done, oT_hi, oT_lo = (
            sem("c_done"), sem("a_ready"), sem("a_masked"), sem("av_done"), sem("oT_hi"), sem("oT_lo"))
        stored = sem("stored")
        small_landed, wr_hi_ready, wr_lo_ready = sem("small_landed"), sem("wr_hi_ready"), sem("wr_lo_ready")
        x2_turned, x2_kept, logits_done, h_turned, rows_kept = (
            sem("x2_turned"), sem("x2_kept"), sem("logits_done"), sem("h_turned"), sem("rows_kept"))
        gap_ready, gap_exp, chosen_ready, ranks_done, tables_ready = (
            sem("gap_ready"), sem("gap_exp"), sem("chosen_ready"), sem("ranks_done"), sem("tables_ready"))
        g_row_landed, cleared = sem("g_row_landed"), sem("cleared")
        pick_ready, sel_done, sel_even, sel_odd, info_done, info_ready = (
            sem("pick_ready"), sem("sel_done"), sem("sel_even"), sem("sel_odd"), sem("info_done"),
            sem("info_ready"))
        g_half, g_summed, g_silu, u_half, u_summed, m_ready, mh_hi, mh_lo = (
            sem("g_half"), sem("g_summed"), sem("g_silu"), sem("u_half"), sem("u_summed"),
            sem("m_ready"), sem("mh_hi"), sem("mh_lo"))
        y_half, yT_ready, y_turned, y_kept, rows_stored = (
            sem("y_half"), sem("yT_ready"), sem("y_turned"), sem("y_kept"), sem("rows_stored"))
        y2_landed, sum_step, ss_ready, root_end, out_ready = (
            [sem(f"y2_landed{k}") for k in range(TT)], sem("sum_step"), sem("ss_ready"), sem("root_end"), sem("out_ready"))

        G_MIX, G_FFN, G_SCALE, G_KV = 0, 16, 32, 40

        def load(sp, c, dst, src, I=0):
            if not (isinstance(I, int) and c + 4 * I < RING):
                sp.wait_ge(lo_ready, c + 4 * I - RING + 1)
            sp.dma_start(dst, src).then_inc(raw_landed[c % RING], 16)

        def split_hi(act, c, I=0):
            act.wait_ge(raw_landed[c % RING], 16 * (c // RING + I + 1))
            if not (isinstance(I, int) and c + 4 * I < RING):
                act.wait_ge(w_used, c + 4 * I - RING + 1)
            act.activation(w_hi[:, c % RING, :], raw[:, c % RING, :], ACT.Copy).then_inc(hi_ready, 1)

        def split_lo(dve, c, I=0):
            dve.wait_ge(hi_ready, c + 4 * I + 1)
            dve.tensor_tensor(w_lo[:, c % RING, :], raw[:, c % RING, :],
                              w_hi[:, c % RING, :].bitcast(F32), ALU.subtract).then_inc(lo_ready, 1)

        def product(pe, o, whi, wlo, hi, lo, start, stop):
            pe.matmul(o, whi, hi, start=start, stop=False)
            pe.matmul(o, whi, lo, start=False, stop=False)
            return pe.matmul(o, wlo, hi, start=False, stop=stop)

        def w_tile(c, k, f, n=CW):
            s = slice(k * n + f * P, k * n + f * P + P)
            return w_hi[:, c % RING, s], w_lo[:, c % RING, s]

        def in_columns(w, c0, n=CW):
            return w.rearrange("(k p) n -> p k n", p=P)[:, :, c0:c0 + n]

        def sub3(c, k, n):
            return raw[:, c % RING, 0:k * n].rearrange("p (k n) -> p k n", k=k)

        def column_done(eng, c, f, I=0):
            eng.wait_ge(w_used if f else half_done, c + 4 * I + 1)

        PAIRS = FE_TILES // 2
        C2 = S_MOE + SUBS_IN

        def task_loop(eng, body):
            eng.wait_ge(tables_ready, 1)
            n_tasks = eng.value_load(n_tasks_i[0:1, 0:1], min_val=NE, max_val=MAX_TASKS)
            with eng.Fori(0, MAX_TASKS) as t:
                with eng.If(t < n_tasks):
                    body(t)
            return n_tasks

        block = ctx.enter_context(nc.Block())

        @block.sync
        def _(sp):
            for t in range(TT):
                sp.dma_start(x_in[:, t, :], x[0, t * P:(t + 1) * P, :]).then_inc(x_landed, 16)
            c = S_POOL
            load(sp, c, sub3(c, DT, GW), in_columns(pool_w[0].rearrange("g c n -> (g c) n"), 0))
            w_in = ffn_in[0]
            w_out = ffn_out[0].rearrange("(f p) n -> p f n", p=P)
            f0 = 0
            for half in range(2):
                nf = F_HALF[half]
                for p in range(nf // 2):
                    for u in range(2):
                        c = S_IN[half] + 2 * p + u
                        load(sp, c, sub3(c, DT, CW), in_columns(w_in, u * FF + (f0 + 2 * p) * P))
                for q in range(4):
                    for s in range(2):
                        c = S_OUT[half] + 2 * q + s
                        load(sp, c, sub3(c, nf // 2, CW),
                             w_out[:, f0 + s * (nf // 2):f0 + (s + 1) * (nf // 2), q * CW:(q + 1) * CW])
                f0 += nf
            if STOP == "ffn":
                for j in range(3):
                    load(sp, S_K + j, sub3(S_K + j, DT, CW), in_columns(w_kv, j * CW))
                sp.wait_ge(fo_added, 16)
                sp.dma_start(out.rearrange("b s d -> (b s d)").rearrange("(k p t) -> p k t", p=P, k=DT), xT[:, :, :]).then_inc(stored, 16)
                sp.wait_ge(stored, 16)
                return
            for w, s0, c0 in ((w_kv, S_K, 0), (w_kv, S_V, D), (w_q[0], S_Q, 0), (w_o[0], S_O, 0)):
                for j in range(4):
                    load(sp, s0 + j, sub3(s0 + j, DT, CW), in_columns(w, c0 + j * CW))
            if STOP == "att":
                sp.wait_ge(o_added, 8)
                sp.dma_start(out.rearrange("b s d -> (b s d)").rearrange("(k p t) -> p k t", p=P, k=DT), xT[:, :, :]).then_inc(stored, 16)
                sp.wait_ge(stored, 16)
                return

            def task_loads(t, e):
                w1 = moe_in[0][bass.ds(e, 1)].rearrange("a (k p) n -> p (a k) n", p=P)
                w2 = moe_out[0][bass.ds(e, 1)].rearrange("a (f p) n -> p (a f) n", p=P)
                T11 = t * (SUBS_TASK // RING)
                with sp.Fori(0, PAIRS // 2) as i:
                    for j in range(4):
                        c = S_MOE + j
                        load(sp, c, sub3(c, DT, CW),
                             w1[:, :, bass.ds(4 * P * i + ((j % 2) * FE + (j // 2) * CW), CW)], T11 + i)
                with sp.Fori(0, Q_OUT) as q:
                    for j in range(4):
                        load(sp, C2 + j, sub3(C2 + j, FS, CW),
                             w2[:, j * FS:(j + 1) * FS, bass.ds(CW * q, CW)], T11 + q)

            with sp.Fori(0, NE) as t:
                task_loads(t, t)
            sp.wait_ge(tables_ready, 1)
            n_tasks = sp.value_load(n_tasks_i[0:1, 0:1], min_val=NE, max_val=MAX_TASKS)
            with sp.Fori(NE, MAX_TASKS) as t:
                with sp.If(t < n_tasks):
                    task_loads(t, sp.value_load(task_e[0:1, bass.ds(t, 1)], min_val=0, max_val=NE - 1))
            for j in range(AHEAD):
                load(sp, S_MOE + j, raw[:, (S_MOE + j) % RING, 0:8], ffn_in[0, 0:P, 0:8], n_tasks * (SUBS_TASK // RING))
            sp.wait_ge(rows_stored, 32 * n_tasks + 32)
            sp.wait_ge(sel_even, DT // 2 * n_tasks + DT // 2)
            sp.wait_ge(sel_odd, DT // 2 * n_tasks + DT // 2)
            for k in range(TT):
                sp.dma_start(y2_in[:, k, :, :], y2_dram[2 * k * P:2 * (k + 1) * P, :]
                             .rearrange("(p two) d -> p two d", two=2)).then_inc(y2_landed[k], 16)
                sp.dma_start(x2_in[:, k, :], x2_dram[k * P:(k + 1) * P, :]).then_inc(y2_landed[k], 16)
            for k in range(TT):
                sp.wait_ge(out_ready, k + 1)
                sp.dma_start(out[0, k * P:(k + 1) * P, :], x2_in[:, k, :]).then_inc(stored, 16)
            sp.wait_ge(stored, 16 * TT)

        @block.gpsimd
        def _(pool):
            pool.memset(eps[:, :], EPS).then_inc(consts, 1)
            pool.memset(ones[:, :], 1.0).then_inc(consts, 1)
            pool.memset(ident[:, :], 0.0).then_inc(const_steps, 1)
            pool.memset(neg_ones[:, :].bitcast(F32), -1.0).then_inc(const_steps, 1)
            pool.iota(count[:, :], pattern=[[1, PAD]], base=1, channel_multiplier=0,
                      allow_small_or_imprecise_dtypes=True).then_inc(const_steps, 1)
            pool.memset(hp[:, :, 0:PAD], 0.0).then_inc(consts, 1)
            pool.memset(sums[:, :, 0:PAD], 0.0).then_inc(consts, 1)
            pool.wait_ge(const_steps, 3)
            pool.affine_select(out=ident[:, :], in_=ident[:, :], compare_op=ALU.not_equal, fill=1.0,
                               base=0, pattern=[[-1, P]], channel_multiplier=1).then_inc(consts, 1)
            pool.affine_select(out=neg_tri[:, :], in_=neg_ones[:, :].bitcast(F32), compare_op=ALU.is_ge,
                               fill=0.0, base=0, pattern=[[-1, P]], channel_multiplier=1).then_inc(consts, 1)
            if STOP == "ffn":
                return
            f = dict(allow_small_or_imprecise_dtypes=True)
            pool.iota(slot_iota[:, :], pattern=[[1, NT]], base=0, channel_multiplier=0, **f).then_inc(cleared, 1)
            pool.iota(e_iota[:, :], pattern=[[1, NE]], base=0, channel_multiplier=0, **f).then_inc(cleared, 1)
            pool.iota(row0[:, :], pattern=[[2 * P, TT]], base=1, channel_multiplier=2, **f).then_inc(cleared, 1)
            pool.iota(spare_row[:, :], pattern=[[P, 2]], base=2 * T + 1, channel_multiplier=1,
                      **f).then_inc(cleared, 1)
            pool.affine_select(out=earlier[:, :], in_=ones[:, :], compare_op=ALU.is_gt, fill=0.0, base=0,
                               pattern=[[1, P]], channel_multiplier=-1).then_inc(cleared, 1)

            def diagonals(n, ready, done):
                pool.wait_ge(ready, n + 1)
                for s in range(TT):
                    d = E[:, n % 2 if isinstance(n, int) else 0, SEG[s]:SEG[s] + P]
                    i = pool.affine_select(out=d, in_=d, compare_op=ALU.is_gt, fill=0.0, base=0,
                                           pattern=[[1, P]], channel_multiplier=-1)
                i.then_inc(done, 1)

            for h in range(NH + 1):
                if h < NH:
                    diagonals(h, sp_ready, sp_masked)
                    pool.wait_ge(sp_masked, h + 1)
                    if h >= 2:
                        pool.wait_ge(c_done, h - 1)
                    pool.tensor_copy(sp_hi[:, h % 2, :], E[:, h % 2, :]).then_inc(sph_ready, 1)
                if h >= 1:
                    diagonals(h - 1, a_ready, a_masked)
            if STOP == "att":
                return
            pool.wait_ge(x2_kept, 8)
            for h in range(2):
                pool.dma_start(x2_dram[h * 256:(h + 1) * 256, :].rearrange("(t p) d -> p t d", p=P),
                               x2_rows[:, 2 * h:2 * h + 2, :]).then_inc(rows_stored, 16)
            pool.wait_ge(rows_stored, 32)
            pool.memset(pick[:, :, NT:].bitcast(F32), 0.0).then_inc(cleared, 1)
            pool.wait_ge(rows_kept, 16)
            pool.memset(yT[:, :, :, NT:], 0.0).then_inc(cleared, 1)

            def task(t):
                with pool.Fori(0, PAIRS // 2) as i:
                    for p in range(2):
                        n = PAIRS * t + 2 * i + p
                        place_ = bass.ds(4 * i + 2 * p, 2)
                        pool.wait_ge(m_ready, n + 3)
                        pool.tensor_copy(hid[:, 0, place_, :], up_s[:, p, :, :]).then_inc(mh_hi, 1)
                        pool.wait_ge(mh_hi, n + 1)
                        pool.tensor_tensor(hid[:, 1, place_, :], up_s[:, p, :, :],
                                           hid[:, 0, place_, :].bitcast(F32), ALU.subtract).then_inc(mh_lo, 1)
                pool.wait_ge(y_kept, 4 * t + 6)
                pool.tensor_tensor(wait_holder[:, :], eps[:, :], eps[:, :], ALU.add)
                for b, n in enumerate((P, NT - P)):
                    pool.indirect_dma_start(
                        out=y2_dram[:, :],
                        out_offset=bass.IndirectOffsetOnAxis(ap=info_row[0:n, b:b + 1].bitcast(U32), axis=0),
                        in_=y_rows[0:n, b, :], in_offset=None).then_inc(rows_stored, 16)

            for k in range(2):
                pool.memset(ss[:, k:k + 1], 0.0).then_inc(mh_lo, 1)
            task_loop(pool, task)

        @block.scalar
        def _(act):
            rows = lambda v: v.rearrange("l (t p) -> (l t) p", p=P)
            act.dma_start(gains_in[G_MIX:G_MIX + 16, :], rows(g_mix)).then_inc(gains_landed, 16)
            act.dma_start(gains_in[G_FFN:G_FFN + 16, :], rows(g_ffn)).then_inc(gains_landed, 16)
            act.dma_start(gains_in[G_SCALE:G_SCALE + 8, :], rows(pool_scale)).then_inc(gains_landed, 16)
            act.dma_start(gains_in[G_KV:G_KV + 8, :], g_kv.rearrange("(t p) -> t p", p=P)).then_inc(gains_landed, 16)
            act.dma_start(wr[:, :, :], w_router[0].rearrange("(k p) e -> p k e", p=P)).then_inc(small_landed, 16)

            def norm(n, final=None, first=0, bank=0):
                for d in range(DT):
                    if final is not None:
                        act.wait_ge(final, first + d + 1)
                    if d >= 2 or n:
                        act.wait_ge(sq_summed, DT * n + d - 1)
                    act.activation(tmp[:, d % 2, :], xT[:, d, :], ACT.Square).then_inc(sq_ready, 1)
                act.wait_ge(sq_summed, DT * (n + 1))
                act.activation(tmp[:, 2, :], psum[:, bank, :], ACT.Sqrt, bias=eps[:, :],
                               scale=1.0 / D).then_inc(root_ready, 1)

            def h_round(n):
                for d in range(DT):
                    act.wait_ge(hf_ready, DT * n + d + 1)
                    act.activation(hT_hi[:, d, :], tmp[:, 3 + d % 2, :], ACT.Copy).then_inc(h_hi, 1)

            for d in range(0, DT, 2):
                act.wait_ge(x_turned, d + 1)
                act.activation(xT[:, d, :], psum[:, d, :], ACT.Copy).then_inc(x_act, 1)
            act.wait_ge(x_dve, DT // 2)
            act.wait_ge(x_act, DT // 2)
            act.wait_ge(consts, 6)
            norm(0)
            h_round(0)
            for c in range(AHEAD):
                split_hi(act, c)

            def hidden(c, F, I):
                column_done(act, c, F % 2, I)
                if F >= 2 or not isinstance(I, int):
                    act.wait_ge(hm_ready, F + 4 * I - 1)
                act.activation(tmp[:, F % 2, :], psum[:, F % 2, :], ACT.Silu).then_inc(sil_ready, 1)

            def hidden_round(F, I, place_):
                act.wait_ge(hm_ready, F + 4 * I + 1)
                act.activation(place_, tmp[:, 3 + F % 2, :], ACT.Copy).then_inc(hid_hi_ready, 1)

            split_hi(act, S_FFN + 2)
            norm(1, pool_added)
            h_round(1)
            f0 = 0
            for half in range(2):
                nf = F_HALF[half]
                if half == 1:
                    column_done(act, S_OUT[0] + 7, 1)

                def pair(p, I):
                    c = S_IN[half] + 2 * p + AHEAD
                    split_hi(act, c, I)
                    for f in range(2):
                        hidden(c - AHEAD, f0 + 2 * p + f, I)
                    split_hi(act, c + 1, I)
                    for f in range(2):
                        hidden_round(f0 + 2 * p + f, I, hid_hi[:, bass.ds(2 * p + f + 4 * I, 1), :]
                                     .rearrange("p a t -> p (a t)"))
                pair(0, 0)
                pair(1, 0)
                with act.Fori(1, nf // 4) as i:
                    pair(0, i)
                    pair(1, i)
                if nf % 4:
                    pair(nf // 2 - 1, 0)
                for j in range(8):
                    split_hi(act, S_OUT[half] + j + AHEAD)
                f0 += nf
            if STOP == "ffn":
                return
            norm(2, fo_added, DT)
            h_round(2)
            for j in range(4):
                split_hi(act, S_K + j + AHEAD)
                for f in range(2):
                    n = 2 * j + f
                    column_done(act, S_K + j, f)
                    act.activation(KT[:, n, :], psum[:, n % 4, :], ACT.Copy).then_inc(proj_kept, 1)
            for j in range(4):
                split_hi(act, S_V + j + AHEAD)
                for t in range(TT):
                    column_done(act, S_V + j, 1)
                    act.activation(V[:, t, j * CW:(j + 1) * CW], psum[:, 4 * (j % 2) + t, 0:CW],
                                   ACT.Copy).then_inc(proj_kept, 1)
            h_round(3)
            for j in range(4):
                if j + AHEAD < 4:
                    split_hi(act, S_Q + j + AHEAD)
                for f in range(2):
                    n = 3 * DT + 2 * j + f
                    column_done(act, S_Q + j, f)
                    act.activation(QT[:, 2 * j + f, :], psum[:, n % 4, :], ACT.Copy,
                                   scale=HD ** -0.5).then_inc(proj_kept, 1)
            for h in range(NH + 3):
                if h < NH:
                    e = E[:, h % 2, :]
                    act.wait_ge(z_done, h + 1)
                    if h >= 2:
                        act.wait_ge(av_done, h - 1)
                    for b, (lo, hi) in enumerate(((0, 512), (512, 1024), (1024, HC))):
                        i = act.activation(E[:, h % 2, lo:hi], psum[:, 3 * (h % 2) + b, 0:hi - lo], ACT.Abs)
                    i.then_inc(abs_ready, 1)
                    act.wait_ge(abs_ready, h + 1)
                    act.activation(e, e, ACT.Exp, scale=-1.0).then_inc(exp_ready, 1)
                    act.wait_ge(exp_ready, h + 1)
                    act.activation(e, e, ACT.Ln, bias=1.0).then_inc(ln_ready, 1)
                if 1 <= h <= NH:
                    n = h - 1
                    act.wait_ge(c_done, n + 1)
                    for b, (lo, hi) in enumerate(((0, 512), (512, 1024), (1024, HC))):
                        i = act.activation(E[:, n % 2, lo:hi], psum[:, 3 * (n % 2) + b, 0:hi - lo], ACT.Exp)
                    i.then_inc(a_ready, 1)
                if h % 2 == 0 and h >= 4:
                    p = (h - 4) // 2
                    act.wait_ge(av_done, 2 * p + 2)
                    act.activation(hT_hi[:, p, :], psum[:, 6 + p % 2, :], ACT.Copy).then_inc(oT_hi, 1)
            for j in range(3):
                split_hi(act, S_O + j)
            split_hi(act, S_O + 3)
            if STOP == "att":
                return
            act.wait_ge(small_landed, 16)
            act.activation(wr_hi[:, :, :], wr[:, :, :], ACT.Copy).then_inc(wr_hi_ready, 1)
            norm(3, o_added, 0, 4)
            X2_BANKS = (0, 1, 2, 3, 5, 6, 7, 4)
            for n in range(8):
                act.wait_ge(x2_turned, n + 1)
                act.activation(x2_rows[:, n // 2, (n % 2) * 512:(n % 2) * 512 + 512], psum[:, X2_BANKS[n], :],
                               ACT.Copy).then_inc(x2_kept, 1)
            h_round(4)
            for m in range(16):
                if m == 4:
                    act.wait_ge(gap_ready, 1)
                    act.activation(gates[:, 1, :], gates[:, 0, :], ACT.Exp).then_inc(gap_exp, 1)
                part, t, half = m // 8, (m // 2) % 4, m % 2
                act.wait_ge(h_turned, m + 1)
                act.activation((rows_lo if part else rows_hi)[:, t, half * 512:half * 512 + 512],
                               psum[:, (1, 2, 3, 5, 6, 7)[m % 6], :], ACT.Copy).then_inc(rows_kept, 1)
            act.wait_ge(rows_stored, 32)
            act.dma_start(g_row[:, :], g_final.partition_broadcast(P)).then_inc(g_row_landed, 16)
            for j in range(AHEAD):
                split_hi(act, S_MOE + j)

            def select(t):
                for k in range(0, DT, 2):
                    act.wait_ge(sel_done, DT * t + k + 1)
                    act.activation(x_sel[:, :, k, :], psum[:, k % 4, 0:2 * NT].rearrange("p (a n) -> p a n", a=2),
                                   ACT.Copy).then_inc(sel_even, 1)

            act.wait_ge(tables_ready, 1)
            select(0)

            def task(t):
                T11 = t * (SUBS_TASK // RING)
                with act.Fori(0, PAIRS // 2) as i:
                    for p in range(2):
                        n = PAIRS * t + 2 * i + p
                        c = S_MOE + 2 * p
                        split_hi(act, c + AHEAD, T11 + i)
                        column_done(act, c, 1, T11 + i)
                        act.wait_ge(m_ready, n + 1)
                        act.activation(gate_s[:, p, :, :], psum[:, 0:2, NT:2 * NT], ACT.Copy).then_inc(g_half, 1)
                        split_hi(act, c + 1 + AHEAD, T11 + i)
                        act.wait_ge(g_summed, n + 2)
                        act.activation(gate_s[:, p, :, :], gate_s[:, p, :, :], ACT.Silu).then_inc(g_silu, 1)
                        column_done(act, c + 1, 1, T11 + i)
                        act.wait_ge(mh_lo, n + 1)
                        act.activation(up_s[:, p, :, :], psum[:, 2:4, NT:2 * NT], ACT.Copy).then_inc(u_half, 1)
                for q in range(Q_OUT):
                    for j in range(4):
                        split_hi(act, C2 + 4 * q + j + AHEAD, T11)
                    column_done(act, C2 + 4 * q + 3, 1, T11)
                    b = 4 + 2 * (q % 2)
                    if q >= 2:
                        act.wait_ge(yT_ready, 4 * t + q - 1)
                    act.activation(y_s[:, q % 2, :, :], psum[:, b:b + 2, NT:2 * NT], ACT.Copy).then_inc(y_half, 1)
                select(t + 1)

            task_loop(act, task)
            for k in range(TT):
                act.wait_ge(sum_step, 2 * k + 2)
                act.activation(y2_in[:, k, 0, :], x2_in[:, k, :], ACT.Square,
                               accum_out=ss[:, k:k + 1]).then_inc(ss_ready, 1)
            act.wait_ge(ss_ready, TT)
            act.activation(ss[:, :], ss[:, :], ACT.Sqrt, bias=eps[:, :], scale=1.0 / D).then_inc(root_end, 1)

        @block.vector
        def _(dve):
            steps = [0]

            def chained(i):
                steps[0] += 1
                i.then_inc(hp_step, 1)
                dve.wait_ge(hp_step, steps[0])

            dve.wait_ge(const_steps, 3)
            chained(dve.reciprocal(inv_count[:, :], count[:, :]))
            dve.wait_ge(gains_T, 1)
            dve.tensor_copy(gains[:, :], psum[:, 7, 0:NV]).then_inc(gains_ready, 1)
            for d in range(1, DT, 2):
                dve.wait_ge(x_turned, d + 1)
                dve.tensor_copy(xT[:, d, :], psum[:, d, :]).then_inc(x_dve, 1)
            dve.wait_ge(x_act, DT // 2)
            dve.wait_ge(x_dve, DT // 2)

            def rstd(n):
                dve.wait_ge(root_ready, n + 1)
                dve.reciprocal(tmp[:, 2, :], tmp[:, 2, :]).then_inc(rstd_ready, 1)
                dve.wait_ge(rstd_ready, n + 1)

            def normed(o, d, g):
                return dve.scalar_tensor_tensor(o, xT[:, d, :], gains[:, g + d:g + d + 1],
                                                tmp[:, 2, :], ALU.mult, ALU.mult)

            def h_minus(n, d):
                dve.wait_ge(h_hi, DT * n + d + 1)
                dve.tensor_tensor(hT_lo[:, d, :], tmp[:, 3 + d % 2, :], hT_hi[:, d, :].bitcast(F32),
                                  ALU.subtract).then_inc(h_lo, 1)

            def norm_tiles(n, g):
                for d in range(DT):
                    if d >= 2:
                        dve.wait_ge(h_lo, DT * n + d - 1)
                    normed(tmp[:, 3 + d % 2, :], d, g).then_inc(hf_ready, 1)
                    if d:
                        h_minus(n, d - 1)
                h_minus(n, DT - 1)

            dve.wait_ge(gains_ready, 1)
            dve.wait_ge(consts, 6)
            rstd(0)
            for d in range(DT):
                gi = d // 2
                w = WINDOWS[gi]
                cur = hp[:, d % 2, :]
                chained(normed(cur[:, PAD:], d, G_MIX))
                span = 1
                s = cur
                while span < w:
                    nxt = sums[:, (0 if span == 1 else 1 if s is not None and span == 2 else 2 if span == 4 else 3), :]
                    chained(dve.tensor_tensor(nxt[:, PAD:], s[:, PAD:], s[:, PAD - span:PAD + T - span], ALU.add))
                    s = nxt
                    span *= 2
                if d >= 2:
                    dve.wait_ge(h_lo, d - 1)
                o = tmp[:, 3 + d % 2, :]
                chained(dve.scalar_tensor_tensor(o, s[:, PAD:], 1.0 / w, cur[:, PAD:], ALU.mult, ALU.subtract))
                chained(dve.tensor_tensor(sums[:, 3, PAD:PAD + w], s[:, PAD:PAD + w], inv_count[:, 0:w], ALU.mult))
                dve.tensor_tensor(o[:, 0:w], sums[:, 3, PAD:PAD + w], cur[:, PAD:PAD + w],
                                  ALU.subtract).then_inc(hf_ready, 1)
                h_minus(0, d)
            for c in range(0, AHEAD):
                split_lo(dve, c)
            split_lo(dve, S_FFN + 2)
            for d in range(DT):
                column_done(dve, S_POOL, d // 4)
                dve.scalar_tensor_tensor(xT[:, d, :], psum[:, d, :], gains[:, G_SCALE + d:G_SCALE + d + 1],
                                         xT[:, d, :], ALU.mult, ALU.add).then_inc(pool_added, 1)
            rstd(1)
            norm_tiles(1, G_FFN)
            f0 = 0
            for half in range(2):
                nf = F_HALF[half]

                def pair(p, I):
                    c = S_IN[half] + 2 * p + AHEAD
                    split_lo(dve, c, I)
                    F = f0 + 2 * p
                    for f in range(2):
                        dve.wait_ge(sil_ready, F + f + 4 * I + 1)
                        column_done(dve, c - AHEAD + 1, f, I)
                        if F + f >= 2 or not isinstance(I, int):
                            dve.wait_ge(hid_lo_ready, F + f + 4 * I - 1)
                        dve.tensor_tensor(tmp[:, 3 + (F + f) % 2, :], tmp[:, (F + f) % 2, :],
                                          psum[:, 2 + (F + f) % 2, :], ALU.mult).then_inc(hm_ready, 1)
                    split_lo(dve, c + 1, I)
                    for f in range(2):
                        dve.wait_ge(hid_hi_ready, F + f + 4 * I + 1)
                        q = bass.ds(2 * p + f + 4 * I, 1)
                        flat = lambda a: a.rearrange("p a t -> p (a t)")
                        dve.tensor_tensor(flat(hid_lo[:, q, :]), tmp[:, 3 + (F + f) % 2, :],
                                          flat(hid_hi[:, q, :]).bitcast(F32), ALU.subtract).then_inc(hid_lo_ready, 1)
                pair(0, 0)
                pair(1, 0)
                with dve.Fori(1, nf // 4) as i:
                    pair(0, i)
                    pair(1, i)
                if nf % 4:
                    pair(nf // 2 - 1, 0)
                for q in range(4):
                    for s in range(2):
                        split_lo(dve, S_OUT[half] + 2 * q + s + AHEAD)
                    for dd in range(2):
                        d = 2 * q + dd
                        column_done(dve, S_OUT[half] + 2 * q + 1, dd)
                        dve.tensor_tensor(xT[:, d, :], xT[:, d, :], psum[:, 4 + d % 4, :],
                                          ALU.add).then_inc(fo_added, 1)
                f0 += nf
            if STOP == "ffn":
                return
            rstd(2)
            norm_tiles(2, G_KV)
            for j in range(8):
                split_lo(dve, S_K + j + AHEAD)
            column_done(dve, S_V + 3, 1)
            norm_tiles(3, G_MIX + DT)
            split_lo(dve, S_Q + 3)

            def over(n):
                return ((b, lo, hi) for b, (lo, hi) in enumerate(((0, 512), (512, 1024), (1024, HC))))
            for h in range(NH + 3):
                if 1 <= h <= NH:
                    n = h - 1
                    dve.wait_ge(sph_ready, n + 1)
                    dve.tensor_tensor(sp_lo[:, n % 2, :], E[:, n % 2, :], sp_hi[:, n % 2, :].bitcast(F32),
                                      ALU.subtract).then_inc(spl_ready, 1)
                if h < NH:
                    dve.wait_ge(ln_ready, h + 1)
                    for b, lo, hi in over(h):
                        e = E[:, h % 2, lo:hi]
                        i = dve.scalar_tensor_tensor(e, psum[:, 3 * (h % 2) + b, 0:hi - lo], 0.0, e,
                                                     ALU.max, ALU.add)
                    i.then_inc(sp_ready, 1)
                if h % 2 == 0 and h >= 4:
                    p = (h - 4) // 2
                    dve.wait_ge(oT_hi, p + 1)
                    dve.tensor_tensor(hT_lo[:, p, :], psum[:, 6 + p % 2, :], hT_hi[:, p, :].bitcast(F32),
                                      ALU.subtract).then_inc(oT_lo, 1)
            for j in range(3):
                split_lo(dve, S_O + j)
            split_lo(dve, S_O + 3)
            for d in range(DT):
                column_done(dve, S_O + d // 2, d % 2)
                dve.tensor_tensor(xT[:, d, :], xT[:, d, :], psum[:, d % 4, :], ALU.add).then_inc(o_added, 1)
            if STOP == "att":
                return
            dve.wait_ge(wr_hi_ready, 1)
            dve.tensor_tensor(wr_lo[:, :, :], wr[:, :, :], wr_hi[:, :, :].bitcast(F32),
                              ALU.subtract).then_inc(wr_lo_ready, 1)
            rstd(3)
            norm_tiles(4, G_FFN + DT)

            dve.wait_ge(h_lo, 5 * DT)
            dve.wait_ge(cleared, 5)
            dve.wait_ge(logits_done, 1)
            chained(dve.tensor_copy(logits[:, :, :], psum[:, 0, 0:TT * NE].rearrange("p (t e) -> p t e", e=NE)))
            for t in range(TT):
                chained(dve.max(top_v[:, t, :], logits[:, t, :]))
                i = dve.max_index(top_i[:, t, :], top_v[:, t, :], logits[:, t, :])
            chained(i)
            dve.tensor_tensor(gates[:, 0, :], top_v[:, :, 1], top_v[:, :, 0], ALU.subtract).then_inc(gap_ready, 1)
            chained(dve.tensor_copy(top_f[:, :, :], top_i[:, :, :]))
            for t in range(TT):
                dve.tensor_scalar(first[:, t, :], e_iota[:, :], top_f[:, t, 0:1], None, ALU.is_equal)
                i = dve.tensor_scalar(second[:, t, :], e_iota[:, :], top_f[:, t, 1:2], None, ALU.is_equal)
            chained(i)
            dve.tensor_tensor(chosen[:, :, :], first[:, :, :], second[:, :, :], ALU.add).then_inc(chosen_ready, 1)
            dve.wait_ge(gap_exp, 1)
            chained(dve.tensor_scalar(gates[:, 0, :], gates[:, 1, :], 1.0, None, ALU.add))
            chained(dve.reciprocal(gates[:, 2, :], gates[:, 0, :]))
            chained(dve.tensor_tensor(gates[:, 3, :], gates[:, 1, :], gates[:, 2, :], ALU.mult))
            for t in range(TT):
                i = dve.tensor_scalar(gate_e[:, t, :], second[:, t, :], gates[:, 3, t:t + 1], None, ALU.mult)
            chained(i)
            for t in range(TT):
                dve.scalar_tensor_tensor(gate_e[:, t, :], first[:, t, :], gates[:, 2, t:t + 1], gate_e[:, t, :],
                                         ALU.mult, ALU.add)
                i = dve.tensor_scalar(row_e[:, t, :], second[:, t, :], row0[:, t:t + 1], None, ALU.add)
            chained(i)
            FAR = 8192.0
            dve.wait_ge(ranks_done, 1)
            chained(dve.scalar_tensor_tensor(rank[:, :, :], psum[:, 4, 0:TT * NE].rearrange("p (t e) -> p t e", e=NE),
                                             FAR, chosen[:, :, :], ALU.add, ALU.mult))
            dve.tensor_scalar(rank[:, :, :], rank[:, :, :], -FAR, None, ALU.add)
            chained(dve.tensor_copy(cnt[:, :], psum[:, 4, 64:64 + NE]))
            ks = range(1, (T - 1) // NT + 1)
            chained(dve.tensor_scalar(extra[:, 0, :], cnt[:, :], float(NT), None, ALU.is_gt))
            for k in ks[1:]:
                chained(dve.scalar_tensor_tensor(extra[:, (k - 1) % 3, :], cnt[:, :], float(k * NT),
                                                 extra[:, (k - 2) % 3, :], ALU.is_gt, ALU.add))
            ex = extra[:, (ks[-1] - 1) % 3, :]
            chained(dve.memset(cum[:, :, :], 0.0))
            chained(dve.tensor_copy(cum[:, 0, 4:], ex))
            for r in range(3):
                chained(dve.tensor_tensor(cum[:, r + 1, 4:], cum[:, r, 4:], cum[:, r, 4 - 2 ** r:4 - 2 ** r + NE],
                                          ALU.add))
            upto = cum[:, 3, 4:]
            chained(dve.tensor_tensor(before[:, :], upto, ex, ALU.subtract))
            dve.tensor_scalar(n_f[:, :], cum[:, 3, 3 + NE:4 + NE], float(NE), None, ALU.add)
            XT = TC - NE
            for j in range(XT):
                dve.tensor_scalar(is_past[:, 0, j, :], upto, float(j), None, ALU.is_le)
                dve.tensor_scalar(is_past[:, 1, j, :], before[:, :], float(j), None, ALU.is_le)
                i = dve.tensor_scalar(start[:, NE + j, :], before[:, :], float(NT), float(1 - (1 + j) * NT),
                                      ALU.mult, ALU.add)
            i = dve.memset(start[:, 0:NE, :], 1.0)
            for t in range(NE):
                i = dve.tensor_scalar(is_mine[:, t, :], e_iota[:, :], float(t), None, ALU.is_equal)
            chained(i)
            chained(dve.tensor_tensor(is_mine[:, NE:, :], is_past[:, 1, :, :], is_past[:, 0, :, :], ALU.subtract))

            def over_tasks(a):
                return a[:, :, :].unsqueeze(2).to_broadcast([P, TT, TC, NE])

            def over_tokens(a):
                return a[:, :, :].unsqueeze(1).to_broadcast([P, TT, TC, NE])

            chained(dve.tensor_reduce(e_f[:, NE:], is_past[:, 0, :, :], AX_X, ALU.add))
            chained(dve.tensor_copy(e_f[:, 0:NE], e_iota[:, :]))
            chained(dve.tensor_scalar(e_f[:, :], e_f[:, :], float(NE - 1), None, ALU.min))
            chained(dve.tensor_copy(task_e[:, :], e_f[:, :]))
            chained(dve.tensor_copy(n_tasks_i[:, :], n_f[:, :]))
            chained(dve.tensor_tensor(wide[:, :, :, :], over_tasks(rank), over_tokens(start), ALU.add))
            chained(dve.tensor_tensor(wide[:, :, :, :], wide[:, :, :, :], over_tokens(is_mine), ALU.mult))
            chained(dve.tensor_reduce(pos[:, :, :], wide[:, :, :, :], AX_X, ALU.add))
            chained(dve.tensor_scalar(pos[:, :, :], pos[:, :, :], -1.0, None, ALU.add))
            for n, a in enumerate((row_e, gate_e)):
                chained(dve.tensor_tensor(wide[:, :, :, :], over_tasks(a), over_tokens(is_mine), ALU.mult))
                chained(dve.tensor_reduce(row_gate[:, :, :, n], wide[:, :, :, :], AX_X, ALU.add))
            dve.memset(primed[:, 0:1], 0.0).then_inc(tables_ready, 1)
            for j in range(AHEAD):
                split_lo(dve, S_MOE + j)
            for k, first_count in enumerate((m_ready, m_ready, y_kept, y_kept, g_summed, u_summed)):
                dve.memset(primed[:, k + 1:k + 2], 0.0).then_inc(first_count, 1)
            dve.wait_ge(cleared, 7)
            dve.wait_ge(g_summed, 1)

            def picks(t):
                for k in range(TT):
                    i = dve.tensor_scalar(pick[:, k, 0:NT], slot_iota[:, :], flat3(pos[:, k, bass.ds(t, 1)]), None,
                                          ALU.is_equal)
                i.then_inc(pick_ready, 1)

            def flat3(a):
                return a

            def select(t):
                for k in range(1, DT, 2):
                    dve.wait_ge(sel_done, DT * t + k + 1)
                    dve.tensor_copy(x_sel[:, :, k, :], psum[:, k % 4, 0:2 * NT]
                                    .rearrange("p (a n) -> p a n", a=2)).then_inc(sel_odd, 1)

            def keep_rows(t, q):
                dve.wait_ge(y_turned, 4 * t + q + 1)
                b = 4 + 2 * (q % 2)
                cols = slice(q * CW, (q + 1) * CW)
                dve.tensor_scalar(y_rows[:, 0, cols], psum[:, b, 0:CW], info[:, 0, 1:2], None, ALU.mult)
                dve.tensor_scalar(y_rows[0:NT - P, 1, cols], psum[0:NT - P, b, CW:2 * CW],
                                  info[0:NT - P, 1, 1:2], None, ALU.mult).then_inc(y_kept, 1)

            picks(0)
            select(0)

            def task(t):
                T11 = t * (SUBS_TASK // RING)
                with dve.Fori(0, PAIRS // 2) as i:
                    for p in range(2):
                        n = PAIRS * t + 2 * i + p
                        c = S_MOE + 2 * p
                        split_lo(dve, c + AHEAD, T11 + i)
                        dve.wait_ge(g_half, n + 1)
                        dve.tensor_tensor(gate_s[:, p, :, :], gate_s[:, p, :, :], psum[:, 0:2, 0:NT],
                                          ALU.add).then_inc(g_summed, 1)
                        split_lo(dve, c + 1 + AHEAD, T11 + i)
                        dve.wait_ge(u_half, n + 1)
                        dve.tensor_tensor(up_s[:, p, :, :], up_s[:, p, :, :], psum[:, 2:4, 0:NT],
                                          ALU.add).then_inc(u_summed, 1)
                        dve.wait_ge(g_silu, n + 1)
                        dve.wait_ge(u_summed, n + 2)
                        dve.tensor_tensor(up_s[:, p, :, :], up_s[:, p, :, :], gate_s[:, p, :, :],
                                          ALU.mult).then_inc(m_ready, 1)
                dve.wait_ge(info_done, t + 1)
                dve.wait_ge(rows_stored, 32 * t + 32)
                dve.tensor_copy(info[:, :, :], psum[:, 5, 0:4].rearrange("p (a b) -> p a b", a=2)).then_inc(info_ready, 1)
                dve.wait_ge(info_ready, 3 * t + 1)
                dve.scalar_tensor_tensor(info_t[:, :], info[:, :, 0], 0.0, spare_row[:, :],
                                         ALU.is_equal, ALU.mult).then_inc(info_ready, 1)
                dve.wait_ge(info_ready, 3 * t + 2)
                dve.scalar_tensor_tensor(info_row[:, :], info[:, :, 0], -1.0, info_t[:, :],
                                         ALU.add, ALU.add).then_inc(info_ready, 1)
                for q in range(Q_OUT):
                    for j in range(4):
                        split_lo(dve, C2 + 4 * q + j + AHEAD, T11)
                        if j == 1 and q:
                            keep_rows(t, q - 1)
                    dve.wait_ge(y_half, 4 * t + q + 1)
                    b = 4 + 2 * (q % 2)
                    dve.tensor_tensor(yT[:, q % 2, :, 0:NT], y_s[:, q % 2, :, :], psum[:, b:b + 2, 0:NT],
                                      ALU.add).then_inc(yT_ready, 1)
                picks(t + 1)
                select(t + 1)
                keep_rows(t, Q_OUT - 1)

            task_loop(dve, task)
            for k in range(TT):
                dve.wait_ge(y2_landed[k], 32)
                dve.tensor_tensor(y2_in[:, k, 0, :], y2_in[:, k, 0, :], y2_in[:, k, 1, :],
                                  ALU.add).then_inc(sum_step, 1)
                dve.wait_ge(sum_step, 2 * k + 1)
                dve.tensor_tensor(x2_in[:, k, :], x2_in[:, k, :], y2_in[:, k, 0, :], ALU.add).then_inc(sum_step, 1)
            dve.wait_ge(root_end, 1)
            chained(dve.reciprocal(ss[:, :], ss[:, :]))
            dve.wait_ge(g_row_landed, 16)
            for k in range(TT):
                dve.scalar_tensor_tensor(x2_in[:, k, :], x2_in[:, k, :], ss[:, k:k + 1], g_row[:, :],
                                         ALU.mult, ALU.mult).then_inc(out_ready, 1)

        @block.tensor
        def _(pe):
            pe.wait_ge(consts, 6)
            pe.wait_ge(gains_landed, 64)
            pe.transpose(psum[:, 7, 0:NV], gains_in[:, :], ident[0:NV, 0:NV]).then_inc(gains_T, 1)
            pe.wait_ge(x_landed, 16 * TT)
            for d in range(DT):
                if d == 7:
                    pe.wait_ge(gains_ready, 1)
                for t in range(TT):
                    i = pe.transpose(psum[:, d, t * P:(t + 1) * P], x_in[:, t, d * P:(d + 1) * P], ident[:, :])
                i.then_inc(x_turned, 1)

            def norm(n, bank=0):
                for d in range(DT):
                    pe.wait_ge(sq_ready, DT * n + d + 1)
                    pe.matmul(psum[:, bank, :], ones[:, :], tmp[:, d % 2, :], start=d == 0,
                              stop=d == DT - 1).then_inc(sq_summed, 1)

            norm(0)
            for d in range(DT):
                if d == 0:
                    pe.wait_ge(lo_ready, 1)
                pe.wait_ge(h_lo, 2 * (d // 2) + 2)
                for k in range(2):
                    n0 = (d // 2) * 2 * GW + k * GW + (d % 2) * P
                    i = product(pe, psum[:, d, :], w_hi[:, 0, n0:n0 + P], w_lo[:, 0, n0:n0 + P],
                                hT_hi[:, 2 * (d // 2) + k, :], hT_lo[:, 2 * (d // 2) + k, :], k == 0, k == 1)
                if d % 4 == 3:
                    i.then_inc(w_used if d == DT - 1 else half_done, 1)
            norm(1)
            pe.wait_ge(h_lo, 2 * DT)
            f0 = 0
            for half in range(2):
                nf = F_HALF[half]

                def pair(p, I):
                    for u in range(2):
                        c = S_IN[half] + 2 * p + u
                        pe.wait_ge(lo_ready, c + 4 * I + 1)
                        for f in range(2):
                            F = f0 + 2 * p + f
                            if F >= 2 or not isinstance(I, int):
                                pe.wait_ge(hm_ready if u else sil_ready, F + 4 * I - 1)
                            for k in range(DT):
                                i = product(pe, psum[:, 2 * u + f, :], *w_tile(c, k, f), hT_hi[:, k, :],
                                            hT_lo[:, k, :], k == 0, k == DT - 1)
                            i.then_inc(w_used if f else half_done, 1)

                pair(0, 0)
                pair(1, 0)
                with pe.Fori(1, nf // 4) as i_:
                    pair(0, i_)
                    pair(1, i_)
                if nf % 4:
                    pair(nf // 2 - 1, 0)
                for q in range(4):
                    for s in range(2):
                        c = S_OUT[half] + 2 * q + s
                        pe.wait_ge(lo_ready, c + 1)
                        if q == 0:
                            pe.wait_ge(hid_lo_ready, f0 + (s + 1) * (nf // 2))
                        for dd in range(2):
                            d = 2 * q + dd
                            if s == 0 and DT * half + d >= 4:
                                pe.wait_ge(fo_added, DT * half + d - 3)
                            for f in range(nf // 2):
                                F = s * (nf // 2) + f
                                i = product(pe, psum[:, 4 + d % 4, :], *w_tile(c, f, dd), hid_hi[:, F, :],
                                            hid_lo[:, F, :], F == 0, F == nf - 1)
                            i.then_inc(w_used if dd else half_done, 1)
                f0 += nf
            if STOP == "ffn":
                return

            def project(s0, n0, free):
                for j in range(4):
                    c = s0 + j
                    pe.wait_ge(lo_ready, c + 1)
                    for f in range(2):
                        n = n0 + 2 * j + f
                        if n >= 4:
                            pe.wait_ge(free, n - 3)
                        for k in range(DT):
                            i = product(pe, psum[:, n % 4, :], *w_tile(c, k, f), hT_hi[:, k, :],
                                        hT_lo[:, k, :], k == 0, k == DT - 1)
                        i.then_inc(w_used if f else half_done, 1)

            norm(2)
            pe.wait_ge(h_lo, 3 * DT)
            project(S_K, 0, proj_kept)
            for j in range(4):
                c = S_V + j
                pe.wait_ge(lo_ready, c + 1)
                for t in range(TT):
                    n = DT + 4 * j + t
                    pe.wait_ge(proj_kept, n - 7 if j >= 2 else DT)
                    for k in range(DT):
                        ts = slice(t * P, (t + 1) * P)
                        o = psum[:, 4 * (j % 2) + t, 0:CW]
                        wh, wl = (w[:, c % RING, k * CW:(k + 1) * CW] for w in (w_hi, w_lo))
                        pe.matmul(o, hT_hi[:, k, ts], wh, start=k == 0, stop=False)
                        pe.matmul(o, hT_hi[:, k, ts], wl, start=False, stop=False)
                        i = pe.matmul(o, hT_lo[:, k, ts], wh, start=False, stop=k == DT - 1)
                    if t % 2:
                        i.then_inc(w_used if t == TT - 1 else half_done, 1)
            pe.wait_ge(h_lo, 4 * DT)
            project(S_Q, 3 * DT, proj_kept)
            pe.wait_ge(proj_kept, 4 * DT)
            for h in range(NH + 2):
                if h < NH:
                    r = slice(HD * (h % 2), HD * (h % 2) + HD)
                    if h >= 2:
                        pe.wait_ge(a_ready, h - 1)
                    for b, blocks in enumerate(((0,), (1, 3), (2,))):
                        col = 0
                        for s in blocks:
                            n = T - s * P
                            i = pe.matmul(psum[:, 3 * (h % 2) + b, col:col + n], KT[r, h // 2, s * P:(s + 1) * P],
                                          QT[r, h // 2, s * P:T], start=col == 0, stop=False,
                                          skip_group_check=True)
                            col += n
                    i.then_inc(z_done, 1)
                if h >= 2:
                    n = h - 2
                    pe.wait_ge(a_masked, n + 1)
                    if n % 2 == 0 and n >= 4:
                        pe.wait_ge(oT_lo, n // 2 - 1)
                    r = slice(HD * (n % 2), HD * (n % 2) + HD)
                    for s in range(TT):
                        i = pe.matmul(psum[r, 6 + (n // 2) % 2, s * P:T], V[:, s, n * HD:(n + 1) * HD],
                                      E[:, n % 2, SEG[s]:SEG[s] + T - s * P], start=s == 0, stop=s == TT - 1,
                                      skip_group_check=True)
                    i.then_inc(av_done, 1)
                if 1 <= h <= NH:
                    n = h - 1
                    pe.wait_ge(spl_ready, n + 1)
                    for s in range(TT):
                        b, col = ((0, 0), (1, 0), (2, 0), (1, 384))[s]
                        for j in range(s, TT):
                            w = T - j * P
                            o = psum[:, 3 * (n % 2) + b, col + (j - s) * P:col + (j - s) * P + w]
                            for part in (sp_hi, sp_lo):
                                i = pe.matmul(o, (neg_tri if j == s else neg_ones)[:, :],
                                              part[:, n % 2, SEG[j]:SEG[j] + w], start=False,
                                              stop=j == TT - 1, skip_group_check=True)
                    i.then_inc(c_done, 1)
            pe.wait_ge(oT_lo, DT)
            project(S_O, 0, o_added)
            if STOP == "att":
                return
            norm(3, 4)
            pe.wait_ge(o_added, DT)
            for n in range(8):
                if n == 7:
                    pe.wait_ge(root_ready, 4)
                for k in range(4):
                    i = pe.transpose(psum[:, (0, 1, 2, 3, 5, 6, 7, 4)[n], k * P:(k + 1) * P],
                                     xT[:, 4 * (n % 2) + k, (n // 2) * P:(n // 2 + 1) * P], ident[:, :])
                i.then_inc(x2_turned, 1)
            pe.wait_ge(h_lo, 5 * DT)
            pe.wait_ge(wr_lo_ready, 1)
            pe.wait_ge(x2_kept, 8)
            for t in range(TT):
                for k in range(DT):
                    ts = slice(t * P, (t + 1) * P)
                    o = psum[:, 0, t * NE:(t + 1) * NE]
                    pe.matmul(o, hT_hi[:, k, ts], wr_hi[:, k, :], start=k == 0, stop=False)
                    pe.matmul(o, hT_hi[:, k, ts], wr_lo[:, k, :], start=False, stop=False)
                    i = pe.matmul(o, hT_lo[:, k, ts], wr_hi[:, k, :], start=False, stop=k == DT - 1)
            i.then_inc(logits_done, 1)
            for m in range(16):
                part, t, half = m // 8, (m // 2) % 4, m % 2
                if m >= 6:
                    pe.wait_ge(rows_kept, m - 5)
                for k in range(4):
                    i = pe.transpose(psum[:, (1, 2, 3, 5, 6, 7)[m % 6], k * P:(k + 1) * P],
                                     (hT_lo if part else hT_hi)[:, 4 * half + k, t * P:(t + 1) * P].bitcast(F32),
                                     ident[:, :])
                i.then_inc(h_turned, 1)
            pe.wait_ge(chosen_ready, 1)
            for t in range(TT):
                for u in range(t + 1):
                    pe.matmul(psum[:, 4, t * NE:(t + 1) * NE], (earlier if u == t else ones)[:, :],
                              chosen[:, u, :], start=u == 0, stop=u == t)
            for u in range(TT):
                i = pe.matmul(psum[:, 4, 64:64 + NE], ones[:, :], chosen[:, u, :], start=u == 0, stop=u == TT - 1)
            i.then_inc(ranks_done, 1)

            def select(t):
                pe.wait_ge(pick_ready, t + 1)
                for k in range(DT):
                    if k >= 4:
                        pe.wait_ge(sel_odd if k % 2 else sel_even, DT // 2 * t + (k - 4) // 2 + 1)
                    for part, rows in enumerate((rows_hi, rows_lo)):
                        for u in range(TT):
                            i = pe.matmul(psum[:, k % 4, part * NT:(part + 1) * NT], rows[:, u, k * P:(k + 1) * P],
                                          pick[:, u, 0:NT], start=u == 0, stop=u == TT - 1)
                    i.then_inc(sel_done, 1)

            pe.wait_ge(rows_kept, 16)
            pe.wait_ge(tables_ready, 1)
            select(0)

            def two(o, c, k, f, x, start_, stop_):
                wh, wl = w_tile(c, k, f)
                both = o.rearrange("p (a n) -> p a n", a=2)
                if stop_:
                    pe.matmul(o[:, 0:NT], wl, x[:, 0, :], start=False, stop=False, skip_group_check=True)
                    return pe.matmul(both, wh, x, start=False, stop=True, skip_group_check=True)
                pe.matmul(both, wh, x, start=start_, stop=False, skip_group_check=True)
                return pe.matmul(o[:, 0:NT], wl, x[:, 0, :], start=False, stop=False, skip_group_check=True)

            def turn(t, q):
                pe.wait_ge(yT_ready, 4 * t + q + 1)
                b = 4 + 2 * (q % 2)
                for part in range(2):
                    for dd in range(2):
                        o = (2 * part + dd) * P
                        i = pe.transpose(psum[:, b, o:o + P], yT[:, q % 2, dd, part * P:(part + 1) * P], ident[:, :])
                i.then_inc(y_turned, 1)

            def task(t):
                T11 = t * (SUBS_TASK // RING)
                pe.wait_ge(sel_even, DT // 2 * t + DT // 2)
                pe.wait_ge(sel_odd, DT // 2 * t + DT // 2)
                pe.wait_ge(y_kept, 4 * t + 2)
                for part in range(2):
                    for u in range(TT):
                        i = pe.matmul(psum[:, 5, 2 * part:2 * part + 2], pick[:, u, part * P:(part + 1) * P].bitcast(F32),
                                      row_gate[:, u, bass.ds(t, 1), :].rearrange("p a b -> p (a b)"),
                                      start=u == 0, stop=u == TT - 1)
                i.then_inc(info_done, 1)
                with pe.Fori(0, PAIRS // 2) as i_:
                    for p in range(2):
                        n = PAIRS * t + 2 * i_ + p
                        for u in range(2):
                            c = S_MOE + 2 * p + u
                            pe.wait_ge(lo_ready, c + 4 * (T11 + i_) + 1)
                            pe.wait_ge(u_summed if u else g_summed, n + 1)
                            for f in range(2):
                                for k in range(DT):
                                    i = two(psum[:, 2 * u + f, 0:2 * NT], c, k, f, x_sel[:, :, k, :], k == 0, k == DT - 1)
                                i.then_inc(w_used if f else half_done, 1)
                pe.wait_ge(info_ready, 3 * t + 1)
                for q in range(Q_OUT):
                    pe.wait_ge(y_kept, 4 * t + q + 1)
                    for j in range(4):
                        c = C2 + 4 * q + j
                        pe.wait_ge(lo_ready, c + 4 * T11 + 1)
                        if q == 0:
                            pe.wait_ge(mh_lo, PAIRS * t + 2 + (FS * (j + 1) + 1) // 2)
                        for dd in range(2):
                            for f in range(FS):
                                i = two(psum[:, 4 + 2 * (q % 2) + dd, 0:2 * NT], c, f, dd, hid[:, :, FS * j + f, :],
                                        j == 0 and f == 0, j == 3 and f == FS - 1)
                            i.then_inc(w_used if dd else half_done, 1)
                        if j == 0 and q:
                            turn(t, q - 1)
                pe.wait_ge(g_summed, PAIRS * t + PAIRS + 1)
                pe.wait_ge(u_summed, PAIRS * t + PAIRS + 1)
                select(t + 1)
                turn(t, Q_OUT - 1)

            task_loop(pe, task)


_OUTS = [((1, 512, 1024), "float32")]
_INS = ["x", "g_mix", "g_ffn", "pool_w", "pool_scale", "g_kv", "w_kv", "w_q", "w_o", "ffn_in", "ffn_out",
        "w_router", "moe_in", "moe_out", "g_final"]


def kernel(**inputs):
    import numpy as _np
    import concourse.bacc as _bacc
    from concourse import mybir as _mybir
    from concourse.bass_utils import run_bass_kernel_spmd as _run

    nc = _bacc.Bacc("TRN2", target_bir_lowering=False, num_devices=1)
    arrays, args = {}, []
    for name in _INS:
        a = _np.ascontiguousarray(inputs[name])
        arrays[f"in_{name}_dram"] = a
        args.append(nc.dram_tensor(f"in_{name}_dram", a.shape, _mybir.dt.from_np(a.dtype), kind="ExternalInput").ap())
    for i, (shape, dtype) in enumerate(_OUTS):
        dt = _mybir.dt.from_np(_np.dtype(dtype))
        args.append(nc.dram_tensor(f"out_{i}_dram", shape, dt, kind="ExternalOutput").ap())
    trunk(nc, *args)
    r = _run(nc, [arrays], core_ids=[0])
    return r.results[0]["out_0_dram"]
```

```python
from contextlib import ExitStack

import concourse.bass as bass
from concourse import mybir

F32 = mybir.dt.float32
F32R = mybir.dt.float32r
I32 = mybir.dt.int32
U32 = mybir.dt.uint32
ALU = mybir.AluOpType
ACT = mybir.ActivationFunctionType
AX_X = mybir.AxisListType.X

P = 128
STOP = "all"


def trunk(nc, x, g_mix, g_ffn, pool_w, pool_scale, g_kv, w_kv, w_q, w_o, ffn_in, ffn_out,
          w_router, moe_in, moe_out, g_final, out):
    _, T, D = x.shape
    DT, TT = D // P, T // P
    NG, GW = pool_w.shape[1], pool_w.shape[2]
    WINDOWS = (2, 4, 8, 16)
    FF = ffn_out.shape[1]
    NE, FE = moe_out.shape[1], moe_out.shape[2]
    HD = 64
    NH = D // HD
    EPS = 1e-6
    RING = 4
    SUB = 2048
    CW = SUB // DT
    AHEAD = 3
    F_TILES = FF // P
    F_HALF = (12, F_TILES - 12)
    S_POOL = 0
    S_FFN = 1
    S_IN = (S_FFN, S_FFN + F_HALF[0] + 8)
    S_OUT = (S_FFN + F_HALF[0], S_FFN + F_TILES + 8)
    S_K = S_FFN + F_TILES + 16
    S_V = S_K + 4
    S_Q = S_V + 4
    S_O = S_Q + 4
    S_MOE = S_O + 4
    NT = 144
    MAX_EXTRA = (2 * T - 1) // NT
    MAX_TASKS = NE + MAX_EXTRA
    FE_TILES = FE // P
    SUBS_IN = FE_TILES
    Q_OUT = D // 256
    SUBS_OUT = Q_OUT * 4
    FS = FE_TILES // 4
    SUBS_TASK = SUBS_IN + SUBS_OUT
    assert SUBS_TASK % RING == 0 and SUBS_IN % RING == 0

    with ExitStack() as ctx:
        base = 16512
        place = [base]

        def at(name, shape, dt, offset):
            return nc.alloc_sbuf_tensor_at(name, shape, dt, offset=offset)

        def take(nbytes):
            o = place[0]
            place[0] += nbytes
            return o

        o_raw, o_hi, o_lo = take(RING * SUB * 4), take(RING * SUB * 4), take(RING * SUB * 4)
        o_xT = take(DT * T * 4)
        o_hT = take(2 * DT * T * 4)
        o_big = take(12 * T * 4 * 2)
        o_tmp = take(5 * T * 4)
        o_const = place[0]

        raw = at("raw", [P, RING, SUB], F32, o_raw)
        w_hi = at("w_hi", [P, RING, SUB], F32R, o_hi)
        w_lo = at("w_lo", [P, RING, SUB], F32R, o_lo)
        xT = at("xT", [P, DT, T], F32, o_xT)
        hT_hi = at("hT_hi", [P, DT, T], F32R, o_hT)
        hT_lo = at("hT_lo", [P, DT, T], F32R, o_hT + DT * T * 4)
        tmp = at("tmp", [P, 5, T], F32, o_tmp)
        hid_hi = at("hid_hi", [P, 12, T], F32R, o_big)
        hid_lo = at("hid_lo", [P, 12, T], F32R, o_big + 12 * T * 4)
        x_in = at("x_in", [P, TT, D], F32, o_big)
        PAD = WINDOWS[-1]
        x_n = at("x_n", [P, TT, D], F32, o_big + TT * D * 4)
        band = at("band", [P, 2, NG, P + PAD], F32, o_big + 2 * TT * D * 4)
        head_cols = at("head_cols", [P, NG, PAD], F32, o_big + 2 * TT * D * 4 + 2 * NG * (P + PAD) * 4)
        KT = at("KT", [P, DT, T], F32, o_big)
        QT = at("QT", [P, DT, T], F32, o_big + 16384)
        V = at("V", [P, TT, D], F32, o_big + 32768)
        SEG = {0: 0, 1: 512, 3: 896, 2: 1024}
        HC = 1280
        E = at("E", [P, 2, HC], F32, o_tmp)
        sp_hi = at("sp_hi", [P, 2, HC], F32R, o_hi)
        sp_lo = at("sp_lo", [P, 2, HC], F32R, o_lo)
        A = at("A", [P, 2, HC], F32, o_hi + 2 * HC * 4)

        def const(name, shape, dt=F32):
            n = 4
            for s in shape[1:]:
                n *= s
            return at(name, shape, dt, take((n + 31) // 32 * 32))

        NV = 48 // 8 * 8
        gains_in = at("gains_in", [NV, P], F32, o_tmp)
        gains = const("gains", [P, NV])
        ident = const("ident", [P, P])
        ones = const("ones", [P, P])
        neg_ones = const("neg_ones", [P, P], F32R)
        ident_r = const("ident_r", [P, P], F32R)
        o_mask = place[0]
        not_causal = const("not_causal", [P, P], F32R)
        neg_tri = const("neg_tri", [P, P], F32R)
        eps = const("eps", [P, 1])
        inv_count = const("inv_count", [P, PAD])
        count = const("count", [P, PAD])
        x2_rows = at("x2_rows", [P, TT, D], F32, o_big)
        SLOTS = 2 * P
        o_pick = o_big + TT * D * 4
        pick = at("pick", [P, TT, SLOTS], F32, o_pick)
        pick_r = at("pick_r", [P, TT, NT], F32, o_pick + TT * SLOTS * 4)
        y_rows = at("y_rows", [P, 2, D], F32, o_pick + 2 * TT * SLOTS * 4)
        g_row = at("g_row", [P, D], F32, o_pick + 2 * TT * SLOTS * 4 + 2 * D * 4)
        x_sel = at("x_sel", [P, 2, DT, NT], F32R, o_xT)
        hid = at("hid", [P, 2, FE_TILES, NT], F32R, o_xT + 2 * DT * NT * 4)
        o_yT = o_xT + 2 * (DT + FE_TILES) * NT * 4
        yT = at("yT", [P, 2, 2, SLOTS], F32, o_yT)
        assert o_yT + 4 * SLOTS * 4 <= o_big
        gate_s = at("gate_s", [P, 2, 2, NT], F32, o_tmp)
        up_s = at("up_s", [P, 2, 2, NT], F32, o_tmp + 4 * NT * 4)
        y_s = at("y_s", [P, 2, 2, NT], F32, o_tmp + 8 * NT * 4)
        TC = MAX_TASKS + 1
        o_t = [o_tmp]

        def table(name, shape, dt=F32):
            n = 4
            for k in shape[1:]:
                n *= k
            a = at(name, shape, dt, o_t[0])
            o_t[0] += (n + 31) // 32 * 32
            return a

        logits, top_v = table("logits", [P, TT, NE]), table("top_v", [P, TT, NE])
        top_i, top_f = table("top_i", [P, TT, NE], U32), table("top_f", [P, TT, NE])
        first, second = table("first", [P, TT, NE]), table("second", [P, TT, NE])
        chosen, gate_e = table("chosen", [P, TT, NE]), table("gate_e", [P, TT, NE])
        rank, row_e = table("rank", [P, TT, NE]), table("row_e", [P, TT, NE])
        gates = table("gates", [P, 4, TT])
        cnt = table("cnt", [P, NE])
        extra = table("extra", [P, 3, NE])
        cum = table("cum", [P, 4, NE + 4])
        before = table("before", [P, NE])
        n_f = table("n_f", [P, 1])
        is_mine = table("is_mine", [P, TC, NE])
        is_past = table("is_past", [P, 2, TC - NE, NE])
        start = table("start", [P, TC, NE])
        e_f = table("e_f", [P, TC])
        wide = table("wide", [P, TT, TC, NE])
        assert o_t[0] <= o_const
        pos = const("pos", [P, TT, TC])
        row_gate = const("row_gate", [P, TT, TC, 2])
        task_e = const("task_e", [P, TC], I32)
        n_tasks_i = const("n_tasks_i", [P, 1], I32)
        slot_iota = const("slot_iota", [P, NT])
        e_iota = const("e_iota", [P, NE])
        row0 = const("row0", [P, TT])
        spare_row = const("spare_row", [P, 2])
        earlier = at("earlier", [P, P], F32, o_mask)
        wr = const("wr", [P, DT, NE])
        wr_g = const("wr_g", [P, DT, NE])
        rstd_tok = const("rstd_tok", [P, TT])
        info = const("info", [P, 2, 2])
        info_t = const("info_t", [P, 2])
        info_row = const("info_row", [P, 2], I32)
        ss = const("ss", [P, TT])
        primed = const("primed", [P, 7])
        wait_holder = const("wait_holder", [P, 1])
        x2_dram = nc.dram_tensor("x2_dram", (T, D), F32, kind="Internal").ap()
        y2_dram = nc.dram_tensor("y2_dram", (2 * T + SLOTS, D), F32, kind="Internal").ap()
        y2_in = at("y2_in", [P, TT, 2, D], F32, o_xT)
        x2_in = at("x2_in", [P, TT, D], F32, o_xT + TT * 2 * D * 4)
        psum = ctx.enter_context(nc.psum_tensor("psum", [P, 8, T], F32))
        assert place[0] <= nc.sbuf_usable_end, place[0]

        def sem(name):
            return ctx.enter_context(nc.semaphore(name))

        raw_landed = [sem(f"raw_landed{s}") for s in range(RING)]
        hi_ready, lo_ready = sem("hi_ready"), sem("lo_ready")
        half_done, w_used = sem("half_done"), sem("w_used")
        consts, const_steps, gains_landed, gains_T, gains_ready = (
            sem("consts"), sem("const_steps"), sem("gains_landed"), sem("gains_T"), sem("gains_ready"))
        x_landed = [sem(f"x_landed{t}") for t in range(TT)]
        x_turned, x_act, x_dve = sem("x_turned"), sem("x_act"), sem("x_dve")
        inv_ready, band_step, bands_ready = sem("inv_ready"), sem("band_step"), sem("bands_ready")
        in_squared, in_root, in_rstd, x_n_act, x_n_dve, pooled = (
            sem("in_squared"), sem("in_root"), sem("in_rstd"), sem("x_n_act"), sem("x_n_dve"), sem("pooled"))
        acc_step = sem("acc_step")
        sq_ready, sq_summed, root_ready, rstd_ready, hf_ready, h_hi, h_lo = (
            sem("sq_ready"), sem("sq_summed"), sem("root_ready"), sem("rstd_ready"),
            sem("hf_ready"), sem("h_hi"), sem("h_lo"))
        hp_step = sem("hp_step")
        pool_added = sem("pool_added")
        sil_ready, hm_ready, hid_hi_ready, hid_lo_ready = (
            sem("sil_ready"), sem("hm_ready"), sem("hid_hi_ready"), sem("hid_lo_ready"))
        fo_added, proj_kept, o_added = sem("fo_added"), sem("proj_kept"), sem("o_added")
        z_done, abs_ready, exp_ready, ln_ready, sp_ready, sph_ready, spl_ready = (
            sem("z_done"), sem("abs_ready"), sem("exp_ready"), sem("ln_ready"), sem("sp_ready"),
            sem("sph_ready"), sem("spl_ready"))
        c_done, a_ready, av_done, oT_hi, oT_lo = (
            sem("c_done"), sem("a_ready"), sem("av_done"), sem("oT_hi"), sem("oT_lo"))
        stored = sem("stored")
        small_landed, wr_g_ready = sem("small_landed"), sem("wr_g_ready")
        x2_turned, x2_kept, logits_done = sem("x2_turned"), sem("x2_kept"), sem("logits_done")
        gap_ready, gap_exp, chosen_ready, ranks_done, tables_ready = (
            sem("gap_ready"), sem("gap_exp"), sem("chosen_ready"), sem("ranks_done"), sem("tables_ready"))
        g_row_landed, cleared = sem("g_row_landed"), sem("cleared")
        pick_ready, sel_done, sel_hi, sel_lo, info_done, info_ready = (
            sem("pick_ready"), sem("sel_done"), sem("sel_hi"), sem("sel_lo"), sem("info_done"),
            sem("info_ready"))
        g_half, g_summed, g_silu, u_half, u_summed, m_ready, mh_hi, mh_lo = (
            sem("g_half"), sem("g_summed"), sem("g_silu"), sem("u_half"), sem("u_summed"),
            sem("m_ready"), sem("mh_hi"), sem("mh_lo"))
        y_half, yT_ready, y_turned, y_kept, rows_stored = (
            sem("y_half"), sem("yT_ready"), sem("y_turned"), sem("y_kept"), sem("rows_stored"))
        y2_landed, sum_step, ss_ready, root_end, out_ready = (
            [sem(f"y2_landed{k}") for k in range(TT)], sem("sum_step"), sem("ss_ready"), sem("root_end"), sem("out_ready"))

        G_MIX, G_FFN, G_SCALE, G_KV = 0, 16, 32, 40

        def load(sp, c, dst, src, I=0):
            if not (isinstance(I, int) and c + 4 * I < RING):
                sp.wait_ge(lo_ready, c + 4 * I - RING + 1)
            sp.dma_start(dst, src).then_inc(raw_landed[c % RING], 16)

        def split_hi(act, c, I=0):
            act.wait_ge(raw_landed[c % RING], 16 * (c // RING + I + 1))
            if not (isinstance(I, int) and c + 4 * I < RING):
                act.wait_ge(w_used, c + 4 * I - RING + 1)
            act.activation(w_hi[:, c % RING, :], raw[:, c % RING, :], ACT.Copy).then_inc(hi_ready, 1)

        def split_lo(dve, c, I=0):
            dve.wait_ge(hi_ready, c + 4 * I + 1)
            dve.tensor_tensor(w_lo[:, c % RING, :], raw[:, c % RING, :],
                              w_hi[:, c % RING, :].bitcast(F32), ALU.subtract).then_inc(lo_ready, 1)

        def product(pe, o, whi, wlo, hi, lo, start, stop):
            pe.matmul(o, whi, hi, start=start, stop=False)
            pe.matmul(o, whi, lo, start=False, stop=False)
            return pe.matmul(o, wlo, hi, start=False, stop=stop)

        def w_tile(c, k, f, n=CW):
            s = slice(k * n + f * P, k * n + f * P + P)
            return w_hi[:, c % RING, s], w_lo[:, c % RING, s]

        def in_columns(w, c0, n=CW):
            return w.rearrange("(k p) n -> p k n", p=P)[:, :, c0:c0 + n]

        def sub3(c, k, n):
            return raw[:, c % RING, 0:k * n].rearrange("p (k n) -> p k n", k=k)

        def column_done(eng, c, f, I=0):
            eng.wait_ge(w_used if f else half_done, c + 4 * I + 1)

        PAIRS = FE_TILES // 2
        C2 = S_MOE + SUBS_IN

        def task_loop(eng, body):
            eng.wait_ge(tables_ready, 1)
            n_tasks = eng.value_load(n_tasks_i[0:1, 0:1], min_val=NE, max_val=MAX_TASKS)
            with eng.Fori(0, MAX_TASKS) as t:
                with eng.If(t < n_tasks):
                    body(t)
            return n_tasks

        def head_z(h):
            return psum[:, 3 * (h % 2):3 * (h % 2) + 3, :].rearrange("p b t -> p (b t)")[:, 0:HC]

        block = ctx.enter_context(nc.Block())

        @block.sync
        def _(sp):
            for t in range(TT):
                sp.dma_start(x_in[:, t, :], x[0, t * P:(t + 1) * P, :]).then_inc(x_landed[t], 16)
            c = S_POOL
            load(sp, c, sub3(c, DT, GW), in_columns(pool_w[0].rearrange("g c n -> (g c) n"), 0))
            w_in = ffn_in[0]
            w_out = ffn_out[0].rearrange("(f p) n -> p f n", p=P)
            f0 = 0
            for half in range(2):
                nf = F_HALF[half]
                for p in range(nf // 2):
                    for u in range(2):
                        c = S_IN[half] + 2 * p + u
                        load(sp, c, sub3(c, DT, CW), in_columns(w_in, u * FF + (f0 + 2 * p) * P))
                for q in range(4):
                    for s in range(2):
                        c = S_OUT[half] + 2 * q + s
                        load(sp, c, sub3(c, nf // 2, CW),
                             w_out[:, f0 + s * (nf // 2):f0 + (s + 1) * (nf // 2), q * CW:(q + 1) * CW])
                f0 += nf
            if STOP == "ffn":
                for j in range(3):
                    load(sp, S_K + j, sub3(S_K + j, DT, CW), in_columns(w_kv, j * CW))
                sp.wait_ge(fo_added, 16)
                sp.dma_start(out.rearrange("b s d -> (b s d)").rearrange("(k p t) -> p k t", p=P, k=DT), xT[:, :, :]).then_inc(stored, 16)
                sp.wait_ge(stored, 16)
                return
            for w, s0, c0 in ((w_kv, S_K, 0), (w_kv, S_V, D), (w_q[0], S_Q, 0), (w_o[0], S_O, 0)):
                for j in range(4):
                    load(sp, s0 + j, sub3(s0 + j, DT, CW), in_columns(w, c0 + j * CW))
            if STOP == "att":
                sp.wait_ge(o_added, 8)
                sp.dma_start(out.rearrange("b s d -> (b s d)").rearrange("(k p t) -> p k t", p=P, k=DT), xT[:, :, :]).then_inc(stored, 16)
                sp.wait_ge(stored, 16)
                return

            def task_loads(t, e):
                w1 = moe_in[0][bass.ds(e, 1)].rearrange("a (k p) n -> p (a k) n", p=P)
                w2 = moe_out[0][bass.ds(e, 1)].rearrange("a (f p) n -> p (a f) n", p=P)
                T11 = t * (SUBS_TASK // RING)
                with sp.Fori(0, PAIRS // 2) as i:
                    for j in range(4):
                        c = S_MOE + j
                        load(sp, c, sub3(c, DT, CW),
                             w1[:, :, bass.ds(4 * P * i + ((j % 2) * FE + (j // 2) * CW), CW)], T11 + i)
                with sp.Fori(0, Q_OUT) as q:
                    for j in range(4):
                        load(sp, C2 + j, sub3(C2 + j, FS, CW),
                             w2[:, j * FS:(j + 1) * FS, bass.ds(CW * q, CW)], T11 + q)

            with sp.Fori(0, NE) as t:
                task_loads(t, t)
            sp.wait_ge(tables_ready, 1)
            n_tasks = sp.value_load(n_tasks_i[0:1, 0:1], min_val=NE, max_val=MAX_TASKS)
            with sp.Fori(NE, MAX_TASKS) as t:
                with sp.If(t < n_tasks):
                    task_loads(t, sp.value_load(task_e[0:1, bass.ds(t, 1)], min_val=0, max_val=NE - 1))
            for j in range(AHEAD):
                load(sp, S_MOE + j, raw[:, (S_MOE + j) % RING, 0:8], ffn_in[0, 0:P, 0:8], n_tasks * (SUBS_TASK // RING))
            sp.wait_ge(rows_stored, 32 * n_tasks + 32)
            sp.wait_ge(sel_lo, DT * n_tasks + DT)
            for k in range(TT):
                sp.dma_start(y2_in[:, k, :, :], y2_dram[2 * k * P:2 * (k + 1) * P, :]
                             .rearrange("(p two) d -> p two d", two=2)).then_inc(y2_landed[k], 16)
                sp.dma_start(x2_in[:, k, :], x2_dram[k * P:(k + 1) * P, :]).then_inc(y2_landed[k], 16)
            for k in range(TT):
                sp.wait_ge(out_ready, k + 1)
                sp.dma_start(out[0, k * P:(k + 1) * P, :], x2_in[:, k, :]).then_inc(stored, 16)
            sp.wait_ge(stored, 16 * TT)

        @block.gpsimd
        def _(pool):
            pool.memset(eps[:, :], EPS).then_inc(consts, 1)
            pool.memset(ones[:, :], 1.0).then_inc(consts, 1)
            pool.memset(ident[:, :], 0.0).then_inc(const_steps, 1)
            pool.memset(neg_ones[:, :].bitcast(F32), -1.0).then_inc(const_steps, 1)
            pool.iota(count[:, :], pattern=[[1, PAD]], base=1, channel_multiplier=0,
                      allow_small_or_imprecise_dtypes=True).then_inc(const_steps, 1)
            pool.wait_ge(const_steps, 3)
            pool.affine_select(out=ident[:, :], in_=ident[:, :], compare_op=ALU.not_equal, fill=1.0,
                               base=0, pattern=[[-1, P]], channel_multiplier=1).then_inc(consts, 1)
            pool.affine_select(out=neg_tri[:, :], in_=neg_ones[:, :].bitcast(F32), compare_op=ALU.is_ge,
                               fill=0.0, base=0, pattern=[[-1, P]], channel_multiplier=1).then_inc(consts, 1)
            for g in range(NG):
                pool.memset(band[:, 1, g, :], 1.0 / WINDOWS[g]).then_inc(band_step, 1)
            pool.wait_ge(band_step, NG)
            pool.affine_select(out=band[:, 1, :, :], in_=band[:, 1, :, :], compare_op=ALU.is_ge, fill=0.0, base=0,
                               pattern=[[0, NG], [1, P + PAD]], channel_multiplier=-1).then_inc(band_step, 1)
            pool.wait_ge(band_step, NG + 1)
            for g in range(NG):
                pool.affine_select(out=band[:, 1, g, :], in_=band[:, 1, g, :], compare_op=ALU.is_ge, fill=0.0,
                                   base=WINDOWS[g] - 1, pattern=[[-1, P + PAD]],
                                   channel_multiplier=1).then_inc(band_step, 1)
            pool.wait_ge(inv_ready, 1)
            for g in range(NG):
                w = WINDOWS[g]
                pool.affine_select(out=head_cols[:, g, 0:w], in_=inv_count[:, 0:w], compare_op=ALU.is_ge, fill=0.0,
                                   base=0, pattern=[[1, w]], channel_multiplier=-1).then_inc(band_step, 1)
            pool.memset(not_causal[:, :].bitcast(F32), -(2.0 ** 60)).then_inc(const_steps, 1)
            pool.wait_ge(consts, 4)
            pool.tensor_copy(ident_r[:, :], ident[:, :]).then_inc(consts, 1)
            pool.wait_ge(const_steps, 4)
            pool.affine_select(out=not_causal[:, :], in_=not_causal[:, :].bitcast(F32), compare_op=ALU.is_ge,
                               fill=0.0, base=0, pattern=[[-1, P]], channel_multiplier=1).then_inc(consts, 1)
            if STOP == "ffn":
                return
            f = dict(allow_small_or_imprecise_dtypes=True)
            pool.iota(slot_iota[:, :], pattern=[[1, NT]], base=0, channel_multiplier=0, **f).then_inc(cleared, 1)
            pool.iota(e_iota[:, :], pattern=[[1, NE]], base=0, channel_multiplier=0, **f).then_inc(cleared, 1)
            pool.iota(row0[:, :], pattern=[[2 * P, TT]], base=1, channel_multiplier=2, **f).then_inc(cleared, 1)
            pool.iota(spare_row[:, :], pattern=[[P, 2]], base=2 * T + 1, channel_multiplier=1,
                      **f).then_inc(cleared, 1)

            if STOP == "att":
                return
            pool.wait_ge(c_done, NH)
            pool.affine_select(out=earlier[:, :], in_=ones[:, :], compare_op=ALU.is_gt, fill=0.0, base=0,
                               pattern=[[1, P]], channel_multiplier=-1).then_inc(cleared, 1)
            pool.wait_ge(av_done, NH)
            pool.memset(pick[:, :, NT:], 0.0).then_inc(cleared, 1)
            pool.wait_ge(o_added, DT)
            pool.memset(yT[:, :, :, NT:], 0.0).then_inc(cleared, 1)
            pool.wait_ge(x2_kept, DT)
            for h in range(2):
                pool.dma_start(x2_dram[h * 256:(h + 1) * 256, :].rearrange("(t p) d -> p t d", p=P),
                               x2_rows[:, 2 * h:2 * h + 2, :]).then_inc(rows_stored, 16)

            def task(t):
                with pool.Fori(0, PAIRS // 2) as i:
                    for p in range(2):
                        n = PAIRS * t + 2 * i + p
                        place_ = bass.ds(4 * i + 2 * p, 2)
                        pool.wait_ge(m_ready, n + 3)
                        pool.tensor_copy(hid[:, 0, place_, :], up_s[:, p, :, :]).then_inc(mh_hi, 1)
                        pool.wait_ge(mh_hi, n + 1)
                        pool.tensor_tensor(hid[:, 1, place_, :], up_s[:, p, :, :],
                                           hid[:, 0, place_, :].bitcast(F32), ALU.subtract).then_inc(mh_lo, 1)
                pool.wait_ge(y_kept, 4 * t + 6)
                pool.tensor_tensor(wait_holder[:, :], eps[:, :], eps[:, :], ALU.add)
                for b, n in enumerate((P, NT - P)):
                    pool.indirect_dma_start(
                        out=y2_dram[:, :],
                        out_offset=bass.IndirectOffsetOnAxis(ap=info_row[0:n, b:b + 1].bitcast(U32), axis=0),
                        in_=y_rows[0:n, b, :], in_offset=None).then_inc(rows_stored, 16)

            for k in range(2):
                pool.memset(ss[:, k:k + 1], 0.0).then_inc(mh_lo, 1)
            task_loop(pool, task)

        @block.scalar
        def _(act):
            rows = lambda v: v.rearrange("l (t p) -> (l t) p", p=P)
            act.dma_start(gains_in[G_MIX:G_MIX + 16, :], rows(g_mix)).then_inc(gains_landed, 16)
            act.dma_start(gains_in[G_FFN:G_FFN + 16, :], rows(g_ffn)).then_inc(gains_landed, 16)
            act.dma_start(gains_in[G_SCALE:G_SCALE + 8, :], rows(pool_scale)).then_inc(gains_landed, 16)
            act.dma_start(gains_in[G_KV:G_KV + 8, :], g_kv.rearrange("(t p) -> t p", p=P)).then_inc(gains_landed, 16)
            act.dma_start(wr[:, :, :], w_router[0].rearrange("(k p) e -> p k e", p=P)).then_inc(small_landed, 16)

            def square(n, d):
                if d >= 2:
                    act.wait_ge(acc_step, 6 * (n - 1) + max(1, d - 2))
                elif n > 1:
                    act.wait_ge(sq_summed, n - 1)
                act.activation(tmp[:, d % 2, :], xT[:, d, :], ACT.Square).then_inc(sq_ready, 1)

            def root(n):
                act.wait_ge(sq_summed, n)
                act.activation(tmp[:, 2, :], psum[:, 0, :], ACT.Sqrt, bias=eps[:, :],
                               scale=1.0 / D).then_inc(root_ready, 1)

            def h_round(n):
                for d in range(DT):
                    act.wait_ge(hf_ready, DT * (n - 1) + d + 1)
                    act.activation(hT_hi[:, d, :], tmp[:, 3 + d % 2, :], ACT.Copy).then_inc(h_hi, 1)

            for t in range(TT):
                act.wait_ge(x_landed[t], 16)
                act.activation(x_n[:, t, :], x_in[:, t, :], ACT.Square, accum_out=ss[:, t:t + 1]).then_inc(in_squared, 1)
            act.wait_ge(in_squared, TT)
            act.wait_ge(consts, 4)
            act.activation(ss[:, :], ss[:, :], ACT.Sqrt, bias=eps[:, :], scale=1.0 / D).then_inc(in_root, 1)
            act.wait_ge(in_rstd, 1)
            for t in range(0, TT, 2):
                act.activation(x_n[:, t, :], x_in[:, t, :], ACT.Copy, scale=ss[:, t:t + 1]).then_inc(x_n_act, 1)
            for d in range(0, DT, 2):
                act.wait_ge(x_turned, d + 1)
                act.activation(xT[:, d, :], psum[:, d, :], ACT.Copy).then_inc(x_act, 1)
            split_hi(act, S_POOL)
            act.wait_ge(gains_ready, 1)
            for d in range(DT):
                act.wait_ge(pooled, d + 1)
                act.activation(hT_hi[:, d, :], psum[:, d, :], ACT.Copy,
                               scale=gains[:, G_MIX + d:G_MIX + d + 1]).then_inc(h_hi, 1)
            act.wait_ge(x_dve, DT // 2)
            act.wait_ge(x_act, DT // 2)
            for c in range(1, AHEAD):
                split_hi(act, c)

            def hidden(c, F, I):
                column_done(act, c, F % 2, I)
                if F >= 2 or not isinstance(I, int):
                    act.wait_ge(hm_ready, F + 4 * I - 1)
                act.activation(tmp[:, F % 2, :], psum[:, F % 2, :], ACT.Silu).then_inc(sil_ready, 1)

            def hidden_round(F, I, place_):
                act.wait_ge(hm_ready, F + 4 * I + 1)
                act.activation(place_, tmp[:, 3 + F % 2, :], ACT.Copy).then_inc(hid_hi_ready, 1)

            split_hi(act, S_FFN + 2)
            for d in range(DT):
                act.wait_ge(pool_added, d + 1)
                square(1, d)
            root(1)
            h_round(1)
            f0 = 0
            for half in range(2):
                nf = F_HALF[half]
                if half == 1:
                    column_done(act, S_OUT[0] + 7, 1)

                def pair(p, I):
                    c = S_IN[half] + 2 * p + AHEAD
                    split_hi(act, c, I)
                    for f in range(2):
                        hidden(c - AHEAD, f0 + 2 * p + f, I)
                    split_hi(act, c + 1, I)
                    for f in range(2):
                        hidden_round(f0 + 2 * p + f, I, hid_hi[:, bass.ds(2 * p + f + 4 * I, 1), :]
                                     .rearrange("p a t -> p (a t)"))
                pair(0, 0)
                pair(1, 0)
                with act.Fori(1, nf // 4) as i:
                    pair(0, i)
                    pair(1, i)
                if nf % 4:
                    pair(nf // 2 - 1, 0)
                for j in range(8):
                    split_hi(act, S_OUT[half] + j + AHEAD)
                    if half == 1 and j % 2 and j >= 3:
                        for d in (j - 3, j - 2):
                            act.wait_ge(fo_added, DT + d + 1)
                            square(2, d)
                f0 += nf
            if STOP == "ffn":
                return
            for d in range(DT - 2, DT):
                act.wait_ge(fo_added, DT + d + 1)
                square(2, d)
            root(2)
            h_round(2)
            for j in range(4):
                split_hi(act, S_K + j + AHEAD)
                for f in range(2):
                    n = 2 * j + f
                    column_done(act, S_K + j, f)
                    act.activation(KT[:, n, :], psum[:, n % 4, :], ACT.Copy).then_inc(proj_kept, 1)
            for j in range(4):
                split_hi(act, S_V + j + AHEAD)
                for t in range(TT):
                    column_done(act, S_V + j, 1)
                    act.activation(V[:, t, j * CW:(j + 1) * CW], psum[:, 4 * (j % 2) + t, 0:CW],
                                   ACT.Copy).then_inc(proj_kept, 1)
            h_round(3)
            for j in range(4):
                if j + AHEAD < 4:
                    split_hi(act, S_Q + j + AHEAD)
                for f in range(2):
                    n = 3 * DT + 2 * j + f
                    column_done(act, S_Q + j, f)
                    act.activation(QT[:, 2 * j + f, :], psum[:, n % 4, :], ACT.Copy,
                                   scale=HD ** -0.5).then_inc(proj_kept, 1)
            act.preload_act_table_set("natural_log_exp_and_others")

            def softplus_part(h, I):
                n, first_uses = h + 4 * I, isinstance(I, int) and h < 2
                act.wait_ge(z_done, n + 1)
                if not first_uses:
                    act.wait_ge(spl_ready, n - 1)
                e = E[:, h % 2, :]
                act.activation(e, head_z(h), ACT.Abs).then_inc(abs_ready, 1)
                act.wait_ge(abs_ready, n + 1)
                act.activation(e, e, ACT.Exp, scale=-1.0).then_inc(exp_ready, 1)
                act.wait_ge(exp_ready, n + 1)
                act.activation(e, e, ACT.Ln, bias=1.0).then_inc(ln_ready, 1)

            def weights(h, I):
                n, first_uses = h + 4 * I, isinstance(I, int) and h < 2
                act.wait_ge(c_done, n + 1)
                if not first_uses:
                    act.wait_ge(av_done, n - 1)
                act.activation(A[:, h % 2, :], head_z(h), ACT.Exp).then_inc(a_ready, 1)

            def o_round(p, I):
                act.wait_ge(av_done, 2 * p + 4 * I + 2)
                act.activation(hT_hi[:, bass.ds(p + 2 * I, 1), :].rearrange("p a t -> p (a t)"), psum[:, 6 + p, :],
                               ACT.Copy).then_inc(oT_hi, 1)

            softplus_part(0, 0)
            for h in range(1, 4):
                softplus_part(h, 0)
                weights(h - 1, 0)
            with act.Fori(1, NH // 4) as i:
                softplus_part(0, i)
                weights(3, i - 1)
                o_round(0, i - 1)
                softplus_part(1, i)
                weights(0, i)
                softplus_part(2, i)
                weights(1, i)
                o_round(1, i - 1)
                softplus_part(3, i)
                weights(2, i)
            weights(3, NH // 4 - 1)
            for p in range(2):
                o_round(p, NH // 4 - 1)
            for j in range(3):
                split_hi(act, S_O + j)
            split_hi(act, S_O + 3)
            if STOP == "att":
                return
            act.wait_ge(av_done, NH)
            act.dma_start(g_row[:, :], g_final.partition_broadcast(P)).then_inc(g_row_landed, 16)

            def keep_x2(d):
                act.wait_ge(x2_turned, d + 1)
                act.activation(x2_rows[:, :, d * P:(d + 1) * P], psum[:, 6 + d % 2, :].rearrange("p (t f) -> p t f", t=TT),
                               ACT.Copy).then_inc(x2_kept, 1)

            for d in range(DT):
                act.wait_ge(o_added, d + 1)
                act.wait_ge(sq_summed, 2 + max(d - 1, 0))
                act.activation(tmp[:, d % 2, :], xT[:, d, :], ACT.Square).then_inc(sq_ready, 1)
                if d:
                    keep_x2(d - 1)
                if d % 2 and d >= 3:
                    split_hi(act, S_MOE + (d - 3) // 2)
            act.wait_ge(sq_summed, 2 + DT)
            act.activation(rstd_tok[:, :], psum[:, 4, 0:TT], ACT.Sqrt, bias=eps[:, :],
                           scale=1.0 / D).then_inc(root_ready, 1)
            keep_x2(DT - 1)
            act.wait_ge(gap_ready, 1)
            act.activation(gates[:, 1, :], gates[:, 0, :], ACT.Exp).then_inc(gap_exp, 1)
            act.preload_act_table_set("silu_and_others")

            def select(t):
                for k in range(DT):
                    act.wait_ge(sel_done, DT * t + k + 1)
                    act.activation(x_sel[:, 0, k, :], psum[:, k % 4, 0:NT], ACT.Copy,
                                   scale=gains[:, G_FFN + DT + k:G_FFN + DT + k + 1]).then_inc(sel_hi, 1)

            select(0)

            def task(t):
                T11 = t * (SUBS_TASK // RING)
                with act.Fori(0, PAIRS // 2) as i:
                    for p in range(2):
                        n = PAIRS * t + 2 * i + p
                        c = S_MOE + 2 * p
                        split_hi(act, c + AHEAD, T11 + i)
                        column_done(act, c, 1, T11 + i)
                        act.wait_ge(m_ready, n + 1)
                        act.activation(gate_s[:, p, :, :], psum[:, 0:2, NT:2 * NT], ACT.Copy).then_inc(g_half, 1)
                        split_hi(act, c + 1 + AHEAD, T11 + i)
                        act.wait_ge(g_summed, n + 2)
                        act.activation(gate_s[:, p, :, :], gate_s[:, p, :, :], ACT.Silu).then_inc(g_silu, 1)
                        column_done(act, c + 1, 1, T11 + i)
                        act.wait_ge(mh_lo, n + 1)
                        act.activation(up_s[:, p, :, :], psum[:, 2:4, NT:2 * NT], ACT.Copy).then_inc(u_half, 1)
                for q in range(Q_OUT):
                    for j in range(4):
                        split_hi(act, C2 + 4 * q + j + AHEAD, T11)
                    column_done(act, C2 + 4 * q + 3, 1, T11)
                    b = 4 + 2 * (q % 2)
                    if q >= 2:
                        act.wait_ge(yT_ready, 4 * t + q - 1)
                    act.activation(y_s[:, q % 2, :, :], psum[:, b:b + 2, NT:2 * NT], ACT.Copy).then_inc(y_half, 1)
                select(t + 1)

            task_loop(act, task)
            for k in range(TT):
                act.wait_ge(sum_step, 2 * k + 2)
                act.activation(y2_in[:, k, 0, :], x2_in[:, k, :], ACT.Square,
                               accum_out=ss[:, k:k + 1]).then_inc(ss_ready, 1)
            act.wait_ge(ss_ready, TT)
            act.activation(ss[:, :], ss[:, :], ACT.Sqrt, bias=eps[:, :], scale=1.0 / D).then_inc(root_end, 1)

        @block.vector
        def _(dve):
            steps = [0]

            def chained(i):
                steps[0] += 1
                i.then_inc(hp_step, 1)
                dve.wait_ge(hp_step, steps[0])

            dve.wait_ge(const_steps, 3)
            dve.reciprocal(inv_count[:, :], count[:, :]).then_inc(inv_ready, 1)
            dve.wait_ge(consts, 4)
            dve.wait_ge(band_step, 2 * NG + 1)
            chained(dve.tensor_tensor(band[:, 1, :, 0:P], band[:, 1, :, 0:P],
                                      ident[:, :].unsqueeze(1).to_broadcast([P, NG, P]), ALU.subtract))
            chained(dve.tensor_copy(band[:, 0, :, :], band[:, 1, :, :]))
            dve.wait_ge(band_step, 3 * NG + 1)
            for g in range(NG):
                w = WINDOWS[g]
                dve.tensor_tensor(band[:, 0, g, 0:w], head_cols[:, g, 0:w], ident[:, 0:w],
                                  ALU.subtract).then_inc(bands_ready, 1)
            dve.wait_ge(in_root, 1)
            dve.reciprocal(ss[:, :], ss[:, :]).then_inc(in_rstd, 1)
            dve.wait_ge(in_rstd, 1)
            for t in range(1, TT, 2):
                dve.tensor_scalar(x_n[:, t, :], x_in[:, t, :], ss[:, t:t + 1], None, ALU.mult).then_inc(x_n_dve, 1)
            for d in range(1, DT, 2):
                dve.wait_ge(x_turned, d + 1)
                dve.tensor_copy(xT[:, d, :], psum[:, d, :]).then_inc(x_dve, 1)
            dve.wait_ge(gains_T, 1)
            dve.tensor_copy(gains[:, :], psum[:, 0, 0:NV]).then_inc(gains_ready, 1)
            split_lo(dve, S_POOL)
            dve.wait_ge(gains_ready, 1)
            for d in range(DT):
                dve.wait_ge(h_hi, d + 1)
                dve.scalar_tensor_tensor(hT_lo[:, d, :], psum[:, d, :], gains[:, G_MIX + d:G_MIX + d + 1],
                                         hT_hi[:, d, :].bitcast(F32), ALU.mult, ALU.subtract).then_inc(h_lo, 1)
            dve.wait_ge(x_act, DT // 2)
            dve.wait_ge(x_dve, DT // 2)

            def add_squares(n, d):
                dve.wait_ge(sq_ready, DT * (n - 1) + d + 1)
                if d == 1:
                    i = dve.tensor_tensor(tmp[:, 2, :], tmp[:, 0, :], tmp[:, 1, :], ALU.add)
                else:
                    dve.wait_ge(acc_step, 6 * (n - 1) + d - 1)
                    i = dve.tensor_tensor(tmp[:, 2, :], tmp[:, 2, :], tmp[:, d % 2, :], ALU.add)
                i.then_inc(acc_step, 1)

            def rstd(n):
                dve.wait_ge(root_ready, n)
                dve.reciprocal(tmp[:, 2, :], tmp[:, 2, :]).then_inc(rstd_ready, 1)
                dve.wait_ge(rstd_ready, n)

            def normed(o, d, g):
                return dve.scalar_tensor_tensor(o, xT[:, d, :], gains[:, g + d:g + d + 1],
                                                tmp[:, 2, :], ALU.mult, ALU.mult)

            def h_minus(n, d):
                dve.wait_ge(h_hi, DT * n + d + 1)
                dve.tensor_tensor(hT_lo[:, d, :], tmp[:, 3 + d % 2, :], hT_hi[:, d, :].bitcast(F32),
                                  ALU.subtract).then_inc(h_lo, 1)

            def norm_tiles(n, g):
                for d in range(DT):
                    if d >= 2:
                        dve.wait_ge(h_lo, DT * n + d - 1)
                    normed(tmp[:, 3 + d % 2, :], d, g).then_inc(hf_ready, 1)
                    if d:
                        h_minus(n, d - 1)
                h_minus(n, DT - 1)

            for c in range(1, AHEAD):
                split_lo(dve, c)
            split_lo(dve, S_FFN + 2)
            for d in range(DT):
                column_done(dve, S_POOL, d // 4)
                dve.scalar_tensor_tensor(xT[:, d, :], psum[:, d, :], gains[:, G_SCALE + d:G_SCALE + d + 1],
                                         xT[:, d, :], ALU.mult, ALU.add).then_inc(pool_added, 1)
                if d >= 2:
                    add_squares(1, d - 1)
            rstd(1)
            norm_tiles(1, G_FFN)
            f0 = 0
            for half in range(2):
                nf = F_HALF[half]

                def pair(p, I):
                    c = S_IN[half] + 2 * p + AHEAD
                    split_lo(dve, c, I)
                    F = f0 + 2 * p
                    for f in range(2):
                        dve.wait_ge(sil_ready, F + f + 4 * I + 1)
                        column_done(dve, c - AHEAD + 1, f, I)
                        if F + f >= 2 or not isinstance(I, int):
                            dve.wait_ge(hid_lo_ready, F + f + 4 * I - 1)
                        dve.tensor_tensor(tmp[:, 3 + (F + f) % 2, :], tmp[:, (F + f) % 2, :],
                                          psum[:, 2 + (F + f) % 2, :], ALU.mult).then_inc(hm_ready, 1)
                    split_lo(dve, c + 1, I)
                    for f in range(2):
                        dve.wait_ge(hid_hi_ready, F + f + 4 * I + 1)
                        q = bass.ds(2 * p + f + 4 * I, 1)
                        flat = lambda a: a.rearrange("p a t -> p (a t)")
                        dve.tensor_tensor(flat(hid_lo[:, q, :]), tmp[:, 3 + (F + f) % 2, :],
                                          flat(hid_hi[:, q, :]).bitcast(F32), ALU.subtract).then_inc(hid_lo_ready, 1)
                pair(0, 0)
                pair(1, 0)
                with dve.Fori(1, nf // 4) as i:
                    pair(0, i)
                    pair(1, i)
                if nf % 4:
                    pair(nf // 2 - 1, 0)
                for q in range(4):
                    for s in range(2):
                        split_lo(dve, S_OUT[half] + 2 * q + s + AHEAD)
                    for dd in range(2):
                        d = 2 * q + dd
                        column_done(dve, S_OUT[half] + 2 * q + 1, dd)
                        dve.tensor_tensor(xT[:, d, :], xT[:, d, :], psum[:, 4 + d % 4, :],
                                          ALU.add).then_inc(fo_added, 1)
                    if half == 1 and q:
                        for d in (2 * q - 2, 2 * q - 1):
                            if d:
                                add_squares(2, d)
                f0 += nf
            if STOP == "ffn":
                return
            add_squares(2, DT - 2)
            rstd(2)
            norm_tiles(2, G_KV)
            for j in range(8):
                split_lo(dve, S_K + j + AHEAD)
            column_done(dve, S_V + 3, 1)
            norm_tiles(3, G_MIX + DT)
            split_lo(dve, S_Q + 3)
            dve.wait_ge(small_landed, 16)
            for k in range(DT):
                i = dve.tensor_scalar(wr_g[:, k, :], wr[:, k, :], gains[:, G_FFN + DT + k:G_FFN + DT + k + 1], None,
                                      ALU.mult)
            i.then_inc(wr_g_ready, 1)

            def softplus(h, I):
                n, first_uses = h + 4 * I, isinstance(I, int) and h < 2
                dve.wait_ge(ln_ready, n + 1)
                e, hi = E[:, h % 2, :], sp_hi[:, h % 2, :]
                dve.scalar_tensor_tensor(e, head_z(h), 0.0, e, ALU.max, ALU.add).then_inc(sp_ready, 1)
                if not first_uses:
                    dve.wait_ge(c_done, n - 1)
                dve.wait_ge(sp_ready, n + 1)
                dve.tensor_copy(hi, e).then_inc(sph_ready, 1)
                dve.wait_ge(sph_ready, n + 1)
                dve.tensor_tensor(sp_lo[:, h % 2, :], e, hi.bitcast(F32), ALU.subtract).then_inc(spl_ready, 1)

            def o_minus(p, I):
                dve.wait_ge(oT_hi, p + 2 * I + 1)
                q = bass.ds(p + 2 * I, 1)
                flat = lambda a: a.rearrange("p a t -> p (a t)")
                dve.tensor_tensor(flat(hT_lo[:, q, :]), psum[:, 6 + p, :], flat(hT_hi[:, q, :]).bitcast(F32),
                                  ALU.subtract).then_inc(oT_lo, 1)

            for h in range(4):
                softplus(h, 0)
            with dve.Fori(1, NH // 4) as i:
                softplus(0, i)
                o_minus(0, i - 1)
                softplus(1, i)
                softplus(2, i)
                o_minus(1, i - 1)
                softplus(3, i)
            for p in range(2):
                o_minus(p, NH // 4 - 1)
            for j in range(3):
                split_lo(dve, S_O + j)
            split_lo(dve, S_O + 3)
            for d in range(DT):
                column_done(dve, S_O + d // 2, d % 2)
                dve.tensor_tensor(xT[:, d, :], xT[:, d, :], psum[:, d % 4, :], ALU.add).then_inc(o_added, 1)
                if d % 2 and d >= 3 and STOP != "att":
                    split_lo(dve, S_MOE + (d - 3) // 2)
            if STOP == "att":
                return

            dve.wait_ge(root_ready, 3)
            chained(dve.reciprocal(rstd_tok[:, :], rstd_tok[:, :]))
            dve.wait_ge(cleared, 5)
            dve.wait_ge(logits_done, 1)
            for t in range(TT):
                i = dve.tensor_scalar(logits[:, t, :], psum[:, 5, t * NE:(t + 1) * NE], rstd_tok[:, t:t + 1], None,
                                      ALU.mult)
            chained(i)
            for t in range(TT):
                chained(dve.max(top_v[:, t, :], logits[:, t, :]))
                i = dve.max_index(top_i[:, t, :], top_v[:, t, :], logits[:, t, :])
            chained(i)
            dve.tensor_tensor(gates[:, 0, :], top_v[:, :, 1], top_v[:, :, 0], ALU.subtract).then_inc(gap_ready, 1)
            chained(dve.tensor_copy(top_f[:, :, :], top_i[:, :, :]))
            for t in range(TT):
                dve.tensor_scalar(first[:, t, :], e_iota[:, :], top_f[:, t, 0:1], None, ALU.is_equal)
                i = dve.tensor_scalar(second[:, t, :], e_iota[:, :], top_f[:, t, 1:2], None, ALU.is_equal)
            chained(i)
            dve.tensor_tensor(chosen[:, :, :], first[:, :, :], second[:, :, :], ALU.add).then_inc(chosen_ready, 1)
            def picks(table_, t):
                for k in range(TT):
                    slot = table_[:, k, bass.ds(t, 1)]
                    dve.tensor_scalar(pick[:, k, 0:NT], slot_iota[:, :], slot, None, ALU.is_equal)
                    i = dve.tensor_scalar(pick_r[:, k, :], slot_iota[:, :], slot, rstd_tok[:, k:k + 1],
                                          ALU.is_equal, ALU.mult)
                i.then_inc(pick_ready, 1)

            FAR = 8192.0
            dve.wait_ge(ranks_done, 1)
            chained(dve.scalar_tensor_tensor(rank[:, :, :], psum[:, 4, 0:TT * NE].rearrange("p (t e) -> p t e", e=NE),
                                             FAR, chosen[:, :, :], ALU.add, ALU.mult))
            chained(dve.tensor_scalar(rank[:, :, :], rank[:, :, :], -FAR, None, ALU.add))
            chained(dve.tensor_copy(cnt[:, :], psum[:, 4, 64:64 + NE]))
            dve.wait_ge(cleared, 7)
            picks(rank, 0)
            dve.wait_ge(gap_exp, 1)
            chained(dve.tensor_scalar(gates[:, 0, :], gates[:, 1, :], 1.0, None, ALU.add))
            chained(dve.reciprocal(gates[:, 2, :], gates[:, 0, :]))
            chained(dve.tensor_tensor(gates[:, 3, :], gates[:, 1, :], gates[:, 2, :], ALU.mult))
            for t in range(TT):
                i = dve.tensor_scalar(gate_e[:, t, :], second[:, t, :], gates[:, 3, t:t + 1], None, ALU.mult)
            chained(i)
            for t in range(TT):
                dve.scalar_tensor_tensor(gate_e[:, t, :], first[:, t, :], gates[:, 2, t:t + 1], gate_e[:, t, :],
                                         ALU.mult, ALU.add)
                i = dve.tensor_scalar(row_e[:, t, :], second[:, t, :], row0[:, t:t + 1], None, ALU.add)
            chained(i)
            ks = range(1, (T - 1) // NT + 1)
            chained(dve.tensor_scalar(extra[:, 0, :], cnt[:, :], float(NT), None, ALU.is_gt))
            for k in ks[1:]:
                chained(dve.scalar_tensor_tensor(extra[:, (k - 1) % 3, :], cnt[:, :], float(k * NT),
                                                 extra[:, (k - 2) % 3, :], ALU.is_gt, ALU.add))
            ex = extra[:, (ks[-1] - 1) % 3, :]
            chained(dve.memset(cum[:, :, :], 0.0))
            chained(dve.tensor_copy(cum[:, 0, 4:], ex))
            for r in range(3):
                chained(dve.tensor_tensor(cum[:, r + 1, 4:], cum[:, r, 4:], cum[:, r, 4 - 2 ** r:4 - 2 ** r + NE],
                                          ALU.add))
            upto = cum[:, 3, 4:]
            chained(dve.tensor_tensor(before[:, :], upto, ex, ALU.subtract))
            dve.tensor_scalar(n_f[:, :], cum[:, 3, 3 + NE:4 + NE], float(NE), None, ALU.add)
            XT = TC - NE
            for j in range(XT):
                dve.tensor_scalar(is_past[:, 0, j, :], upto, float(j), None, ALU.is_le)
                dve.tensor_scalar(is_past[:, 1, j, :], before[:, :], float(j), None, ALU.is_le)
                i = dve.tensor_scalar(start[:, NE + j, :], before[:, :], float(NT), float(1 - (1 + j) * NT),
                                      ALU.mult, ALU.add)
            i = dve.memset(start[:, 0:NE, :], 1.0)
            for t in range(NE):
                i = dve.tensor_scalar(is_mine[:, t, :], e_iota[:, :], float(t), None, ALU.is_equal)
            chained(i)
            chained(dve.tensor_tensor(is_mine[:, NE:, :], is_past[:, 1, :, :], is_past[:, 0, :, :], ALU.subtract))

            def over_tasks(a):
                return a[:, :, :].unsqueeze(2).to_broadcast([P, TT, TC, NE])

            def over_tokens(a):
                return a[:, :, :].unsqueeze(1).to_broadcast([P, TT, TC, NE])

            chained(dve.tensor_reduce(e_f[:, NE:], is_past[:, 0, :, :], AX_X, ALU.add))
            chained(dve.tensor_copy(e_f[:, 0:NE], e_iota[:, :]))
            chained(dve.tensor_scalar(e_f[:, :], e_f[:, :], float(NE - 1), None, ALU.min))
            chained(dve.tensor_copy(task_e[:, :], e_f[:, :]))
            chained(dve.tensor_copy(n_tasks_i[:, :], n_f[:, :]))
            chained(dve.tensor_tensor(wide[:, :, :, :], over_tasks(rank), over_tokens(start), ALU.add))
            chained(dve.tensor_tensor(wide[:, :, :, :], wide[:, :, :, :], over_tokens(is_mine), ALU.mult))
            chained(dve.tensor_reduce(pos[:, :, :], wide[:, :, :, :], AX_X, ALU.add))
            chained(dve.tensor_scalar(pos[:, :, :], pos[:, :, :], -1.0, None, ALU.add))
            for n, a in enumerate((row_e, gate_e)):
                chained(dve.tensor_tensor(wide[:, :, :, :], over_tasks(a), over_tokens(is_mine), ALU.mult))
                chained(dve.tensor_reduce(row_gate[:, :, :, n], wide[:, :, :, :], AX_X, ALU.add))
            dve.memset(primed[:, 0:1], 0.0).then_inc(tables_ready, 1)
            for k, first_count in enumerate((m_ready, m_ready, y_kept, y_kept, g_summed, u_summed)):
                dve.memset(primed[:, k + 1:k + 2], 0.0).then_inc(first_count, 1)
            dve.wait_ge(g_summed, 1)

            def select(t):
                for k in range(DT):
                    dve.wait_ge(sel_hi, DT * t + k + 1)
                    dve.scalar_tensor_tensor(x_sel[:, 1, k, :], psum[:, k % 4, 0:NT],
                                             gains[:, G_FFN + DT + k:G_FFN + DT + k + 1],
                                             x_sel[:, 0, k, :].bitcast(F32), ALU.mult, ALU.subtract).then_inc(sel_lo, 1)

            def keep_rows(t, q):
                dve.wait_ge(y_turned, 4 * t + q + 1)
                b = 4 + 2 * (q % 2)
                cols = slice(q * CW, (q + 1) * CW)
                dve.tensor_scalar(y_rows[:, 0, cols], psum[:, b, 0:CW], info[:, 0, 1:2], None, ALU.mult)
                dve.tensor_scalar(y_rows[0:NT - P, 1, cols], psum[0:NT - P, b, CW:2 * CW],
                                  info[0:NT - P, 1, 1:2], None, ALU.mult).then_inc(y_kept, 1)

            select(0)

            def task(t):
                T11 = t * (SUBS_TASK // RING)
                dve.wait_ge(info_done, t + 1)
                dve.wait_ge(y_kept, 4 * t + 2)
                dve.tensor_copy(info[:, :, :], psum[:, 5, 0:4].rearrange("p (a b) -> p a b", a=2)).then_inc(info_ready, 1)
                with dve.Fori(0, PAIRS // 2) as i:
                    for p in range(2):
                        n = PAIRS * t + 2 * i + p
                        c = S_MOE + 2 * p
                        split_lo(dve, c + AHEAD, T11 + i)
                        dve.wait_ge(g_half, n + 1)
                        dve.tensor_tensor(gate_s[:, p, :, :], gate_s[:, p, :, :], psum[:, 0:2, 0:NT],
                                          ALU.add).then_inc(g_summed, 1)
                        split_lo(dve, c + 1 + AHEAD, T11 + i)
                        dve.wait_ge(u_half, n + 1)
                        dve.tensor_tensor(up_s[:, p, :, :], up_s[:, p, :, :], psum[:, 2:4, 0:NT],
                                          ALU.add).then_inc(u_summed, 1)
                        dve.wait_ge(g_silu, n + 1)
                        dve.wait_ge(u_summed, n + 2)
                        dve.tensor_tensor(up_s[:, p, :, :], up_s[:, p, :, :], gate_s[:, p, :, :],
                                          ALU.mult).then_inc(m_ready, 1)
                dve.wait_ge(rows_stored, 32 * t + 32)
                dve.wait_ge(info_ready, 3 * t + 1)
                dve.scalar_tensor_tensor(info_t[:, :], info[:, :, 0], 0.0, spare_row[:, :],
                                         ALU.is_equal, ALU.mult).then_inc(info_ready, 1)
                dve.wait_ge(info_ready, 3 * t + 2)
                dve.scalar_tensor_tensor(info_row[:, :], info[:, :, 0], -1.0, info_t[:, :],
                                         ALU.add, ALU.add).then_inc(info_ready, 1)
                for q in range(Q_OUT):
                    for j in range(4):
                        split_lo(dve, C2 + 4 * q + j + AHEAD, T11)
                        if j == 1 and q:
                            keep_rows(t, q - 1)
                        if j == 1 and q == 0:
                            picks(pos, t + 1)
                    dve.wait_ge(y_half, 4 * t + q + 1)
                    b = 4 + 2 * (q % 2)
                    dve.tensor_tensor(yT[:, q % 2, :, 0:NT], y_s[:, q % 2, :, :], psum[:, b:b + 2, 0:NT],
                                      ALU.add).then_inc(yT_ready, 1)
                select(t + 1)
                keep_rows(t, Q_OUT - 1)

            task_loop(dve, task)
            for k in range(TT):
                dve.wait_ge(y2_landed[k], 32)
                dve.tensor_tensor(y2_in[:, k, 0, :], y2_in[:, k, 0, :], y2_in[:, k, 1, :],
                                  ALU.add).then_inc(sum_step, 1)
                dve.wait_ge(sum_step, 2 * k + 1)
                dve.tensor_tensor(x2_in[:, k, :], x2_in[:, k, :], y2_in[:, k, 0, :], ALU.add).then_inc(sum_step, 1)
            dve.wait_ge(root_end, 1)
            chained(dve.reciprocal(ss[:, :], ss[:, :]))
            dve.wait_ge(g_row_landed, 16)
            for k in range(TT):
                dve.scalar_tensor_tensor(x2_in[:, k, :], x2_in[:, k, :], ss[:, k:k + 1], g_row[:, :],
                                         ALU.mult, ALU.mult).then_inc(out_ready, 1)

        @block.tensor
        def _(pe):
            pe.wait_ge(consts, 4)
            for t in range(TT):
                pe.wait_ge(x_landed[t], 16)
                for d in range(DT):
                    i = pe.transpose(psum[:, d, t * P:(t + 1) * P], x_in[:, t, d * P:(d + 1) * P], ident[:, :])
                    if t == TT - 1:
                        i.then_inc(x_turned, 1)
            pe.wait_ge(x_act, 1)
            pe.wait_ge(gains_landed, 64)
            pe.transpose(psum[:, 0, 0:NV], gains_in[:, :], ident[0:NV, 0:NV]).then_inc(gains_T, 1)
            pe.wait_ge(gains_ready, 1)
            pe.wait_ge(bands_ready, NG)
            pe.wait_ge(x_n_act, TT // 2)
            pe.wait_ge(x_n_dve, TT // 2)
            for d in range(DT):
                pe.wait_ge(x_dve if d % 2 else x_act, d // 2 + 1)
                for t in range(TT):
                    n = min(P + PAD, T - t * P)
                    i = pe.matmul(psum[:, d, t * P:t * P + n], x_n[:, t, d * P:(d + 1) * P], band[:, min(t, 1), d // 2, 0:n],
                                  start=t == 0, stop=t == TT - 1, skip_group_check=True)
                i.then_inc(pooled, 1)

            def norm(n):
                pe.wait_ge(acc_step, 6 * n)
                pe.matmul(psum[:, 0, :], ones[:, :], tmp[:, 2, :], start=True, stop=False)
                pe.wait_ge(sq_ready, DT * n)
                pe.matmul(psum[:, 0, :], ones[:, :], tmp[:, 1, :], start=False, stop=True).then_inc(sq_summed, 1)

            for d in range(DT):
                if d == 0:
                    pe.wait_ge(lo_ready, 1)
                pe.wait_ge(h_lo, 2 * (d // 2) + 2)
                for k in range(2):
                    n0 = (d // 2) * 2 * GW + k * GW + (d % 2) * P
                    i = product(pe, psum[:, d, :], w_hi[:, 0, n0:n0 + P], w_lo[:, 0, n0:n0 + P],
                                hT_hi[:, 2 * (d // 2) + k, :], hT_lo[:, 2 * (d // 2) + k, :], k == 0, k == 1)
                if d % 4 == 3:
                    i.then_inc(w_used if d == DT - 1 else half_done, 1)
            norm(1)
            f0 = 0
            for half in range(2):
                nf = F_HALF[half]

                def pair(p, I):
                    for u in range(2):
                        c = S_IN[half] + 2 * p + u
                        pe.wait_ge(lo_ready, c + 4 * I + 1)
                        for f in range(2):
                            F = f0 + 2 * p + f
                            if F >= 2 or not isinstance(I, int):
                                pe.wait_ge(hm_ready if u else sil_ready, F + 4 * I - 1)
                            for k in range(DT):
                                if F == 0 and u == 0 and isinstance(I, int):
                                    pe.wait_ge(h_lo, DT + k + 1)
                                i = product(pe, psum[:, 2 * u + f, :], *w_tile(c, k, f), hT_hi[:, k, :],
                                            hT_lo[:, k, :], k == 0, k == DT - 1)
                            i.then_inc(w_used if f else half_done, 1)

                pair(0, 0)
                pair(1, 0)
                with pe.Fori(1, nf // 4) as i_:
                    pair(0, i_)
                    pair(1, i_)
                if nf % 4:
                    pair(nf // 2 - 1, 0)
                for q in range(4):
                    for s in range(2):
                        c = S_OUT[half] + 2 * q + s
                        pe.wait_ge(lo_ready, c + 1)
                        if q == 0:
                            pe.wait_ge(hid_lo_ready, f0 + (s + 1) * (nf // 2))
                        for dd in range(2):
                            d = 2 * q + dd
                            if s == 0 and DT * half + d >= 4:
                                pe.wait_ge(fo_added, DT * half + d - 3)
                            for f in range(nf // 2):
                                F = s * (nf // 2) + f
                                i = product(pe, psum[:, 4 + d % 4, :], *w_tile(c, f, dd), hid_hi[:, F, :],
                                            hid_lo[:, F, :], F == 0, F == nf - 1)
                            i.then_inc(w_used if dd else half_done, 1)
                f0 += nf
            if STOP == "ffn":
                return

            def project(s0, n0, free, after=None, h=None):
                for j in range(4):
                    c = s0 + j
                    pe.wait_ge(lo_ready, c + 1)
                    for f in range(2):
                        n = n0 + 2 * j + f
                        if n >= 4:
                            pe.wait_ge(free, n - 3)
                        for k in range(DT):
                            if h is not None and n == n0:
                                pe.wait_ge(h_lo, h * DT + k + 1)
                            i = product(pe, psum[:, n % 4, :], *w_tile(c, k, f), hT_hi[:, k, :],
                                        hT_lo[:, k, :], k == 0, k == DT - 1)
                        i.then_inc(w_used if f else half_done, 1)
                        if after and n > n0:
                            after(n - n0 - 1)

            norm(2)
            project(S_K, 0, proj_kept, h=2)
            for j in range(4):
                c = S_V + j
                pe.wait_ge(lo_ready, c + 1)
                for t in range(TT):
                    n = DT + 4 * j + t
                    pe.wait_ge(proj_kept, n - 7 if j >= 2 else DT)
                    for k in range(DT):
                        ts = slice(t * P, (t + 1) * P)
                        o = psum[:, 4 * (j % 2) + t, 0:CW]
                        wh, wl = (w[:, c % RING, k * CW:(k + 1) * CW] for w in (w_hi, w_lo))
                        pe.matmul(o, hT_hi[:, k, ts], wh, start=k == 0, stop=False)
                        pe.matmul(o, hT_hi[:, k, ts], wl, start=False, stop=False)
                        i = pe.matmul(o, hT_lo[:, k, ts], wh, start=False, stop=k == DT - 1)
                    if t % 2:
                        i.then_inc(w_used if t == TT - 1 else half_done, 1)
            project(S_Q, 3 * DT, proj_kept, h=3)
            pe.wait_ge(proj_kept, 4 * DT)
            pe.wait_ge(consts, 6)
            for h in range(NH + 2):
                if h < NH:
                    r = slice(HD * (h % 2), HD * (h % 2) + HD)
                    if h >= 2:
                        pe.wait_ge(a_ready, h - 1)
                    for b, blocks in enumerate(((0,), (1, 3), (2,))):
                        col = 0
                        for s in blocks:
                            n = T - s * P
                            pe.matmul(psum[:, 3 * (h % 2) + b, col:col + n], KT[r, h // 2, s * P:(s + 1) * P],
                                      QT[r, h // 2, s * P:T], start=col == 0, stop=False, skip_group_check=True)
                            i = pe.matmul(psum[:, 3 * (h % 2) + b, col:col + P], ident_r[:, :], not_causal[:, :],
                                          start=False, stop=False, skip_group_check=True)
                            col += n
                    i.then_inc(z_done, 1)
                if 1 <= h <= NH:
                    n = h - 1
                    for part, ready in ((sp_hi, sph_ready), (sp_lo, spl_ready)):
                        pe.wait_ge(ready, n + 1)
                        for s in range(TT):
                            b, col = ((0, 0), (1, 0), (2, 0), (1, 384))[s]
                            for j in range(s, TT):
                                w = T - j * P
                                o = psum[:, 3 * (n % 2) + b, col + (j - s) * P:col + (j - s) * P + w]
                                i = pe.matmul(o, (neg_tri if j == s else neg_ones)[:, :],
                                              part[:, n % 2, SEG[j]:SEG[j] + w], start=False,
                                              stop=part is sp_lo and j == TT - 1, skip_group_check=True)
                    i.then_inc(c_done, 1)
                if h >= 2:
                    n = h - 2
                    pe.wait_ge(a_ready, n + 1)
                    if n % 2 == 0 and n >= 4:
                        pe.wait_ge(oT_lo, n // 2 - 1)
                    r = slice(HD * (n % 2), HD * (n % 2) + HD)
                    for s in range(TT):
                        i = pe.matmul(psum[r, 6 + (n // 2) % 2, s * P:T], V[:, s, n * HD:(n + 1) * HD],
                                      A[:, n % 2, SEG[s]:SEG[s] + T - s * P], start=s == 0, stop=s == TT - 1,
                                      skip_group_check=True)
                    i.then_inc(av_done, 1)
            pe.wait_ge(oT_lo, DT)

            def follow(d):
                pe.wait_ge(o_added, d + 1)
                if d >= 2:
                    pe.wait_ge(x2_kept, d - 1)
                for t in range(TT):
                    i = pe.transpose(psum[:, 6 + d % 2, t * P:(t + 1) * P], xT[:, d, t * P:(t + 1) * P], ident[:, :])
                i.then_inc(x2_turned, 1)
                if d == 0:
                    pe.wait_ge(wr_g_ready, 1)
                for t in range(TT):
                    i = pe.matmul(psum[:, 5, t * NE:(t + 1) * NE], xT[:, d, t * P:(t + 1) * P], wr_g[:, d, :],
                                  start=d == 0 and t == 0, stop=d == DT - 1, skip_group_check=True)
                if d == DT - 1:
                    i.then_inc(logits_done, 1)
                pe.wait_ge(sq_ready, 2 * DT + d + 1)
                for t in range(TT):
                    i = pe.matmul(psum[:, 4, t:t + 1], tmp[:, d % 2, t * P:(t + 1) * P], ones[:, 0:1],
                                  start=d == 0 and t == 0, stop=d == DT - 1, skip_group_check=True)
                i.then_inc(sq_summed, 1)

            project(S_O, 0, o_added, follow)
            follow(DT - 1)
            pe.wait_ge(chosen_ready, 1)
            for t in range(TT):
                for u in range(t + 1):
                    pe.matmul(psum[:, 4, t * NE:(t + 1) * NE], (earlier if u == t else ones)[:, :],
                              chosen[:, u, :], start=u == 0, stop=u == t)
            for u in range(TT):
                i = pe.matmul(psum[:, 4, 64:64 + NE], ones[:, :], chosen[:, u, :], start=u == 0, stop=u == TT - 1)
            i.then_inc(ranks_done, 1)

            def select(t):
                pe.wait_ge(pick_ready, t + 1)
                for k in range(DT):
                    if k >= 4:
                        pe.wait_ge(sel_lo, DT * t + k - 3)
                    for u in range(TT):
                        i = pe.matmul(psum[:, k % 4, 0:NT], x2_rows[:, u, k * P:(k + 1) * P], pick_r[:, u, :],
                                      start=u == 0, stop=u == TT - 1)
                    i.then_inc(sel_done, 1)

            pe.wait_ge(x2_kept, DT)
            select(0)

            def two(o, c, k, f, x, start_, stop_):
                wh, wl = w_tile(c, k, f)
                both = o.rearrange("p (a n) -> p a n", a=2)
                if stop_:
                    pe.matmul(o[:, 0:NT], wl, x[:, 0, :], start=False, stop=False, skip_group_check=True)
                    return pe.matmul(both, wh, x, start=False, stop=True, skip_group_check=True)
                pe.matmul(both, wh, x, start=start_, stop=False, skip_group_check=True)
                return pe.matmul(o[:, 0:NT], wl, x[:, 0, :], start=False, stop=False, skip_group_check=True)

            def turn(t, q):
                pe.wait_ge(yT_ready, 4 * t + q + 1)
                b = 4 + 2 * (q % 2)
                for part in range(2):
                    for dd in range(2):
                        o = (2 * part + dd) * P
                        i = pe.transpose(psum[:, b, o:o + P], yT[:, q % 2, dd, part * P:(part + 1) * P], ident[:, :])
                i.then_inc(y_turned, 1)

            def task(t):
                T11 = t * (SUBS_TASK // RING)
                pe.wait_ge(sel_lo, DT * t + DT)
                for part in range(2):
                    for u in range(TT):
                        i = pe.matmul(psum[:, 5, 2 * part:2 * part + 2], pick[:, u, part * P:(part + 1) * P],
                                      row_gate[:, u, bass.ds(t, 1), :].rearrange("p a b -> p (a b)"),
                                      start=u == 0, stop=u == TT - 1)
                i.then_inc(info_done, 1)
                with pe.Fori(0, PAIRS // 2) as i_:
                    for p in range(2):
                        n = PAIRS * t + 2 * i_ + p
                        for u in range(2):
                            c = S_MOE + 2 * p + u
                            pe.wait_ge(lo_ready, c + 4 * (T11 + i_) + 1)
                            pe.wait_ge(u_summed if u else g_summed, n + 1)
                            for f in range(2):
                                for k in range(DT):
                                    i = two(psum[:, 2 * u + f, 0:2 * NT], c, k, f, x_sel[:, :, k, :], k == 0, k == DT - 1)
                                i.then_inc(w_used if f else half_done, 1)
                pe.wait_ge(info_ready, 3 * t + 1)
                for q in range(Q_OUT):
                    pe.wait_ge(y_kept, 4 * t + q + 1)
                    for j in range(4):
                        c = C2 + 4 * q + j
                        pe.wait_ge(lo_ready, c + 4 * T11 + 1)
                        if q == 0:
                            pe.wait_ge(mh_lo, PAIRS * t + 2 + (FS * (j + 1) + 1) // 2)
                        for dd in range(2):
                            for f in range(FS):
                                i = two(psum[:, 4 + 2 * (q % 2) + dd, 0:2 * NT], c, f, dd, hid[:, :, FS * j + f, :],
                                        j == 0 and f == 0, j == 3 and f == FS - 1)
                            i.then_inc(w_used if dd else half_done, 1)
                        if j == 0 and q:
                            turn(t, q - 1)
                pe.wait_ge(g_summed, PAIRS * t + PAIRS + 1)
                pe.wait_ge(u_summed, PAIRS * t + PAIRS + 1)
                select(t + 1)
                turn(t, Q_OUT - 1)

            task_loop(pe, task)


_OUTS = [((1, 512, 1024), "float32")]
_INS = ["x", "g_mix", "g_ffn", "pool_w", "pool_scale", "g_kv", "w_kv", "w_q", "w_o", "ffn_in", "ffn_out",
        "w_router", "moe_in", "moe_out", "g_final"]


def kernel(**inputs):
    import numpy as _np
    import concourse.bacc as _bacc
    from concourse import mybir as _mybir
    from concourse.bass_utils import run_bass_kernel_spmd as _run

    nc = _bacc.Bacc("TRN2", target_bir_lowering=False, num_devices=1)
    arrays, args = {}, []
    for name in _INS:
        a = _np.ascontiguousarray(inputs[name])
        arrays[f"in_{name}_dram"] = a
        args.append(nc.dram_tensor(f"in_{name}_dram", a.shape, _mybir.dt.from_np(a.dtype), kind="ExternalInput").ap())
    for i, (shape, dtype) in enumerate(_OUTS):
        dt = _mybir.dt.from_np(_np.dtype(dtype))
        args.append(nc.dram_tensor(f"out_{i}_dram", shape, dt, kind="ExternalOutput").ap())
    trunk(nc, *args)
    r = _run(nc, [arrays], core_ids=[0])
    return r.results[0]["out_0_dram"]
```

```python
from contextlib import ExitStack

import concourse.bass as bass
from concourse import mybir

F32 = mybir.dt.float32
F32R = mybir.dt.float32r
I32 = mybir.dt.int32
U32 = mybir.dt.uint32
ALU = mybir.AluOpType
ACT = mybir.ActivationFunctionType
AX_X = mybir.AxisListType.X

P = 128


def trunk(nc, x, g_mix, g_ffn, pool_w, pool_scale, g_kv, w_kv, w_q, w_o, ffn_in, ffn_out,
          w_router, moe_in, moe_out, g_final, out):
    _, T, D = x.shape
    DT, TT = D // P, T // P
    NG, GW = pool_w.shape[1], pool_w.shape[2]
    WINDOWS = (2, 4, 8, 16)
    FF = ffn_out.shape[1]
    NE, FE = moe_out.shape[1], moe_out.shape[2]
    HD = 64
    NH = D // HD
    EPS = 1e-6
    RING = 4
    SUB = 2048
    CW = SUB // DT
    AHEAD = 3
    F_TILES = FF // P
    F_HALF = (12, F_TILES - 12)
    S_POOL = 0
    S_FFN = 1
    S_IN = (S_FFN, S_FFN + F_HALF[0] + 8)
    S_OUT = (S_FFN + F_HALF[0], S_FFN + F_TILES + 8)
    S_K = S_FFN + F_TILES + 16
    S_V = S_K + 4
    S_Q = S_V + 4
    S_O = S_Q + 4
    S_MOE = S_O + 4
    NT = 144
    MAX_EXTRA = (2 * T - 1) // NT
    MAX_TASKS = NE + MAX_EXTRA
    FE_TILES = FE // P
    SUBS_IN = FE_TILES
    Q_OUT = D // 256
    SUBS_OUT = Q_OUT * 4
    FS = FE_TILES // 4
    SUBS_TASK = SUBS_IN + SUBS_OUT
    assert SUBS_TASK % RING == 0 and SUBS_IN % RING == 0

    with ExitStack() as ctx:
        base = 16512
        place = [base]

        def at(name, shape, dt, offset):
            return nc.alloc_sbuf_tensor_at(name, shape, dt, offset=offset)

        def take(nbytes):
            o = place[0]
            place[0] += nbytes
            return o

        o_raw, o_hi, o_lo = take(RING * SUB * 4), take(RING * SUB * 4), take(RING * SUB * 4)
        o_xT = take(DT * T * 4)
        o_hT = take(2 * DT * T * 4)
        o_big = take(12 * T * 4 * 2)
        o_tmp = take(5 * T * 4)
        o_const = place[0]

        raw = at("raw", [P, RING, SUB], F32, o_raw)
        w_hi = at("w_hi", [P, RING, SUB], F32R, o_hi)
        w_lo = at("w_lo", [P, RING, SUB], F32R, o_lo)
        xT = at("xT", [P, DT, T], F32, o_xT)
        hT_hi = at("hT_hi", [P, DT, T], F32R, o_hT)
        hT_lo = at("hT_lo", [P, DT, T], F32R, o_hT + DT * T * 4)
        tmp = at("tmp", [P, 5, T], F32, o_tmp)
        hid_hi = at("hid_hi", [P, 12, T], F32R, o_big)
        hid_lo = at("hid_lo", [P, 12, T], F32R, o_big + 12 * T * 4)
        x_in = at("x_in", [P, TT, D], F32, o_big)
        PAD = WINDOWS[-1]
        x_n = at("x_n", [P, TT, D], F32, o_big + TT * D * 4)
        band = at("band", [P, 2, NG, P + PAD], F32, o_big + 2 * TT * D * 4)
        head_cols = at("head_cols", [P, NG, PAD], F32, o_big + 2 * TT * D * 4 + 2 * NG * (P + PAD) * 4)
        KT = at("KT", [P, DT, T], F32, o_big)
        QT = at("QT", [P, DT, T], F32, o_big + DT * T * 4)
        V = at("V", [P, TT, D], F32, o_big + 2 * DT * T * 4)
        SEG = {0: 0, 1: 512, 3: 896, 2: 1024}
        HC = 1280
        E = at("E", [P, 2, HC], F32, o_tmp)
        sp_hi = at("sp_hi", [P, HC], F32R, o_hi + (S_Q % RING) * SUB * 4)
        sp_lo = at("sp_lo", [P, HC], F32R, o_lo + (S_Q % RING) * SUB * 4)
        oT_hi = at("oT_hi", [P, DT, T], F32R, o_big + DT * T * 4)
        oT_lo = at("oT_lo", [P, DT, T], F32R, o_big)

        def const(name, shape, dt=F32):
            n = 4
            for s in shape[1:]:
                n *= s
            return at(name, shape, dt, take((n + 31) // 32 * 32))

        NV = 6 * DT
        gains_in = at("gains_in", [NV, P], F32, o_tmp)
        gains = const("gains", [P, NV])
        ident = const("ident", [P, P])
        ones = const("ones", [P, P])
        neg_ones = const("neg_ones", [P, P], F32R)
        ident_r = const("ident_r", [P, P], F32R)
        o_mask = place[0]
        not_causal = const("not_causal", [P, P], F32R)
        neg_tri = const("neg_tri", [P, P], F32R)
        eps = const("eps", [P, 1])
        inv_count = const("inv_count", [P, PAD])
        count = const("count", [P, PAD])
        x2_rows = at("x2_rows", [P, TT, D], F32, o_big + 2 * DT * T * 4)
        SLOTS = 2 * P
        o_pick = o_big
        pick = at("pick", [P, TT, SLOTS], F32, o_pick)
        pick_r = at("pick_r", [P, TT, NT], F32, o_pick + TT * SLOTS * 4)
        y_rows = at("y_rows", [P, 2, D], F32, o_pick + 2 * TT * SLOTS * 4)
        g_row = at("g_row", [P, D], F32, o_pick + 2 * TT * SLOTS * 4 + 2 * D * 4)
        x_sel = at("x_sel", [P, 2, DT, NT], F32R, o_xT)
        hid = at("hid", [P, 2, FE_TILES, NT], F32R, o_xT + 2 * DT * NT * 4)
        o_yT = o_xT + 2 * (DT + FE_TILES) * NT * 4
        yT = at("yT", [P, 2, 2, SLOTS], F32, o_yT)
        assert o_yT + 4 * SLOTS * 4 <= o_big
        gate_s = at("gate_s", [P, 2, 2, NT], F32, o_tmp)
        up_s = at("up_s", [P, 2, 2, NT], F32, o_tmp + 4 * NT * 4)
        y_s = at("y_s", [P, 2, 2, NT], F32, o_tmp + 8 * NT * 4)
        TC = MAX_TASKS + 1
        o_t = [o_pick + 2 * TT * SLOTS * 4 + 3 * D * 4]

        def table(name, shape, dt=F32):
            n = 4
            for k in shape[1:]:
                n *= k
            a = at(name, shape, dt, o_t[0])
            o_t[0] += (n + 31) // 32 * 32
            return a

        logits, top_v = table("logits", [P, TT, NE]), table("top_v", [P, TT, NE])
        top_i, top_f = table("top_i", [P, TT, NE], U32), table("top_f", [P, TT, NE])
        first, second = table("first", [P, TT, NE]), table("second", [P, TT, NE])
        chosen, gate_e = table("chosen", [P, TT, NE]), table("gate_e", [P, TT, NE])
        rank, row_e = table("rank", [P, TT, NE]), table("row_e", [P, TT, NE])
        gates = table("gates", [P, 4, TT])
        cnt = table("cnt", [P, NE])
        extra = table("extra", [P, 3, NE])
        cum = table("cum", [P, 4, NE + 4])
        before = table("before", [P, NE])
        n_f = table("n_f", [P, 1])
        is_mine = table("is_mine", [P, TC, NE])
        is_past = table("is_past", [P, 2, TC - NE, NE])
        start = table("start", [P, TC, NE])
        e_f = table("e_f", [P, TC])
        wide = table("wide", [P, TT, TC, NE])
        assert o_t[0] <= o_big + 2 * DT * T * 4
        pos = const("pos", [P, TT, TC])
        row_gate = const("row_gate", [P, TT, TC, 2])
        task_e = const("task_e", [P, TC], I32)
        n_tasks_i = const("n_tasks_i", [P, 1], I32)
        slot_iota = const("slot_iota", [P, NT])
        e_iota = const("e_iota", [P, NE])
        row0 = const("row0", [P, TT])
        spare_row = const("spare_row", [P, 2])
        earlier = at("earlier", [P, P], F32, o_mask)
        wr = const("wr", [P, DT, NE])
        wr_g = const("wr_g", [P, DT, NE])
        rstd_tok = const("rstd_tok", [P, TT])
        info = const("info", [P, 2, 2])
        info_t = const("info_t", [P, 2])
        info_row = const("info_row", [P, 2], I32)
        ss = const("ss", [P, TT])
        primed = const("primed", [P, 7])
        wait_holder = const("wait_holder", [P, 1])
        y2_dram = nc.dram_tensor("y2_dram", (2 * T + SLOTS, D), F32, kind="Internal").ap()
        y2_in = at("y2_in", [P, TT, 2, D], F32, o_xT)
        sq_out = at("sq_out", [P, 2, D], F32, o_xT + TT * 2 * D * 4)
        psum = ctx.enter_context(nc.psum_tensor("psum", [P, 8, T], F32))
        assert place[0] <= nc.sbuf_usable_end, place[0]

        def sem(name):
            return ctx.enter_context(nc.semaphore(name))

        raw_landed = [sem(f"raw_landed{s}") for s in range(RING)]
        hi_ready, lo_ready = sem("hi_ready"), sem("lo_ready")
        half_done, w_used = sem("half_done"), sem("w_used")
        consts, const_steps, gains_landed, gains_T, gains_ready = (
            sem("consts"), sem("const_steps"), sem("gains_landed"), sem("gains_T"), sem("gains_ready"))
        x_landed = [sem(f"x_landed{t}") for t in range(TT)]
        x_turned, x_act, x_dve = sem("x_turned"), sem("x_act"), sem("x_dve")
        inv_ready, band_step, bands_ready = sem("inv_ready"), sem("band_step"), sem("bands_ready")
        in_squared, in_root, in_rstd, x_n_act, x_n_dve, pooled = (
            sem("in_squared"), sem("in_root"), sem("in_rstd"), sem("x_n_act"), sem("x_n_dve"), sem("pooled"))
        acc_step = sem("acc_step")
        sq_ready, sq_summed, root_ready, rstd_ready, hf_ready, h_hi, h_lo = (
            sem("sq_ready"), sem("sq_summed"), sem("root_ready"), sem("rstd_ready"),
            sem("hf_ready"), sem("h_hi"), sem("h_lo"))
        dve_step = sem("dve_step")
        pool_added = sem("pool_added")
        sil_ready, hm_ready, hid_hi_ready, hid_lo_ready = (
            sem("sil_ready"), sem("hm_ready"), sem("hid_hi_ready"), sem("hid_lo_ready"))
        fo_added, proj_kept, o_added = sem("fo_added"), sem("proj_kept"), sem("o_added")
        z_done, abs_ready, exp_ready, ln_ready, sp_ready, sph_ready, spl_ready = (
            sem("z_done"), sem("abs_ready"), sem("exp_ready"), sem("ln_ready"), sem("sp_ready"),
            sem("sph_ready"), sem("spl_ready"))
        c_done, a_ready, av_done, o_hi_ready, o_lo_ready = (
            sem("c_done"), sem("a_ready"), sem("av_done"), sem("o_hi_ready"), sem("o_lo_ready"))
        stored = sem("stored")
        small_landed, wr_g_ready = sem("small_landed"), sem("wr_g_ready")
        x2_turned, x2_kept, logits_done = sem("x2_turned"), sem("x2_kept"), sem("logits_done")
        gap_ready, gap_exp, chosen_ready, ranks_done, tables_ready = (
            sem("gap_ready"), sem("gap_exp"), sem("chosen_ready"), sem("ranks_done"), sem("tables_ready"))
        cleared = sem("cleared")
        pick_ready, sel_done, sel_hi, sel_lo, info_done, info_ready = (
            sem("pick_ready"), sem("sel_done"), sem("sel_hi"), sem("sel_lo"), sem("info_done"),
            sem("info_ready"))
        g_half, g_summed, g_silu, u_half, u_summed, m_ready, mh_hi, mh_lo = (
            sem("g_half"), sem("g_summed"), sem("g_silu"), sem("u_half"), sem("u_summed"),
            sem("m_ready"), sem("mh_hi"), sem("mh_lo"))
        y_half, yT_ready, y_turned, y_kept, rows_stored = (
            sem("y_half"), sem("yT_ready"), sem("y_turned"), sem("y_kept"), sem("rows_stored"))
        y2_landed, sum_step, ss_ready, root_end, out_ready = (
            [sem(f"y2_landed{k}") for k in range(TT)], sem("sum_step"), sem("ss_ready"), sem("root_end"), sem("out_ready"))

        G_MIX, G_FFN, G_SCALE, G_KV = 0, 16, 32, 40

        def load(sp, c, dst, src, I=0):
            if not (isinstance(I, int) and c + 4 * I < RING):
                sp.wait_ge(lo_ready, c + 4 * I - RING + 1)
            sp.dma_start(dst, src).then_inc(raw_landed[c % RING], 16)

        def split_hi(act, c, I=0):
            act.wait_ge(raw_landed[c % RING], 16 * (c // RING + I + 1))
            if not (isinstance(I, int) and c + 4 * I < RING):
                act.wait_ge(w_used, c + 4 * I - RING + 1)
            act.activation(w_hi[:, c % RING, :], raw[:, c % RING, :], ACT.Copy).then_inc(hi_ready, 1)

        def split_lo(dve, c, I=0):
            dve.wait_ge(hi_ready, c + 4 * I + 1)
            dve.tensor_tensor(w_lo[:, c % RING, :], raw[:, c % RING, :],
                              w_hi[:, c % RING, :].bitcast(F32), ALU.subtract).then_inc(lo_ready, 1)

        def product(pe, o, whi, wlo, hi, lo, start, stop):
            pe.matmul(o, whi, hi, start=start, stop=False)
            pe.matmul(o, whi, lo, start=False, stop=False)
            return pe.matmul(o, wlo, hi, start=False, stop=stop)

        def w_tile(c, k, f, n=CW):
            s = slice(k * n + f * P, k * n + f * P + P)
            return w_hi[:, c % RING, s], w_lo[:, c % RING, s]

        def in_columns(w, c0, n=CW):
            return w.rearrange("(k p) n -> p k n", p=P)[:, :, c0:c0 + n]

        def sub3(c, k, n):
            return raw[:, c % RING, 0:k * n].rearrange("p (k n) -> p k n", k=k)

        def column_done(eng, c, f, I=0):
            eng.wait_ge(w_used if f else half_done, c + 4 * I + 1)

        def column_done_q(eng, m, I):
            eng.wait_ge(w_used if m % 2 else half_done, S_Q + m // 2 + I + 1)

        PAIRS = FE_TILES // 2
        C2 = S_MOE + SUBS_IN

        def task_loop(eng, body):
            eng.wait_ge(tables_ready, 1)
            n_tasks = eng.value_load(n_tasks_i[0:1, 0:1], min_val=NE, max_val=MAX_TASKS)
            with eng.Fori(0, MAX_TASKS) as t:
                with eng.If(t < n_tasks):
                    body(t)
            return n_tasks

        def head_z(h):
            return psum[:, 3 * (h % 2):3 * (h % 2) + 3, :].rearrange("p b t -> p (b t)")[:, 0:HC]

        block = ctx.enter_context(nc.Block())

        @block.sync
        def _(sp):
            for t in range(TT):
                sp.dma_start(x_in[:, t, :], x[0, t * P:(t + 1) * P, :]).then_inc(x_landed[t], 16)
            c = S_POOL
            load(sp, c, sub3(c, DT, GW), in_columns(pool_w[0].rearrange("g c n -> (g c) n"), 0))
            w_in = ffn_in[0]
            w_out = ffn_out[0].rearrange("(f p) n -> p f n", p=P)
            f0 = 0
            for half in range(2):
                nf = F_HALF[half]
                for p in range(nf // 2):
                    for u in range(2):
                        c = S_IN[half] + 2 * p + u
                        load(sp, c, sub3(c, DT, CW), in_columns(w_in, u * FF + (f0 + 2 * p) * P))
                for q in range(4):
                    for s in range(2):
                        c = S_OUT[half] + 2 * q + s
                        load(sp, c, sub3(c, nf // 2, CW),
                             w_out[:, f0 + s * (nf // 2):f0 + (s + 1) * (nf // 2), q * CW:(q + 1) * CW])
                f0 += nf
            for w, s0, c0 in ((w_kv, S_K, 0), (w_kv, S_V, D), (w_q[0], S_Q, 0), (w_o[0], S_O, 0)):
                for j in range(4):
                    load(sp, s0 + j, sub3(s0 + j, DT, CW), in_columns(w, c0 + j * CW))
            def task_loads(t, e):
                w1 = moe_in[0][bass.ds(e, 1)].rearrange("a (k p) n -> p (a k) n", p=P)
                w2 = moe_out[0][bass.ds(e, 1)].rearrange("a (f p) n -> p (a f) n", p=P)
                T11 = t * (SUBS_TASK // RING)
                with sp.Fori(0, PAIRS // 2) as i:
                    for j in range(4):
                        c = S_MOE + j
                        load(sp, c, sub3(c, DT, CW),
                             w1[:, :, bass.ds(4 * P * i + ((j % 2) * FE + (j // 2) * CW), CW)], T11 + i)
                with sp.Fori(0, Q_OUT) as q:
                    for j in range(4):
                        load(sp, C2 + j, sub3(C2 + j, FS, CW),
                             w2[:, j * FS:(j + 1) * FS, bass.ds(CW * q, CW)], T11 + q)

            with sp.Fori(0, NE) as t:
                task_loads(t, t)
            sp.wait_ge(tables_ready, 2)
            n_tasks = sp.value_load(n_tasks_i[0:1, 0:1], min_val=NE, max_val=MAX_TASKS)
            with sp.Fori(NE, MAX_TASKS) as t:
                with sp.If(t < n_tasks):
                    task_loads(t, sp.value_load(task_e[0:1, bass.ds(t, 1)], min_val=0, max_val=NE - 1))
            for j in range(AHEAD):
                load(sp, S_MOE + j, raw[:, (S_MOE + j) % RING, 0:8], ffn_in[0, 0:P, 0:8], n_tasks * (SUBS_TASK // RING))
            sp.wait_ge(rows_stored, 32 * n_tasks + 32)
            sp.wait_ge(sel_lo, DT * n_tasks + DT)
            for k in range(TT):
                sp.dma_start(y2_in[:, k, :, :], y2_dram[2 * k * P:2 * (k + 1) * P, :]
                             .rearrange("(p two) d -> p two d", two=2)).then_inc(y2_landed[k], 16)
            for k in range(TT):
                sp.wait_ge(out_ready, k + 1)
                sp.dma_start(out[0, k * P:(k + 1) * P, :], x2_rows[:, k, :]).then_inc(stored, 16)
            sp.wait_ge(stored, 16 * TT)

        @block.gpsimd
        def _(pool):
            pool.memset(eps[:, :], EPS).then_inc(consts, 1)
            pool.memset(ones[:, :], 1.0).then_inc(consts, 1)
            pool.memset(ident[:, :], 0.0).then_inc(const_steps, 1)
            pool.memset(neg_ones[:, :].bitcast(F32), -1.0).then_inc(const_steps, 1)
            pool.iota(count[:, :], pattern=[[1, PAD]], base=1, channel_multiplier=0,
                      allow_small_or_imprecise_dtypes=True).then_inc(const_steps, 1)
            pool.wait_ge(const_steps, 3)
            pool.affine_select(out=ident[:, :], in_=ident[:, :], compare_op=ALU.not_equal, fill=1.0,
                               base=0, pattern=[[-1, P]], channel_multiplier=1).then_inc(consts, 1)
            pool.affine_select(out=neg_tri[:, :], in_=neg_ones[:, :].bitcast(F32), compare_op=ALU.is_ge,
                               fill=0.0, base=0, pattern=[[-1, P]], channel_multiplier=1).then_inc(consts, 1)
            for g in range(NG):
                pool.memset(band[:, 1, g, :], 1.0 / WINDOWS[g]).then_inc(band_step, 1)
            pool.wait_ge(band_step, NG)
            pool.affine_select(out=band[:, 1, :, :], in_=band[:, 1, :, :], compare_op=ALU.is_ge, fill=0.0, base=0,
                               pattern=[[0, NG], [1, P + PAD]], channel_multiplier=-1).then_inc(band_step, 1)
            pool.wait_ge(band_step, NG + 1)
            for g in range(NG):
                pool.affine_select(out=band[:, 1, g, :], in_=band[:, 1, g, :], compare_op=ALU.is_ge, fill=0.0,
                                   base=WINDOWS[g] - 1, pattern=[[-1, P + PAD]],
                                   channel_multiplier=1).then_inc(band_step, 1)
            pool.wait_ge(inv_ready, 1)
            for g in range(NG):
                w = WINDOWS[g]
                pool.affine_select(out=head_cols[:, g, 0:w], in_=inv_count[:, 0:w], compare_op=ALU.is_ge, fill=0.0,
                                   base=0, pattern=[[1, w]], channel_multiplier=-1).then_inc(band_step, 1)
            pool.memset(not_causal[:, :].bitcast(F32), -(2.0 ** 60)).then_inc(const_steps, 1)
            pool.wait_ge(consts, 4)
            pool.tensor_copy(ident_r[:, :], ident[:, :]).then_inc(consts, 1)
            pool.wait_ge(const_steps, 4)
            pool.affine_select(out=not_causal[:, :], in_=not_causal[:, :].bitcast(F32), compare_op=ALU.is_ge,
                               fill=0.0, base=0, pattern=[[-1, P]], channel_multiplier=1).then_inc(consts, 1)
            f = dict(allow_small_or_imprecise_dtypes=True)
            pool.iota(slot_iota[:, :], pattern=[[1, NT]], base=0, channel_multiplier=0, **f).then_inc(cleared, 1)
            pool.iota(e_iota[:, :], pattern=[[1, NE]], base=0, channel_multiplier=0, **f).then_inc(cleared, 1)
            pool.iota(row0[:, :], pattern=[[2 * P, TT]], base=1, channel_multiplier=2, **f).then_inc(cleared, 1)
            pool.iota(spare_row[:, :], pattern=[[P, 2]], base=2 * T + 1, channel_multiplier=1,
                      **f).then_inc(cleared, 1)

            pool.wait_ge(c_done, NH)
            pool.affine_select(out=earlier[:, :], in_=ones[:, :], compare_op=ALU.is_gt, fill=0.0, base=0,
                               pattern=[[1, P]], channel_multiplier=-1).then_inc(cleared, 1)
            pool.wait_ge(o_added, DT)
            pool.memset(pick[:, :, NT:], 0.0).then_inc(cleared, 1)
            pool.memset(yT[:, :, :, NT:], 0.0).then_inc(cleared, 1)
            for h in range(2):
                c = slice(h * (D // 2), (h + 1) * (D // 2))
                pool.dma_start(g_row[:, c], g_final[c].partition_broadcast(P)).then_inc(rows_stored, 16)

            def task(t):
                with pool.Fori(0, PAIRS // 2) as i:
                    for p in range(2):
                        n = PAIRS * t + 2 * i + p
                        place_ = bass.ds(4 * i + 2 * p, 2)
                        pool.wait_ge(m_ready, n + 3)
                        pool.tensor_copy(hid[:, 0, place_, :], up_s[:, p, :, :]).then_inc(mh_hi, 1)
                        pool.wait_ge(mh_hi, n + 1)
                        pool.tensor_tensor(hid[:, 1, place_, :], up_s[:, p, :, :],
                                           hid[:, 0, place_, :].bitcast(F32), ALU.subtract).then_inc(mh_lo, 1)
                pool.wait_ge(y_kept, 4 * t + 6)
                pool.tensor_tensor(wait_holder[:, :], eps[:, :], eps[:, :], ALU.add)
                for b, n in enumerate((P, NT - P)):
                    pool.indirect_dma_start(
                        out=y2_dram[:, :],
                        out_offset=bass.IndirectOffsetOnAxis(ap=info_row[0:n, b:b + 1].bitcast(U32), axis=0),
                        in_=y_rows[0:n, b, :], in_offset=None).then_inc(rows_stored, 16)

            for k in range(2):
                pool.memset(ss[:, k:k + 1], 0.0).then_inc(mh_lo, 1)
            task_loop(pool, task)

        @block.scalar
        def _(act):
            rows = lambda v: v.rearrange("l (t p) -> (l t) p", p=P)
            act.dma_start(gains_in[G_MIX:G_MIX + 16, :], rows(g_mix)).then_inc(gains_landed, 16)
            act.dma_start(gains_in[G_FFN:G_FFN + 16, :], rows(g_ffn)).then_inc(gains_landed, 16)
            act.dma_start(gains_in[G_SCALE:G_SCALE + 8, :], rows(pool_scale)).then_inc(gains_landed, 16)
            act.dma_start(gains_in[G_KV:G_KV + 8, :], g_kv.rearrange("(t p) -> t p", p=P)).then_inc(gains_landed, 16)
            act.dma_start(wr[:, :, :], w_router[0].rearrange("(k p) e -> p k e", p=P)).then_inc(small_landed, 16)

            def square(n, d):
                if d >= 2:
                    act.wait_ge(acc_step, 6 * (n - 1) + max(1, d - 2))
                elif n > 1:
                    act.wait_ge(sq_summed, n - 1)
                act.activation(tmp[:, d % 2, :], xT[:, d, :], ACT.Square).then_inc(sq_ready, 1)

            def root(n):
                act.wait_ge(sq_summed, n)
                act.activation(tmp[:, 2, :], psum[:, 0, :], ACT.Sqrt, bias=eps[:, :],
                               scale=1.0 / D).then_inc(root_ready, 1)

            def h_round(n):
                for d in range(DT):
                    act.wait_ge(hf_ready, DT * (n - 1) + d + 1)
                    act.activation(hT_hi[:, d, :], tmp[:, 3 + d % 2, :], ACT.Copy).then_inc(h_hi, 1)

            for t in range(TT):
                act.wait_ge(x_landed[t], 16)
                act.activation(x_n[:, t, :], x_in[:, t, :], ACT.Square, accum_out=ss[:, t:t + 1]).then_inc(in_squared, 1)
            act.wait_ge(in_squared, TT)
            act.wait_ge(consts, 4)
            act.activation(ss[:, :], ss[:, :], ACT.Sqrt, bias=eps[:, :], scale=1.0 / D).then_inc(in_root, 1)
            act.wait_ge(in_rstd, 1)
            for t in range(0, TT, 2):
                act.activation(x_n[:, t, :], x_in[:, t, :], ACT.Copy, scale=ss[:, t:t + 1]).then_inc(x_n_act, 1)
            for d in range(0, DT, 2):
                act.wait_ge(x_turned, d + 1)
                act.activation(xT[:, d, :], psum[:, d, :], ACT.Copy).then_inc(x_act, 1)
            split_hi(act, S_POOL)
            act.wait_ge(gains_ready, 1)
            for d in range(DT):
                act.wait_ge(pooled, d + 1)
                act.activation(hT_hi[:, d, :], psum[:, d, :], ACT.Copy,
                               scale=gains[:, G_MIX + d:G_MIX + d + 1]).then_inc(h_hi, 1)
            act.wait_ge(x_dve, DT // 2)
            act.wait_ge(x_act, DT // 2)
            for c in range(1, AHEAD):
                split_hi(act, c)

            def hidden(c, F, I):
                column_done(act, c, F % 2, I)
                if F >= 2 or not isinstance(I, int):
                    act.wait_ge(hm_ready, F + 4 * I - 1)
                act.activation(tmp[:, F % 2, :], psum[:, F % 2, :], ACT.Silu).then_inc(sil_ready, 1)

            def hidden_round(F, I, place_):
                act.wait_ge(hm_ready, F + 4 * I + 1)
                act.activation(place_, tmp[:, 3 + F % 2, :], ACT.Copy).then_inc(hid_hi_ready, 1)

            split_hi(act, S_FFN + 2)
            for d in range(DT):
                act.wait_ge(pool_added, d + 1)
                square(1, d)
            root(1)
            h_round(1)
            f0 = 0
            for half in range(2):
                nf = F_HALF[half]
                if half == 1:
                    column_done(act, S_OUT[0] + 7, 1)

                def pair(p, I):
                    c = S_IN[half] + 2 * p + AHEAD
                    split_hi(act, c, I)
                    for f in range(2):
                        hidden(c - AHEAD, f0 + 2 * p + f, I)
                    split_hi(act, c + 1, I)
                    for f in range(2):
                        hidden_round(f0 + 2 * p + f, I, hid_hi[:, bass.ds(2 * p + f + 4 * I, 1), :]
                                     .rearrange("p a t -> p (a t)"))
                pair(0, 0)
                pair(1, 0)
                with act.Fori(1, nf // 4) as i:
                    pair(0, i)
                    pair(1, i)
                if nf % 4:
                    pair(nf // 2 - 1, 0)
                for j in range(8):
                    split_hi(act, S_OUT[half] + j + AHEAD)
                    if half == 1 and j % 2 and j >= 3:
                        for d in (j - 3, j - 2):
                            act.wait_ge(fo_added, DT + d + 1)
                            square(2, d)
                f0 += nf
            for d in range(DT - 2, DT):
                act.wait_ge(fo_added, DT + d + 1)
                square(2, d)
            root(2)
            h_round(2)
            for j in range(4):
                split_hi(act, S_K + j + AHEAD)
                for f in range(2):
                    n = 2 * j + f
                    column_done(act, S_K + j, f)
                    act.activation(KT[:, n, :], psum[:, n % 4, :], ACT.Copy).then_inc(proj_kept, 1)
            for j in range(4):
                split_hi(act, S_V + j + AHEAD)
                for t in range(TT):
                    column_done(act, S_V + j, 1)
                    act.activation(V[:, t, j * CW:(j + 1) * CW], psum[:, 4 * (j % 2) + t, 0:CW],
                                   ACT.Copy).then_inc(proj_kept, 1)
            h_round(3)
            split_hi(act, S_Q + 3)

            def keep_q(m, I=0):
                column_done_q(act, m, I)
                act.activation(QT[:, bass.ds(m + 2 * I, 1), :].rearrange("p a t -> p (a t)"), psum[:, 7 if m else 6, :],
                               ACT.Copy, scale=HD ** -0.5).then_inc(proj_kept, 1)

            keep_q(0)
            keep_q(1)
            act.preload_act_table_set("natural_log_exp_and_others")

            def softplus_part(h, I):
                n, first_uses = h + 4 * I, isinstance(I, int) and h < 2
                act.wait_ge(z_done, n + 1)
                if not first_uses:
                    act.wait_ge(av_done, n - 1)
                e = E[:, h % 2, :]
                act.activation(e, head_z(h), ACT.Abs).then_inc(abs_ready, 1)
                act.wait_ge(abs_ready, n + 1)
                act.activation(e, e, ACT.Exp, scale=-1.0).then_inc(exp_ready, 1)
                act.wait_ge(exp_ready, n + 1)
                act.activation(e, e, ACT.Ln, bias=1.0).then_inc(ln_ready, 1)

            def weights(h, I):
                act.wait_ge(c_done, h + 4 * I + 1)
                act.activation(E[:, h % 2, :], head_z(h), ACT.Exp).then_inc(a_ready, 1)

            def o_round(p, I):
                act.wait_ge(av_done, 2 * p + 4 * I + 2)
                act.activation(oT_hi[:, bass.ds(p + 2 * I, 1), :].rearrange("p a t -> p (a t)"), psum[:, 6, :],
                               ACT.Copy).then_inc(o_hi_ready, 1)

            def four_heads(I, q_tiles):
                softplus_part(0, I)
                weights(3, I - 1)
                if q_tiles:
                    keep_q(1, I)
                o_round(1, I - 1)
                softplus_part(1, I)
                weights(0, I)
                softplus_part(2, I)
                weights(1, I)
                if q_tiles == 2:
                    keep_q(2, I)
                o_round(0, I)
                softplus_part(3, I)
                weights(2, I)

            softplus_part(0, 0)
            softplus_part(1, 0)
            weights(0, 0)
            softplus_part(2, 0)
            weights(1, 0)
            keep_q(2)
            o_round(0, 0)
            softplus_part(3, 0)
            weights(2, 0)
            with act.Fori(1, NH // 4 - 1) as i:
                four_heads(i, 2)
            four_heads(NH // 4 - 1, 1)
            weights(3, NH // 4 - 1)
            o_round(1, NH // 4 - 1)
            for j in range(4):
                split_hi(act, S_O + j)

            def keep_x2(d):
                act.wait_ge(x2_turned, d + 1)
                act.activation(x2_rows[:, :, d * P:(d + 1) * P], psum[:, 6 + d % 2, :].rearrange("p (t f) -> p t f", t=TT),
                               ACT.Copy).then_inc(x2_kept, 1)

            for d in range(DT):
                act.wait_ge(o_added, d + 1)
                act.wait_ge(sq_summed, 2 + max(d - 1, 0))
                act.activation(tmp[:, d % 2, :], xT[:, d, :], ACT.Square).then_inc(sq_ready, 1)
                if d:
                    keep_x2(d - 1)
                if d % 2 and d >= 3:
                    split_hi(act, S_MOE + (d - 3) // 2)
            act.wait_ge(sq_summed, 2 + DT)
            act.activation(rstd_tok[:, :], psum[:, 4, 0:TT], ACT.Sqrt, bias=eps[:, :],
                           scale=1.0 / D).then_inc(root_ready, 1)
            keep_x2(DT - 1)
            act.wait_ge(gap_ready, 1)
            act.activation(gates[:, 1, :], gates[:, 0, :], ACT.Exp).then_inc(gap_exp, 1)
            act.preload_act_table_set("silu_and_others")

            def select(t):
                for k in range(DT):
                    act.wait_ge(sel_done, DT * t + k + 1)
                    act.activation(x_sel[:, 0, k, :], psum[:, k % 4, 0:NT], ACT.Copy,
                                   scale=gains[:, G_FFN + DT + k:G_FFN + DT + k + 1]).then_inc(sel_hi, 1)

            select(0)

            def task(t):
                T11 = t * (SUBS_TASK // RING)
                with act.Fori(0, PAIRS // 2) as i:
                    for p in range(2):
                        n = PAIRS * t + 2 * i + p
                        c = S_MOE + 2 * p
                        split_hi(act, c + AHEAD, T11 + i)
                        column_done(act, c, 1, T11 + i)
                        act.wait_ge(m_ready, n + 1)
                        act.activation(gate_s[:, p, :, :], psum[:, 0:2, NT:2 * NT], ACT.Copy).then_inc(g_half, 1)
                        split_hi(act, c + 1 + AHEAD, T11 + i)
                        act.wait_ge(g_summed, n + 2)
                        act.activation(gate_s[:, p, :, :], gate_s[:, p, :, :], ACT.Silu).then_inc(g_silu, 1)
                        column_done(act, c + 1, 1, T11 + i)
                        act.wait_ge(mh_lo, n + 1)
                        act.activation(up_s[:, p, :, :], psum[:, 2:4, NT:2 * NT], ACT.Copy).then_inc(u_half, 1)
                for q in range(Q_OUT):
                    for j in range(4):
                        split_hi(act, C2 + 4 * q + j + AHEAD, T11)
                    column_done(act, C2 + 4 * q + 3, 1, T11)
                    b = 4 + 2 * (q % 2)
                    if q >= 2:
                        act.wait_ge(yT_ready, 4 * t + q - 1)
                    act.activation(y_s[:, q % 2, :, :], psum[:, b:b + 2, NT:2 * NT], ACT.Copy).then_inc(y_half, 1)
                select(t + 1)

            task_loop(act, task)
            for k in range(TT):
                act.wait_ge(sum_step, 2 * k + 2)
                if k >= 2:
                    act.wait_ge(ss_ready, k - 1)
                act.activation(sq_out[:, k % 2, :], x2_rows[:, k, :], ACT.Square,
                               accum_out=ss[:, k:k + 1]).then_inc(ss_ready, 1)
                act.wait_ge(ss_ready, k + 1)
                act.activation(ss[:, k:k + 1], ss[:, k:k + 1], ACT.Sqrt, bias=eps[:, :],
                               scale=1.0 / D).then_inc(root_end, 1)

        @block.vector
        def _(dve):
            steps = [0]

            def chained(i):
                steps[0] += 1
                i.then_inc(dve_step, 1)
                dve.wait_ge(dve_step, steps[0])

            dve.wait_ge(const_steps, 3)
            dve.reciprocal(inv_count[:, :], count[:, :]).then_inc(inv_ready, 1)
            dve.wait_ge(consts, 4)
            dve.wait_ge(band_step, 2 * NG + 1)
            chained(dve.tensor_tensor(band[:, 1, :, 0:P], band[:, 1, :, 0:P],
                                      ident[:, :].unsqueeze(1).to_broadcast([P, NG, P]), ALU.subtract))
            chained(dve.tensor_copy(band[:, 0, :, :], band[:, 1, :, :]))
            dve.wait_ge(band_step, 3 * NG + 1)
            for g in range(NG):
                w = WINDOWS[g]
                dve.tensor_tensor(band[:, 0, g, 0:w], head_cols[:, g, 0:w], ident[:, 0:w],
                                  ALU.subtract).then_inc(bands_ready, 1)
            dve.wait_ge(in_root, 1)
            dve.reciprocal(ss[:, :], ss[:, :]).then_inc(in_rstd, 1)
            dve.wait_ge(in_rstd, 1)
            for t in range(1, TT, 2):
                dve.tensor_scalar(x_n[:, t, :], x_in[:, t, :], ss[:, t:t + 1], None, ALU.mult).then_inc(x_n_dve, 1)
            for d in range(1, DT, 2):
                dve.wait_ge(x_turned, d + 1)
                dve.tensor_copy(xT[:, d, :], psum[:, d, :]).then_inc(x_dve, 1)
            dve.wait_ge(gains_T, 1)
            dve.tensor_copy(gains[:, :], psum[:, 0, 0:NV]).then_inc(gains_ready, 1)
            split_lo(dve, S_POOL)
            dve.wait_ge(gains_ready, 1)
            for d in range(DT):
                dve.wait_ge(h_hi, d + 1)
                dve.scalar_tensor_tensor(hT_lo[:, d, :], psum[:, d, :], gains[:, G_MIX + d:G_MIX + d + 1],
                                         hT_hi[:, d, :].bitcast(F32), ALU.mult, ALU.subtract).then_inc(h_lo, 1)
            dve.wait_ge(x_act, DT // 2)
            dve.wait_ge(x_dve, DT // 2)

            def add_squares(n, d):
                dve.wait_ge(sq_ready, DT * (n - 1) + d + 1)
                if d == 1:
                    i = dve.tensor_tensor(tmp[:, 2, :], tmp[:, 0, :], tmp[:, 1, :], ALU.add)
                else:
                    dve.wait_ge(acc_step, 6 * (n - 1) + d - 1)
                    i = dve.tensor_tensor(tmp[:, 2, :], tmp[:, 2, :], tmp[:, d % 2, :], ALU.add)
                i.then_inc(acc_step, 1)

            def rstd(n):
                dve.wait_ge(root_ready, n)
                dve.reciprocal(tmp[:, 2, :], tmp[:, 2, :]).then_inc(rstd_ready, 1)
                dve.wait_ge(rstd_ready, n)

            def normed(o, d, g):
                return dve.scalar_tensor_tensor(o, xT[:, d, :], gains[:, g + d:g + d + 1],
                                                tmp[:, 2, :], ALU.mult, ALU.mult)

            def h_minus(n, d):
                dve.wait_ge(h_hi, DT * n + d + 1)
                dve.tensor_tensor(hT_lo[:, d, :], tmp[:, 3 + d % 2, :], hT_hi[:, d, :].bitcast(F32),
                                  ALU.subtract).then_inc(h_lo, 1)

            def norm_tiles(n, g):
                for d in range(DT):
                    if d >= 2:
                        dve.wait_ge(h_lo, DT * n + d - 1)
                    normed(tmp[:, 3 + d % 2, :], d, g).then_inc(hf_ready, 1)
                    if d:
                        h_minus(n, d - 1)
                h_minus(n, DT - 1)

            for c in range(1, AHEAD):
                split_lo(dve, c)
            split_lo(dve, S_FFN + 2)
            for d in range(DT):
                column_done(dve, S_POOL, d // 4)
                dve.scalar_tensor_tensor(xT[:, d, :], psum[:, d, :], gains[:, G_SCALE + d:G_SCALE + d + 1],
                                         xT[:, d, :], ALU.mult, ALU.add).then_inc(pool_added, 1)
                if d >= 2:
                    add_squares(1, d - 1)
            rstd(1)
            norm_tiles(1, G_FFN)
            f0 = 0
            for half in range(2):
                nf = F_HALF[half]

                def pair(p, I):
                    c = S_IN[half] + 2 * p + AHEAD
                    split_lo(dve, c, I)
                    F = f0 + 2 * p
                    for f in range(2):
                        dve.wait_ge(sil_ready, F + f + 4 * I + 1)
                        column_done(dve, c - AHEAD + 1, f, I)
                        if F + f >= 2 or not isinstance(I, int):
                            dve.wait_ge(hid_lo_ready, F + f + 4 * I - 1)
                        dve.tensor_tensor(tmp[:, 3 + (F + f) % 2, :], tmp[:, (F + f) % 2, :],
                                          psum[:, 2 + (F + f) % 2, :], ALU.mult).then_inc(hm_ready, 1)
                    split_lo(dve, c + 1, I)
                    for f in range(2):
                        dve.wait_ge(hid_hi_ready, F + f + 4 * I + 1)
                        q = bass.ds(2 * p + f + 4 * I, 1)
                        flat = lambda a: a.rearrange("p a t -> p (a t)")
                        dve.tensor_tensor(flat(hid_lo[:, q, :]), tmp[:, 3 + (F + f) % 2, :],
                                          flat(hid_hi[:, q, :]).bitcast(F32), ALU.subtract).then_inc(hid_lo_ready, 1)
                pair(0, 0)
                pair(1, 0)
                with dve.Fori(1, nf // 4) as i:
                    pair(0, i)
                    pair(1, i)
                if nf % 4:
                    pair(nf // 2 - 1, 0)
                for q in range(4):
                    for s in range(2):
                        split_lo(dve, S_OUT[half] + 2 * q + s + AHEAD)
                    for dd in range(2):
                        d = 2 * q + dd
                        column_done(dve, S_OUT[half] + 2 * q + 1, dd)
                        dve.tensor_tensor(xT[:, d, :], xT[:, d, :], psum[:, 4 + d % 4, :],
                                          ALU.add).then_inc(fo_added, 1)
                    if half == 1 and q:
                        for d in (2 * q - 2, 2 * q - 1):
                            if d:
                                add_squares(2, d)
                f0 += nf
            add_squares(2, DT - 2)
            rstd(2)
            norm_tiles(2, G_KV)
            for j in range(8):
                split_lo(dve, S_K + j + AHEAD)
            column_done(dve, S_V + 3, 1)
            norm_tiles(3, G_MIX + DT)
            split_lo(dve, S_Q + 3)
            dve.wait_ge(small_landed, 16)
            for k in range(DT):
                i = dve.tensor_scalar(wr_g[:, k, :], wr[:, k, :], gains[:, G_FFN + DT + k:G_FFN + DT + k + 1], None,
                                      ALU.mult)
            i.then_inc(wr_g_ready, 1)

            def softplus(h, I):
                n = h + 4 * I
                dve.wait_ge(ln_ready, n + 1)
                e, hi = E[:, h % 2, :], sp_hi[:, :]
                dve.scalar_tensor_tensor(e, head_z(h), 0.0, e, ALU.max, ALU.add).then_inc(sp_ready, 1)
                if h or not isinstance(I, int):
                    dve.wait_ge(c_done, n)
                dve.wait_ge(sp_ready, n + 1)
                dve.tensor_copy(hi, e).then_inc(sph_ready, 1)
                dve.wait_ge(sph_ready, n + 1)
                dve.tensor_tensor(sp_lo[:, :], e, hi.bitcast(F32), ALU.subtract).then_inc(spl_ready, 1)

            def o_minus(p, I):
                dve.wait_ge(o_hi_ready, p + 2 * I + 1)
                q = bass.ds(p + 2 * I, 1)
                flat = lambda a: a.rearrange("p a t -> p (a t)")
                dve.tensor_tensor(flat(oT_lo[:, q, :]), psum[:, 6, :], flat(oT_hi[:, q, :]).bitcast(F32),
                                  ALU.subtract).then_inc(o_lo_ready, 1)

            softplus(0, 0)
            softplus(1, 0)
            softplus(2, 0)
            o_minus(0, 0)
            softplus(3, 0)
            with dve.Fori(1, NH // 4) as i:
                softplus(0, i)
                o_minus(1, i - 1)
                softplus(1, i)
                softplus(2, i)
                o_minus(0, i)
                softplus(3, i)
            o_minus(1, NH // 4 - 1)
            for j in range(4):
                split_lo(dve, S_O + j)
            for d in range(DT):
                column_done(dve, S_O + d // 2, d % 2)
                dve.tensor_tensor(xT[:, d, :], xT[:, d, :], psum[:, d % 4, :], ALU.add).then_inc(o_added, 1)
                if d % 2 and d >= 3:
                    split_lo(dve, S_MOE + (d - 3) // 2)

            dve.wait_ge(root_ready, 3)
            chained(dve.reciprocal(rstd_tok[:, :], rstd_tok[:, :]))
            dve.wait_ge(cleared, 5)
            dve.wait_ge(logits_done, 1)
            for t in range(TT):
                i = dve.tensor_scalar(logits[:, t, :], psum[:, 5, t * NE:(t + 1) * NE], rstd_tok[:, t:t + 1], None,
                                      ALU.mult)
            chained(i)
            for t in range(TT):
                chained(dve.max(top_v[:, t, :], logits[:, t, :]))
                i = dve.max_index(top_i[:, t, :], top_v[:, t, :], logits[:, t, :])
            chained(i)
            dve.tensor_tensor(gates[:, 0, :], top_v[:, :, 1], top_v[:, :, 0], ALU.subtract).then_inc(gap_ready, 1)
            chained(dve.tensor_copy(top_f[:, :, :], top_i[:, :, :]))
            for t in range(TT):
                dve.tensor_scalar(first[:, t, :], e_iota[:, :], top_f[:, t, 0:1], None, ALU.is_equal)
                i = dve.tensor_scalar(second[:, t, :], e_iota[:, :], top_f[:, t, 1:2], None, ALU.is_equal)
            chained(i)
            dve.tensor_tensor(chosen[:, :, :], first[:, :, :], second[:, :, :], ALU.add).then_inc(chosen_ready, 1)

            def picks(table_, t):
                for k in range(TT):
                    slot = table_[:, k, bass.ds(t, 1)]
                    dve.tensor_scalar(pick[:, k, 0:NT], slot_iota[:, :], slot, None, ALU.is_equal)
                    i = dve.tensor_scalar(pick_r[:, k, :], slot_iota[:, :], slot, rstd_tok[:, k:k + 1],
                                          ALU.is_equal, ALU.mult)
                i.then_inc(pick_ready, 1)

            FAR = 8192.0
            dve.wait_ge(ranks_done, 1)
            chained(dve.scalar_tensor_tensor(rank[:, :, :], psum[:, 4, 0:TT * NE].rearrange("p (t e) -> p t e", e=NE),
                                             FAR, chosen[:, :, :], ALU.add, ALU.mult))
            chained(dve.tensor_scalar(rank[:, :, :], rank[:, :, :], -FAR, None, ALU.add))
            chained(dve.tensor_copy(cnt[:, :], psum[:, 4, TT * NE:(TT + 1) * NE]))
            dve.wait_ge(cleared, 7)
            picks(rank, 0)
            ks = range(1, (T - 1) // NT + 1)
            chained(dve.tensor_scalar(extra[:, 0, :], cnt[:, :], float(NT), None, ALU.is_gt))
            for k in ks[1:]:
                chained(dve.scalar_tensor_tensor(extra[:, (k - 1) % 3, :], cnt[:, :], float(k * NT),
                                                 extra[:, (k - 2) % 3, :], ALU.is_gt, ALU.add))
            ex = extra[:, (ks[-1] - 1) % 3, :]
            chained(dve.memset(cum[:, :, :], 0.0))
            chained(dve.tensor_copy(cum[:, 0, 4:], ex))
            for r in range(3):
                chained(dve.tensor_tensor(cum[:, r + 1, 4:], cum[:, r, 4:], cum[:, r, 4 - 2 ** r:4 - 2 ** r + NE],
                                          ALU.add))
            upto = cum[:, 3, 4:]
            chained(dve.tensor_tensor(before[:, :], upto, ex, ALU.subtract))
            chained(dve.tensor_scalar(n_f[:, :], cum[:, 3, 3 + NE:4 + NE], float(NE), None, ALU.add))
            dve.tensor_copy(n_tasks_i[:, :], n_f[:, :]).then_inc(tables_ready, 1)
            for k, first_count in enumerate((m_ready, m_ready, y_kept, y_kept, g_summed, u_summed)):
                dve.memset(primed[:, k + 1:k + 2], 0.0).then_inc(first_count, 1)

            def select(t):
                for k in range(DT):
                    dve.wait_ge(sel_hi, DT * t + k + 1)
                    dve.scalar_tensor_tensor(x_sel[:, 1, k, :], psum[:, k % 4, 0:NT],
                                             gains[:, G_FFN + DT + k:G_FFN + DT + k + 1],
                                             x_sel[:, 0, k, :].bitcast(F32), ALU.mult, ALU.subtract).then_inc(sel_lo, 1)

            select(0)
            dve.wait_ge(gap_exp, 1)
            chained(dve.tensor_scalar(gates[:, 0, :], gates[:, 1, :], 1.0, None, ALU.add))
            chained(dve.reciprocal(gates[:, 2, :], gates[:, 0, :]))
            chained(dve.tensor_tensor(gates[:, 3, :], gates[:, 1, :], gates[:, 2, :], ALU.mult))
            for t in range(TT):
                i = dve.tensor_scalar(gate_e[:, t, :], second[:, t, :], gates[:, 3, t:t + 1], None, ALU.mult)
            chained(i)
            for t in range(TT):
                dve.scalar_tensor_tensor(gate_e[:, t, :], first[:, t, :], gates[:, 2, t:t + 1], gate_e[:, t, :],
                                         ALU.mult, ALU.add)
                i = dve.tensor_scalar(row_e[:, t, :], second[:, t, :], row0[:, t:t + 1], None, ALU.add)
            chained(i)
            XT = TC - NE
            number = lambda n: slot_iota[:, 0:n].unsqueeze(2).to_broadcast([P, n, NE])
            per_task = lambda a, n: a.unsqueeze(1).to_broadcast([P, n, NE])
            dve.tensor_tensor(is_past[:, 0, :, :], per_task(upto, XT), number(XT), ALU.is_le)
            dve.tensor_tensor(is_past[:, 1, :, :], per_task(before[:, :], XT), number(XT), ALU.is_le)
            dve.tensor_tensor(is_mine[:, 0:NE, :], per_task(e_iota[:, :], NE), number(NE), ALU.is_equal)
            dve.memset(start[:, 0:NE, :], 1.0)
            chained(dve.tensor_tensor(start[:, NE:, :], per_task(before[:, :], XT), number(XT), ALU.subtract))
            chained(dve.tensor_scalar(start[:, NE:, :], start[:, NE:, :], float(NT), float(1 - NT), ALU.mult, ALU.add))
            chained(dve.tensor_tensor(is_mine[:, NE:, :], is_past[:, 1, :, :], is_past[:, 0, :, :], ALU.subtract))

            def over_tasks(a):
                return a[:, :, :].unsqueeze(2).to_broadcast([P, TT, TC, NE])

            def over_tokens(a):
                return a[:, :, :].unsqueeze(1).to_broadcast([P, TT, TC, NE])

            chained(dve.tensor_reduce(e_f[:, NE:], is_past[:, 0, :, :], AX_X, ALU.add))
            chained(dve.tensor_copy(e_f[:, 0:NE], e_iota[:, :]))
            chained(dve.tensor_scalar(e_f[:, :], e_f[:, :], float(NE - 1), None, ALU.min))
            chained(dve.tensor_copy(task_e[:, :], e_f[:, :]))
            chained(dve.tensor_tensor(wide[:, :, :, :], over_tasks(rank), over_tokens(start), ALU.add))
            chained(dve.tensor_tensor(wide[:, :, :, :], wide[:, :, :, :], over_tokens(is_mine), ALU.mult))
            chained(dve.tensor_reduce(pos[:, :, :], wide[:, :, :, :], AX_X, ALU.add))
            chained(dve.tensor_scalar(pos[:, :, :], pos[:, :, :], -1.0, None, ALU.add))
            for n, a in enumerate((row_e, gate_e)):
                chained(dve.tensor_tensor(wide[:, :, :, :], over_tasks(a), over_tokens(is_mine), ALU.mult))
                chained(dve.tensor_reduce(row_gate[:, :, :, n], wide[:, :, :, :], AX_X, ALU.add))
            dve.memset(primed[:, 0:1], 0.0).then_inc(tables_ready, 1)

            def keep_rows(t, q):
                dve.wait_ge(y_turned, 4 * t + q + 1)
                b = 4 + 2 * (q % 2)
                cols = slice(q * CW, (q + 1) * CW)
                dve.tensor_scalar(y_rows[:, 0, cols], psum[:, b, 0:CW], info[:, 0, 1:2], None, ALU.mult)
                dve.tensor_scalar(y_rows[0:NT - P, 1, cols], psum[0:NT - P, b, CW:2 * CW],
                                  info[0:NT - P, 1, 1:2], None, ALU.mult).then_inc(y_kept, 1)

            def rows_of_slots(t):
                dve.wait_ge(info_done, t + 1)
                dve.wait_ge(y_kept, 4 * t + 2)
                dve.tensor_copy(info[:, :, :], psum[:, 0, 0:4].rearrange("p (a b) -> p a b", a=2)).then_inc(info_ready, 1)
                dve.wait_ge(rows_stored, 32 * t + 32)
                dve.wait_ge(info_ready, 3 * t + 1)
                dve.scalar_tensor_tensor(info_t[:, :], info[:, :, 0], 0.0, spare_row[:, :],
                                         ALU.is_equal, ALU.mult).then_inc(info_ready, 1)
                dve.wait_ge(info_ready, 3 * t + 2)
                dve.scalar_tensor_tensor(info_row[:, :], info[:, :, 0], -1.0, info_t[:, :],
                                         ALU.add, ALU.add).then_inc(info_ready, 1)

            def task(t):
                T11 = t * (SUBS_TASK // RING)
                with dve.Fori(0, PAIRS // 2) as i:
                    for p in range(2):
                        n = PAIRS * t + 2 * i + p
                        c = S_MOE + 2 * p
                        split_lo(dve, c + AHEAD, T11 + i)
                        dve.wait_ge(g_half, n + 1)
                        dve.tensor_tensor(gate_s[:, p, :, :], gate_s[:, p, :, :], psum[:, 0:2, 0:NT],
                                          ALU.add).then_inc(g_summed, 1)
                        split_lo(dve, c + 1 + AHEAD, T11 + i)
                        dve.wait_ge(u_half, n + 1)
                        dve.tensor_tensor(up_s[:, p, :, :], up_s[:, p, :, :], psum[:, 2:4, 0:NT],
                                          ALU.add).then_inc(u_summed, 1)
                        dve.wait_ge(g_silu, n + 1)
                        dve.wait_ge(u_summed, n + 2)
                        dve.tensor_tensor(up_s[:, p, :, :], up_s[:, p, :, :], gate_s[:, p, :, :],
                                          ALU.mult).then_inc(m_ready, 1)
                for q in range(Q_OUT):
                    for j in range(4):
                        split_lo(dve, C2 + 4 * q + j + AHEAD, T11)
                        if j == 1 and q:
                            keep_rows(t, q - 1)
                        if j == 1 and q == 0:
                            rows_of_slots(t)
                            picks(pos, t + 1)
                    dve.wait_ge(y_half, 4 * t + q + 1)
                    b = 4 + 2 * (q % 2)
                    dve.tensor_tensor(yT[:, q % 2, :, 0:NT], y_s[:, q % 2, :, :], psum[:, b:b + 2, 0:NT],
                                      ALU.add).then_inc(yT_ready, 1)
                select(t + 1)
                keep_rows(t, Q_OUT - 1)

            task_loop(dve, task)
            def finish(k):
                dve.wait_ge(root_end, k + 1)
                chained(dve.reciprocal(ss[:, k:k + 1], ss[:, k:k + 1]))
                dve.scalar_tensor_tensor(x2_rows[:, k, :], x2_rows[:, k, :], ss[:, k:k + 1], g_row[:, :],
                                         ALU.mult, ALU.mult).then_inc(out_ready, 1)

            for k in range(TT):
                dve.wait_ge(y2_landed[k], 16)
                dve.tensor_tensor(y2_in[:, k, 0, :], y2_in[:, k, 0, :], y2_in[:, k, 1, :],
                                  ALU.add).then_inc(sum_step, 1)
                dve.wait_ge(sum_step, 2 * k + 1)
                dve.tensor_tensor(x2_rows[:, k, :], x2_rows[:, k, :], y2_in[:, k, 0, :], ALU.add).then_inc(sum_step, 1)
                if k:
                    finish(k - 1)
            finish(TT - 1)

        @block.tensor
        def _(pe):
            pe.wait_ge(consts, 4)
            for t in range(TT):
                pe.wait_ge(x_landed[t], 16)
                for d in range(DT):
                    i = pe.transpose(psum[:, d, t * P:(t + 1) * P], x_in[:, t, d * P:(d + 1) * P], ident[:, :])
                    if t == TT - 1:
                        i.then_inc(x_turned, 1)
            pe.wait_ge(x_act, 1)
            pe.wait_ge(gains_landed, 64)
            pe.transpose(psum[:, 0, 0:NV], gains_in[:, :], ident[0:NV, 0:NV]).then_inc(gains_T, 1)
            pe.wait_ge(gains_ready, 1)
            pe.wait_ge(bands_ready, NG)
            pe.wait_ge(x_n_act, TT // 2)
            pe.wait_ge(x_n_dve, TT // 2)
            for d in range(DT):
                pe.wait_ge(x_dve if d % 2 else x_act, d // 2 + 1)
                for t in range(TT):
                    n = min(P + PAD, T - t * P)
                    i = pe.matmul(psum[:, d, t * P:t * P + n], x_n[:, t, d * P:(d + 1) * P], band[:, min(t, 1), d // 2, 0:n],
                                  start=t == 0, stop=t == TT - 1, skip_group_check=True)
                i.then_inc(pooled, 1)

            def norm(n):
                pe.wait_ge(acc_step, 6 * n)
                pe.matmul(psum[:, 0, :], ones[:, :], tmp[:, 2, :], start=True, stop=False)
                pe.wait_ge(sq_ready, DT * n)
                pe.matmul(psum[:, 0, :], ones[:, :], tmp[:, 1, :], start=False, stop=True).then_inc(sq_summed, 1)

            for d in range(DT):
                if d == 0:
                    pe.wait_ge(lo_ready, 1)
                pe.wait_ge(h_lo, 2 * (d // 2) + 2)
                for k in range(2):
                    n0 = (d // 2) * 2 * GW + k * GW + (d % 2) * P
                    i = product(pe, psum[:, d, :], w_hi[:, 0, n0:n0 + P], w_lo[:, 0, n0:n0 + P],
                                hT_hi[:, 2 * (d // 2) + k, :], hT_lo[:, 2 * (d // 2) + k, :], k == 0, k == 1)
                if d % 4 == 3:
                    i.then_inc(w_used if d == DT - 1 else half_done, 1)
            norm(1)
            f0 = 0
            for half in range(2):
                nf = F_HALF[half]

                def pair(p, I):
                    for u in range(2):
                        c = S_IN[half] + 2 * p + u
                        pe.wait_ge(lo_ready, c + 4 * I + 1)
                        for f in range(2):
                            F = f0 + 2 * p + f
                            if F >= 2 or not isinstance(I, int):
                                pe.wait_ge(hm_ready if u else sil_ready, F + 4 * I - 1)
                            for k in range(DT):
                                if F == 0 and u == 0 and isinstance(I, int):
                                    pe.wait_ge(h_lo, DT + k + 1)
                                i = product(pe, psum[:, 2 * u + f, :], *w_tile(c, k, f), hT_hi[:, k, :],
                                            hT_lo[:, k, :], k == 0, k == DT - 1)
                            i.then_inc(w_used if f else half_done, 1)

                pair(0, 0)
                pair(1, 0)
                with pe.Fori(1, nf // 4) as i_:
                    pair(0, i_)
                    pair(1, i_)
                if nf % 4:
                    pair(nf // 2 - 1, 0)
                for q in range(4):
                    for s in range(2):
                        c = S_OUT[half] + 2 * q + s
                        pe.wait_ge(lo_ready, c + 1)
                        if q == 0:
                            pe.wait_ge(hid_lo_ready, f0 + (s + 1) * (nf // 2))
                        for dd in range(2):
                            d = 2 * q + dd
                            if s == 0 and DT * half + d >= 4:
                                pe.wait_ge(fo_added, DT * half + d - 3)
                            for f in range(nf // 2):
                                F = s * (nf // 2) + f
                                i = product(pe, psum[:, 4 + d % 4, :], *w_tile(c, f, dd), hid_hi[:, F, :],
                                            hid_lo[:, F, :], F == 0, F == nf - 1)
                            i.then_inc(w_used if dd else half_done, 1)
                f0 += nf

            def project(s0, n0, free, after=None, h=None, x=(hT_hi, hT_lo)):
                for j in range(4):
                    c = s0 + j
                    pe.wait_ge(lo_ready, c + 1)
                    for f in range(2):
                        n = n0 + 2 * j + f
                        if n >= 4:
                            pe.wait_ge(free, n - 3)
                        for k in range(DT):
                            if h is not None and n == n0:
                                pe.wait_ge(h_lo, h * DT + k + 1)
                            i = product(pe, psum[:, n % 4, :], *w_tile(c, k, f), x[0][:, k, :],
                                        x[1][:, k, :], k == 0, k == DT - 1)
                        i.then_inc(w_used if f else half_done, 1)
                        if after and n > n0:
                            after(n - n0 - 1)

            norm(2)
            project(S_K, 0, proj_kept, h=2)
            for j in range(4):
                c = S_V + j
                pe.wait_ge(lo_ready, c + 1)
                for t in range(TT):
                    n = DT + 4 * j + t
                    pe.wait_ge(proj_kept, n - 7 if j >= 2 else DT)
                    for k in range(DT):
                        ts = slice(t * P, (t + 1) * P)
                        o = psum[:, 4 * (j % 2) + t, 0:CW]
                        wh, wl = (w[:, c % RING, k * CW:(k + 1) * CW] for w in (w_hi, w_lo))
                        pe.matmul(o, hT_hi[:, k, ts], wh, start=k == 0, stop=False)
                        pe.matmul(o, hT_hi[:, k, ts], wl, start=False, stop=False)
                        i = pe.matmul(o, hT_lo[:, k, ts], wh, start=False, stop=k == DT - 1)
                    if t % 2:
                        i.then_inc(w_used if t == TT - 1 else half_done, 1)

            def q_part(m, half):
                c = S_Q + m // 2
                if half == 0:
                    pe.wait_ge(lo_ready, c + 1)
                    pe.wait_ge(proj_kept, 3 * DT + max(m - 1, 0) + (m > 1))
                for k in range(4 * half, 4 * half + 4):
                    if m == 0:
                        pe.wait_ge(h_lo, 3 * DT + k + 1)
                    i = product(pe, psum[:, 7 if m else 6, :], *w_tile(c, k, m % 2), hT_hi[:, k, :],
                                hT_lo[:, k, :], k == 0, k == DT - 1)
                if half:
                    i.then_inc(w_used if m % 2 else half_done, 1)

            for m in range(2):
                q_part(m, 0)
                q_part(m, 1)
            pe.wait_ge(consts, 6)
            for h in range(NH + 2):
                if h >= 2:
                    n = h - 2
                    pe.wait_ge(a_ready, n + 1)
                    if n % 2 == 0 and n:
                        pe.wait_ge(o_lo_ready, n // 2)
                    r = slice(HD * (n % 2), HD * (n % 2) + HD)
                    for s in range(TT):
                        i = pe.matmul(psum[r, 6, s * P:T], V[:, s, n * HD:(n + 1) * HD],
                                      E[:, n % 2, SEG[s]:SEG[s] + T - s * P], start=s == 0, stop=s == TT - 1,
                                      skip_group_check=True)
                    i.then_inc(av_done, 1)
                if h < NH:
                    r = slice(HD * (h % 2), HD * (h % 2) + HD)
                    pe.wait_ge(proj_kept, 3 * DT + h // 2 + 1)
                    for b, blocks in enumerate(((0,), (1, 3), (2,))):
                        col = 0
                        for s in blocks:
                            n = T - s * P
                            pe.matmul(psum[:, 3 * (h % 2) + b, col:col + n], KT[r, h // 2, s * P:(s + 1) * P],
                                      QT[r, h // 2, s * P:T], start=col == 0, stop=False, skip_group_check=True)
                            i = pe.matmul(psum[:, 3 * (h % 2) + b, col:col + P], ident_r[:, :], not_causal[:, :],
                                          start=False, stop=False, skip_group_check=True)
                            col += n
                    i.then_inc(z_done, 1)
                if 1 <= h <= NH:
                    n = h - 1
                    for part, ready in ((sp_hi, sph_ready), (sp_lo, spl_ready)):
                        pe.wait_ge(ready, n + 1)
                        for s in range(TT):
                            b, col = ((0, 0), (1, 0), (2, 0), (1, 384))[s]
                            for j in range(s, TT):
                                w = T - j * P
                                o = psum[:, 3 * (n % 2) + b, col + (j - s) * P:col + (j - s) * P + w]
                                i = pe.matmul(o, (neg_tri if j == s else neg_ones)[:, :],
                                              part[:, SEG[j]:SEG[j] + w], start=False,
                                              stop=part is sp_lo and j == TT - 1, skip_group_check=True)
                    i.then_inc(c_done, 1)
                m, half = (h + 3) // 2, (h + 1) % 2
                if h and m < DT:
                    q_part(m, half)
            pe.wait_ge(o_lo_ready, DT)

            def follow(d):
                pe.wait_ge(o_added, d + 1)
                if d >= 2:
                    pe.wait_ge(x2_kept, d - 1)
                for t in range(TT):
                    i = pe.transpose(psum[:, 6 + d % 2, t * P:(t + 1) * P], xT[:, d, t * P:(t + 1) * P], ident[:, :])
                i.then_inc(x2_turned, 1)
                if d == 0:
                    pe.wait_ge(wr_g_ready, 1)
                for t in range(TT):
                    i = pe.matmul(psum[:, 5, t * NE:(t + 1) * NE], xT[:, d, t * P:(t + 1) * P], wr_g[:, d, :],
                                  start=d == 0 and t == 0, stop=d == DT - 1, skip_group_check=True)
                if d == DT - 1:
                    i.then_inc(logits_done, 1)
                pe.wait_ge(sq_ready, 2 * DT + d + 1)
                for t in range(TT):
                    i = pe.matmul(psum[:, 4, t:t + 1], tmp[:, d % 2, t * P:(t + 1) * P], ones[:, 0:1],
                                  start=d == 0 and t == 0, stop=d == DT - 1, skip_group_check=True)
                i.then_inc(sq_summed, 1)

            project(S_O, 0, o_added, follow, x=(oT_hi, oT_lo))
            follow(DT - 1)
            pe.wait_ge(chosen_ready, 1)
            for u in range(TT):
                pe.matmul(psum[:, 4, u * NE:(u + 1) * NE], earlier[:, :], chosen[:, u, :], start=u == 0, stop=True,
                          skip_group_check=True)
                n = TT - u
                i = pe.matmul(psum[:, 4, (u + 1) * NE:(TT + 1) * NE].rearrange("p (t e) -> p t e", e=NE), ones[:, :],
                              chosen[:, u:u + 1, :].to_broadcast([P, n, NE]), start=False, stop=u == TT - 1,
                              skip_group_check=True)
            i.then_inc(ranks_done, 1)

            def select(t):
                pe.wait_ge(pick_ready, t + 1)
                for k in range(DT):
                    if k >= 4:
                        pe.wait_ge(sel_lo, DT * t + k - 3)
                    for u in range(TT):
                        i = pe.matmul(psum[:, k % 4, 0:NT], x2_rows[:, u, k * P:(k + 1) * P], pick_r[:, u, :],
                                      start=u == 0, stop=u == TT - 1)
                    i.then_inc(sel_done, 1)

            pe.wait_ge(x2_kept, DT)
            select(0)

            def two(o, c, k, f, x, start_, stop_):
                wh, wl = w_tile(c, k, f)
                both = o.rearrange("p (a n) -> p a n", a=2)
                if stop_:
                    pe.matmul(o[:, 0:NT], wl, x[:, 0, :], start=False, stop=False, skip_group_check=True)
                    return pe.matmul(both, wh, x, start=False, stop=True, skip_group_check=True)
                pe.matmul(both, wh, x, start=start_, stop=False, skip_group_check=True)
                return pe.matmul(o[:, 0:NT], wl, x[:, 0, :], start=False, stop=False, skip_group_check=True)

            def turn(t, q):
                pe.wait_ge(yT_ready, 4 * t + q + 1)
                b = 4 + 2 * (q % 2)
                for part in range(2):
                    for dd in range(2):
                        o = (2 * part + dd) * P
                        i = pe.transpose(psum[:, b, o:o + P], yT[:, q % 2, dd, part * P:(part + 1) * P], ident[:, :])
                i.then_inc(y_turned, 1)

            def slot_info(t):
                pe.wait_ge(g_summed, PAIRS * t + PAIRS + 1)
                pe.wait_ge(tables_ready, 2)
                for part in range(2):
                    for u in range(TT):
                        i = pe.matmul(psum[:, 0, 2 * part:2 * part + 2], pick[:, u, part * P:(part + 1) * P],
                                      row_gate[:, u, bass.ds(t, 1), :].rearrange("p a b -> p (a b)"),
                                      start=u == 0, stop=u == TT - 1)
                i.then_inc(info_done, 1)

            def task(t):
                T11 = t * (SUBS_TASK // RING)
                with pe.Fori(0, PAIRS // 2) as i_:
                    pe.wait_ge(sel_lo, DT * t + DT)
                    for p in range(2):
                        n = PAIRS * t + 2 * i_ + p
                        for u in range(2):
                            c = S_MOE + 2 * p + u
                            pe.wait_ge(lo_ready, c + 4 * (T11 + i_) + 1)
                            pe.wait_ge(u_summed if u else g_summed, n + 1)
                            for f in range(2):
                                for k in range(DT):
                                    i = two(psum[:, 2 * u + f, 0:2 * NT], c, k, f, x_sel[:, :, k, :], k == 0, k == DT - 1)
                                i.then_inc(w_used if f else half_done, 1)
                for q in range(Q_OUT):
                    pe.wait_ge(y_kept, 4 * t + q + 1)
                    for j in range(4):
                        c = C2 + 4 * q + j
                        pe.wait_ge(lo_ready, c + 4 * T11 + 1)
                        if q == 0:
                            pe.wait_ge(mh_lo, PAIRS * t + 2 + (FS * (j + 1) + 1) // 2)
                        for dd in range(2):
                            for f in range(FS):
                                i = two(psum[:, 4 + 2 * (q % 2) + dd, 0:2 * NT], c, f, dd, hid[:, :, FS * j + f, :],
                                        j == 0 and f == 0, j == 3 and f == FS - 1)
                            i.then_inc(w_used if dd else half_done, 1)
                        if j == 0 and q:
                            turn(t, q - 1)
                        if j == 0 and q == 0:
                            slot_info(t)
                pe.wait_ge(g_summed, PAIRS * t + PAIRS + 1)
                pe.wait_ge(u_summed, PAIRS * t + PAIRS + 1)
                select(t + 1)
                turn(t, Q_OUT - 1)

            task_loop(pe, task)


_OUTS = [((1, 512, 1024), "float32")]
_INS = ["x", "g_mix", "g_ffn", "pool_w", "pool_scale", "g_kv", "w_kv", "w_q", "w_o", "ffn_in", "ffn_out",
        "w_router", "moe_in", "moe_out", "g_final"]


def kernel(**inputs):
    import numpy as _np
    import concourse.bacc as _bacc
    from concourse import mybir as _mybir
    from concourse.bass_utils import run_bass_kernel_spmd as _run

    nc = _bacc.Bacc("TRN2", target_bir_lowering=False, num_devices=1)
    arrays, args = {}, []
    for name in _INS:
        a = _np.ascontiguousarray(inputs[name])
        arrays[f"in_{name}_dram"] = a
        args.append(nc.dram_tensor(f"in_{name}_dram", a.shape, _mybir.dt.from_np(a.dtype), kind="ExternalInput").ap())
    for i, (shape, dtype) in enumerate(_OUTS):
        dt = _mybir.dt.from_np(_np.dtype(dtype))
        args.append(nc.dram_tensor(f"out_{i}_dram", shape, dt, kind="ExternalOutput").ap())
    trunk(nc, *args)
    r = _run(nc, [arrays], core_ids=[0])
    return r.results[0]["out_0_dram"]
```
